# Optimizing a Trainium2 kernel written in Bass

```python
import jax, jax.numpy as jnp
from jax import lax
import numpy as np

D_MODEL = 1024
BATCH = 1
SEQ = 256
DEPTH = 1

CHUNK = 64
ROPE_THETA = 10000.0
NORM_EPS = 1e-6

MLA_HEADS = 8
MLA_Q_LORA = 384
MLA_KV_LORA = 256
MLA_NOPE = 128
MLA_ROPE = 64
MLA_V = 128
MLA_QK = MLA_NOPE + MLA_ROPE
MLA_Q_BLOCK = 128

DSA_HEADS = 8
DSA_HEAD_DIM = 128
IDX_HEADS = 8
IDX_HEAD_DIM = 64
IDX_ROPE = 32
DSA_TOPK_MAX = 256
DSA_Q_BLOCK = 16

N_BRANCHES = 2

IN_SPLIT_SIZES = (
    MLA_Q_LORA,
    MLA_KV_LORA,
    MLA_ROPE,
    3 * DSA_HEADS * DSA_HEAD_DIM,
    IDX_HEADS * IDX_HEAD_DIM,
    IDX_HEAD_DIM,
    IDX_HEADS,
    N_BRANCHES * D_MODEL,
)
D_IN = (MLA_Q_LORA + MLA_KV_LORA + MLA_ROPE + 3 * DSA_HEADS * DSA_HEAD_DIM
        + IDX_HEADS * IDX_HEAD_DIM + IDX_HEAD_DIM + IDX_HEADS + N_BRANCHES * D_MODEL)

N_EXPERTS = 32
MOE_TOP_K = 4
D_EXPERT = 1024
SWIGLU_LIMIT = 7.0
SWIGLU_ALPHA = 1.702
MOE_BLOCK = 128

kernel_name = "hybrid_mla_dsa_gated_moe_block"

def rms_norm(x, g):
    xf = x.astype(jnp.float32)
    y = xf * lax.rsqrt(jnp.mean(xf * xf, axis=-1, keepdims=True) + NORM_EPS)
    return (y * g.astype(jnp.float32)).astype(x.dtype)

def rope(x, pos, rot_dim):
    half = rot_dim // 2
    inv_freq = ROPE_THETA ** (-jnp.arange(half, dtype=jnp.float32) / half)
    ang = pos.astype(jnp.float32)[:, None] * inv_freq[None, :]
    cos = jnp.cos(ang)[:, None, :].astype(x.dtype)
    sin = jnp.sin(ang)[:, None, :].astype(x.dtype)
    x1, x2, xp = x[..., :half], x[..., half:rot_dim], x[..., rot_dim:]
    return jnp.concatenate([x1 * cos - x2 * sin, x2 * cos + x1 * sin, xp], axis=-1)

def split_cols(proj):
    points, acc = [], 0
    for s in IN_SPLIT_SIZES[:-1]:
        acc += s
        points.append(acc)
    return jnp.split(proj, points, axis=-1)

def mla_attention(c_q, c_kv, k_r, q_lora_g, kv_lora_g, w_uq, w_uk, w_uv, pos):
    B, S, _ = c_q.shape
    cq = rms_norm(c_q, q_lora_g)
    ckv = rms_norm(c_kv, kv_lora_g)
    q = (cq @ w_uq).reshape(B, S, MLA_HEADS, MLA_QK)
    q = jnp.concatenate([q[..., :MLA_NOPE], rope(q[..., MLA_NOPE:], pos, MLA_ROPE)], axis=-1)
    q = q * (MLA_QK ** -0.5)
    k_nope = (ckv @ w_uk).reshape(B, S, MLA_HEADS, MLA_NOPE)
    k_rope = rope(k_r[:, :, None, :], pos, MLA_ROPE)
    k = jnp.concatenate([k_nope, jnp.broadcast_to(k_rope, (B, S, MLA_HEADS, MLA_ROPE))], axis=-1)
    v = (ckv @ w_uv).reshape(B, S, MLA_HEADS, MLA_V)
    key_chunk = pos // CHUNK
    n_blocks = S // MLA_Q_BLOCK

    def block(i):
        q_blk = lax.dynamic_slice_in_dim(q, i * MLA_Q_BLOCK, MLA_Q_BLOCK, axis=1)
        q_chunk = lax.dynamic_slice_in_dim(key_chunk, i * MLA_Q_BLOCK, MLA_Q_BLOCK)
        s = jnp.einsum('bqhd,bkhd->bhqk', q_blk, k).astype(jnp.float32)
        mask = key_chunk[None, :] <= q_chunk[:, None]
        s = jnp.where(mask[None, None], s, -jnp.inf)
        p = jax.nn.softmax(s, axis=-1).astype(v.dtype)
        return jnp.einsum('bhqk,bkhd->bqhd', p, v)

    o = lax.map(block, jnp.arange(n_blocks))
    return o.transpose(1, 0, 2, 3, 4).reshape(B, S, MLA_HEADS * MLA_V)

def dsa_attention(qkv, q_idx, k_idx, w_idx, pos, top_k):
    B, S, _ = qkv.shape
    q, k, v = jnp.split(qkv.reshape(B, S, 3, DSA_HEADS, DSA_HEAD_DIM), 3, axis=2)
    q, k, v = q[:, :, 0], k[:, :, 0], v[:, :, 0]
    q = rope(q, pos, DSA_HEAD_DIM) * (DSA_HEAD_DIM ** -0.5)
    k = rope(k, pos, DSA_HEAD_DIM)
    qi = rope(q_idx.reshape(B, S, IDX_HEADS, IDX_HEAD_DIM), pos, IDX_ROPE) * (IDX_HEAD_DIM ** -0.5)
    ki = rope(k_idx[:, :, None, :], pos, IDX_ROPE)[:, :, 0, :]
    wi = w_idx * (IDX_HEADS ** -0.5)
    key_chunk = pos // CHUNK
    n_blocks = S // DSA_Q_BLOCK
    gather_rows = jax.vmap(lambda kb, ib: kb[ib])

    def block(i):
        start = i * DSA_Q_BLOCK
        qi_b = lax.dynamic_slice_in_dim(qi, start, DSA_Q_BLOCK, axis=1)
        wi_b = lax.dynamic_slice_in_dim(wi, start, DSA_Q_BLOCK, axis=1)
        q_b = lax.dynamic_slice_in_dim(q, start, DSA_Q_BLOCK, axis=1)
        q_chunk = lax.dynamic_slice_in_dim(key_chunk, start, DSA_Q_BLOCK)
        raw = jnp.einsum('bqhd,bsd->bqhs', qi_b, ki)
        score = jnp.einsum('bqh,bqhs->bqs', wi_b, jax.nn.relu(raw)).astype(jnp.float32)
        admissible = key_chunk[None, :] <= q_chunk[:, None]
        score = jnp.where(admissible[None], score, -jnp.inf)
        _, sel = lax.top_k(score, top_k)
        valid = (sel // CHUNK) <= q_chunk[None, :, None]
        k_sel = gather_rows(k, sel)
        v_sel = gather_rows(v, sel)
        s = jnp.einsum('bqhd,bqkhd->bqhk', q_b, k_sel).astype(jnp.float32)
        s = jnp.where(valid[:, :, None, :], s, -jnp.inf)
        p = jax.nn.softmax(s, axis=-1).astype(v.dtype)
        return jnp.einsum('bqhk,bqkhd->bqhd', p, v_sel)

    o = lax.map(block, jnp.arange(n_blocks))
    return o.transpose(1, 0, 2, 3, 4).reshape(B, S, DSA_HEADS * DSA_HEAD_DIM)

def moe_ffn(xn, w_router, b_router, w_gate_up, b_gate_up, w_down, b_down):
    B, S, D = xn.shape
    T = B * S
    xt = xn.reshape(T, D)
    logits = (xt @ w_router + b_router).astype(jnp.float32)
    top_vals, top_idx = lax.top_k(logits, MOE_TOP_K)
    gates = jax.nn.softmax(top_vals, axis=-1)
    A = T * MOE_TOP_K
    e_flat = top_idx.reshape(A)
    tok_flat = jnp.arange(A, dtype=jnp.int32) // MOE_TOP_K
    g_flat = gates.reshape(A)
    order = jnp.argsort(e_flat)
    e_s, tok_s, g_s = e_flat[order], tok_flat[order], g_flat[order]
    counts = jax.ops.segment_sum(jnp.ones((A,), jnp.int32), e_flat, num_segments=N_EXPERTS)
    offsets = jnp.cumsum(counts) - counts
    padded = ((counts + MOE_BLOCK - 1) // MOE_BLOCK) * MOE_BLOCK
    pad_end = jnp.cumsum(padded)
    pad_off = pad_end - padded
    dest = pad_off[e_s] + jnp.arange(A, dtype=jnp.int32) - offsets[e_s]
    P = A + N_EXPERTS * MOE_BLOCK
    n_blocks = P // MOE_BLOCK
    tok_buf = jnp.full((P,), T, jnp.int32).at[dest].set(tok_s)
    g_buf = jnp.zeros((P,), jnp.float32).at[dest].set(g_s)
    blk_start = jnp.arange(n_blocks, dtype=jnp.int32) * MOE_BLOCK
    blk_expert = jnp.minimum(jnp.searchsorted(pad_end, blk_start, side='right'), N_EXPERTS - 1)
    x_pad = jnp.concatenate([xt, jnp.zeros((1, D), xt.dtype)], axis=0)

    def expert_block(args):
        toks, e = args
        xb = x_pad[toks]
        h = xb @ w_gate_up[e] + b_gate_up[e]
        gate = jnp.minimum(h[:, :D_EXPERT], SWIGLU_LIMIT)
        lin = jnp.clip(h[:, D_EXPERT:], -SWIGLU_LIMIT, SWIGLU_LIMIT)
        glu = gate * jax.nn.sigmoid(SWIGLU_ALPHA * gate)
        return ((lin + 1.0) * glu) @ w_down[e] + b_down[e]

    y = lax.map(expert_block, (tok_buf.reshape(n_blocks, MOE_BLOCK), blk_expert))
    y = y.reshape(P, D) * g_buf[:, None].astype(y.dtype)
    out = jnp.zeros((T + 1, D), y.dtype).at[tok_buf].add(y)[:T]
    return out.reshape(B, S, D)

def setup_inputs(seed: int = 0) -> dict:
    key = jax.random.key(seed)
    ks = jax.random.split(key, 20)

    def w(k, shape, fan_in):
        return jax.random.normal(k, shape, jnp.float32) * (fan_in ** -0.5)

    def gain(k, shape):
        return 1.0 + 0.05 * jax.random.normal(k, shape, jnp.float32)

    def bias(k, shape, scale=0.01):
        return scale * jax.random.normal(k, shape, jnp.float32)

    L = DEPTH
    return {
        "x": jax.random.normal(ks[0], (BATCH, SEQ, D_MODEL), jnp.float32),
        "norm_attn_g": gain(ks[1], (L, D_MODEL)),
        "w_in": w(ks[2], (L, D_MODEL, D_IN), D_MODEL),
        "q_lora_g": gain(ks[3], (L, MLA_Q_LORA)),
        "kv_lora_g": gain(ks[4], (L, MLA_KV_LORA)),
        "w_uq": w(ks[5], (L, MLA_Q_LORA, MLA_HEADS * MLA_QK), MLA_Q_LORA),
        "w_uk": w(ks[6], (L, MLA_KV_LORA, MLA_HEADS * MLA_NOPE), MLA_KV_LORA),
        "w_uv": w(ks[7], (L, MLA_KV_LORA, MLA_HEADS * MLA_V), MLA_KV_LORA),
        "w_o_mla": w(ks[8], (L, MLA_HEADS * MLA_V, D_MODEL), MLA_HEADS * MLA_V),
        "w_o_dsa": w(ks[9], (L, DSA_HEADS * DSA_HEAD_DIM, D_MODEL), DSA_HEADS * DSA_HEAD_DIM),
        "b_gate": bias(ks[10], (L, N_BRANCHES * D_MODEL), 0.1),
        "w_out": w(ks[11], (L, D_MODEL, D_MODEL), D_MODEL),
        "norm_ffn_g": gain(ks[12], (L, D_MODEL)),
        "w_router": w(ks[13], (L, D_MODEL, N_EXPERTS), D_MODEL),
        "b_router": bias(ks[14], (L, N_EXPERTS)),
        "w_gate_up": w(ks[15], (L, N_EXPERTS, D_MODEL, 2 * D_EXPERT), D_MODEL),
        "b_gate_up": bias(ks[16], (L, N_EXPERTS, 2 * D_EXPERT)),
        "w_down": w(ks[17], (L, N_EXPERTS, D_EXPERT, D_MODEL), D_EXPERT),
        "b_down": bias(ks[18], (L, N_EXPERTS, D_MODEL)),
        "norm_final_g": gain(ks[19], (D_MODEL,)),
    }

def reference(x, norm_attn_g, w_in, q_lora_g, kv_lora_g, w_uq, w_uk, w_uv, w_o_mla, w_o_dsa,
              b_gate, w_out, norm_ffn_g, w_router, b_router, w_gate_up, b_gate_up, w_down,
              b_down, norm_final_g):
    B, S, D = x.shape
    pos = jnp.arange(S, dtype=jnp.int32)
    top_k = min(DSA_TOPK_MAX, S // 4)
    for l in range(DEPTH):
        h = rms_norm(x, norm_attn_g[l])
        proj = h @ w_in[l]
        c_q, c_kv, k_r, qkv, q_idx, k_idx, w_idx, gate_cols = split_cols(proj)
        y_a = mla_attention(c_q, c_kv, k_r, q_lora_g[l], kv_lora_g[l],
                            w_uq[l], w_uk[l], w_uv[l], pos) @ w_o_mla[l]
        y_b = dsa_attention(qkv, q_idx, k_idx, w_idx, pos, top_k) @ w_o_dsa[l]
        g = jax.nn.sigmoid(gate_cols + b_gate[l]).reshape(B, S, N_BRANCHES, D)
        merged = g[:, :, 0, :] * y_a + g[:, :, 1, :] * y_b
        x = x + merged @ w_out[l]
        hn = rms_norm(x, norm_ffn_g[l])
        x = x + moe_ffn(hn, w_router[l], b_router[l], w_gate_up[l], b_gate_up[l],
                        w_down[l], b_down[l])
    return rms_norm(x, norm_final_g)


_drawn_inputs = setup_inputs


def setup_inputs(seed=0):
    import zlib

    import numpy as np

    out = dict(_drawn_inputs(seed))
    spreads = {}
    factors = {'q_lora_g': 2.893, 'b_gate_up': 8.0, 'b_down': 8.0}
    for name, (base, spread) in spreads.items():
        noise = np.random.default_rng([zlib.crc32(name.encode()), seed]).standard_normal(out[name].shape)
        drawn = base * np.exp(spread * noise) if base else spread * noise
        out[name] = __import__('jax').numpy.asarray(drawn.astype(out[name].dtype))
    for name, factor in factors.items():
        out[name] = (out[name] * factor).astype(out[name].dtype)
    return out
```

```python
import concourse.bass as bass
from concourse import mybir
from contextlib import ExitStack

D_MODEL = 1024
SEQ = 256
CHUNK = 64
NORM_EPS = 1e-6
ROPE_THETA = 10000.0
HEADS = 8
HD = 128
Q_LORA = 384
KV_LORA = 256
MLA_ROPE = 64
MLA_QK = HD + MLA_ROPE
IDX_HEADS = 8
IDX_DIM = 64
IDX_ROPE = 32
TOP_K = SEQ // 4
N_EXPERTS = 32
MOE_TOP_K = 4
D_EXPERT = 1024
SWIGLU_LIMIT = 7.0
SWIGLU_ALPHA = 1.702

P = 128
T = SEQ // P
KD = D_MODEL // P
COLS = 512
W_LAT = Q_LORA + KV_LORA + MLA_ROPE
W_IDX = IDX_HEADS * IDX_DIM + IDX_DIM + IDX_HEADS
C_QKV = W_LAT
C_IDX = C_QKV + 3 * HEADS * HD
C_GATE = C_IDX + W_IDX
D_IN = C_GATE + 2 * D_MODEL
LATC = W_LAT // 2
IDXC = W_IDX // 2

SLOTS = 64
ASSIGNED = SEQ * MOE_TOP_K
MAX_ITEMS = N_EXPERTS + (ASSIGNED - 1) // SLOTS
ITEM_COLS = 48
assert MAX_ITEMS < ITEM_COLS

MASKED = -(2.0 ** 100)
TAKEN = -(2.0 ** 127)

RING = 6
RINGW = 4096

CONST = {}
_at = 0
for _name, _w in (("ident", P), ("cos_d", T * HD), ("sin_d", T * HD), ("cos_m", T * MLA_ROPE),
                  ("sin_m", T * MLA_ROPE), ("cos_i", T * IDX_ROPE), ("sin_i", T * IDX_ROPE),
                  ("chunk_mask", 3 * P), ("before", P), ("ones", P), ("slot_no", SLOTS),
                  ("item_base", ITEM_COLS), ("item_no", ITEM_COLS), ("first_row", SLOTS), ("zero", P)):
    CONST[_name] = (_at, _w)
    _at += _w
CONST_W = _at


def hybrid_block_kernel(nc, x, norm_attn_g, w_in, q_lora_g, kv_lora_g, w_uq, w_uk, w_uv, w_o_mla, w_o_dsa,
                        b_gate, w_out, norm_ffn_g, w_router, b_router, w_gate_up, b_gate_up, w_down,
                        b_down, norm_final_g, consts, out):
    fp32 = mybir.dt.float32
    i32 = mybir.dt.int32
    ALU = mybir.AluOpType
    ACT = mybir.ActivationFunctionType
    AX = mybir.AxisListType.X

    x_v = x.rearrange("b (t p) d -> p (b t) d", p=P)
    out_v = out.rearrange("b (t p) d -> p (b t) d", p=P)
    w_in_v = w_in.rearrange("a (k p) n -> p (a k) n", p=P)
    uq_v = w_uq.rearrange("a (k p) (h c) -> p (a k) h c", p=P, c=MLA_QK)
    uk_v = w_uk.rearrange("a (k p) n -> p (a k) n", p=P)
    uv_v = w_uv.rearrange("a (k p) n -> p (a k) n", p=P)
    oa_v = w_o_mla.rearrange("a (k p) n -> p (a k) n", p=P)
    ob_v = w_o_dsa.rearrange("a (k p) n -> p (a k) n", p=P)
    wo_v = w_out.rearrange("a (k p) n -> p (a k) n", p=P)
    wr_v = w_router.rearrange("a (k p) n -> p (a k) n", p=P)
    gu_v = w_gate_up.rearrange("a e (h p k) n -> (a e) h p k n", h=2, k=4)
    dn_v = w_down.rearrange("a e (h p k) n -> (a e) h p k n", h=2, k=4)
    bgu_v = b_gate_up.rearrange("a e n -> (a e) n")
    bdn_v = b_down.rearrange("a e n -> (a e) n")

    READER = {"lat0": "lat01", "lat1": "lat11", "idx0": "idx01", "idx1": "idx11", "uqn": "qn3", "uqr": "qr1",
              "ukv": "vm11"}
    READER.update({f"qkv{c}": (f"qk{c}1" if c < 4 else f"v{c - 4}1") for c in range(6)})
    READER.update({f"gate{c}": f"gate{c}1" for c in range(4)})
    READER.update({f"{u}{c}": f"{n}{c}1" for u, n in (("oa", "ya"), ("ob", "yb"), ("wo", "xo")) for c in range(2)})
    UNITS = list(READER)
    DMAS = {"uqn": 3, "uqr": 3, "ukv": 2}
    NU = len(UNITS)
    loaded = [0] * RING
    UNIT = {}
    for n, name in enumerate(UNITS):
        s = n % RING
        loaded[s] += 16 * DMAS.get(name, 1)
        UNIT[name] = (s, loaded[s], UNITS[n - RING] if n >= RING else None)
    ITEM_SLOT = [(NU + j) % RING for j in range(RING)]
    LOADED0 = [loaded[s] for s in ITEM_SLOT]
    LAST_FRONT = [READER[UNITS[NU - RING + j]] for j in range(RING)]
    GU_UNITS = 4

    tiles = [f"hT{t}{q}" for t in range(T) for q in range(2)]
    tiles += [f"lat{c}{t}" for c in range(2) for t in range(T)]
    tiles += [f"idx{c}{t}" for c in range(2) for t in range(T)]
    tiles += [f"{n}{t}" for t in range(T) for n in ("cqT", "ckvT")]
    tiles += [f"qn{g}" for g in range(4)] + [f"qr{t}" for t in range(T)] + [f"kn{g}" for g in range(4)]
    tiles += [f"vm{c}{t}" for c in range(2) for t in range(T)]
    tiles += [f"qiT{t}" for t in range(T)] + ["kiT"] + [f"qrT{t}" for t in range(T)]
    tiles += [f"raw{t}{g}" for t in range(T) for g in range(4)]
    QK = [(c, t) for c in range(4) for t in range(T)]
    for n in range(len(QK) + 1):
        if n < len(QK):
            tiles.append("qk%d%d" % QK[n])
        if n:
            tiles.append("qkT%d%d" % QK[n - 1])
    tiles += [f"v{c}{t}" for c in range(2) for t in range(T)]
    NH = 2 * HEADS
    for s in range(NH + 3):
        tiles += [f"s{s}"] * (s < NH) + [f"pT{s - 2}"] * (2 <= s < NH + 2) + [f"o{s - 3}"] * (s >= 3)
    tiles += [f"gate{c}{t}" for c in range(4) for t in range(T)]
    tiles += [f"{n}{c}{t}" for n in ("ya", "yb") for c in range(2) for t in range(T)]
    tiles += [f"mT{t}{q}" for t in range(T) for q in range(2)]
    tiles += [f"xo{c}{t}" for c in range(2) for t in range(T)]
    tiles += [f"nT{t}{q}" for t in range(T) for q in range(2)]
    tiles += ["logits", "rank", "count", "gT"]
    NBANK = 8
    ROUTING = {"logits": 4, "rank": 5, "count": 6, "gT": 7}
    TILE, USES = {}, [0] * NBANK
    for n, name in enumerate(tiles):
        b = ROUTING.get(name, n % NBANK)
        TILE[name] = (b, USES[b])
        USES[b] += 1

    with ExitStack() as ctx:
        def sb(name, cols, parts=P, dt=fp32):
            return ctx.enter_context(nc.sbuf_tensor(name, [parts, cols], dt))

        def sem(name):
            return ctx.enter_context(nc.semaphore(name))

        ring = [sb(f"ring{s}", RINGW) for s in range(RING)]
        cst = sb("cst", CONST_W)
        resid = sb("resid", T * D_MODEL)
        hT_m = sb("hT_m", KD * SEQ)
        mem_q = sb("mem_q", 2048)
        mem_k = sb("mem_k", 2048)
        mem_v = sb("mem_v", 2048)
        mem_qn = sb("mem_qn", 2048)
        mem_qr = sb("mem_qr", 1024)
        mem_kv = sb("mem_kv", 4096)
        mem_lt = sb("mem_lt", 1280)
        roped = sb("roped", 3 * COLS)
        rot_a = sb("rot_a", COLS)
        rot_b = sb("rot_b", COLS)
        att = sb("att", 7 * 3 * P)
        kr_pad = sb("kr_pad", T * 3 * MLA_ROPE)
        ki_pad = sb("ki_pad", T * 3 * IDX_DIM)
        krT = sb("krT", 2 * SEQ)
        score = sb("score", 3 * P)
        sel_mask = sb("sel_mask", 3 * P)
        top8 = sb("top8", 8)
        wi = sb("wi", T * IDX_HEADS)
        ssq = sb("ssq", 4)
        msq = sb("msq", 4)
        root = sb("root", 4)
        rstd = sb("rstd", 4)
        negmax = sb("negmax", T * NH)
        psums = sb("psums", T * NH)
        rsum = sb("rsum", T * NH)
        table_i = sb("table_i", 64, 1, i32)

        def const(name, t=None):
            a, w = CONST[name]
            if t is None:
                return cst[:, a:a + w]
            w //= T
            return cst[:, a + t * w:a + (t + 1) * w]

        ident = const("ident")

        X = resid[:, :].rearrange("p (t d) -> p t d", t=T)
        HT = hT_m[:, :].rearrange("p (k n) -> p k n", k=KD)
        H = mem_q[:, :].rearrange("p (t d) -> p t d", t=T)
        QI = mem_q[:, 0:1024].rearrange("p (g n) -> p g n", g=4)
        QT = mem_q[:, :].rearrange("p (h n) -> p h n", h=HEADS)
        IDX = mem_k[:, 0:T * W_IDX].rearrange("p (t d) -> p t d", t=T)
        KI = mem_k[:, 1280:1280 + 2 * SEQ].rearrange("p (e n) -> p e n", e=2)
        KT = mem_k[:, :].rearrange("p (h n) -> p h n", h=HEADS)
        gain_ffn = mem_k[:, 0:D_MODEL]
        gain_out = mem_k[:, D_MODEL:2 * D_MODEL]
        LAT = mem_v[:, 0:T * W_LAT].rearrange("p (t d) -> p t d", t=T)
        VD = mem_v[:, :].rearrange("p (t d) -> p t d", t=T)
        MG = VD
        HN = VD
        QN = mem_qn[:, :].rearrange("p (h n) -> p h n", h=HEADS)
        lora_gain = mem_qr[:, 0:Q_LORA + KV_LORA]
        QR = mem_qr[:, :].rearrange("p (g n) -> p g n", g=4)
        gain_attn = mem_kv[:, 0:D_MODEL]
        KN = mem_kv[:, 0:2048].rearrange("p (h n) -> p h n", h=HEADS)
        VM = mem_kv[:, 2048:4096].rearrange("p (t d) -> p t d", t=T)
        G = mem_kv[:, :].rearrange("p (t d) -> p t d", t=T)
        gate_bias = [mem_qr[:, 0:COLS], mem_qr[:, COLS:2 * COLS], mem_lt[:, 0:COLS], mem_lt[:, COLS:2 * COLS]]
        LT = mem_lt[:, :].rearrange("p (k n) -> p k n", k=5)
        KR = krT[:, :].rearrange("p (e n) -> p e n", e=2)
        S = [att[:, 3 * P * b:3 * P * (b + 1)] for b in range(2)]
        PR = [att[:, 3 * P * (2 + b):3 * P * (3 + b)] for b in range(3)]
        PT = [att[:, 3 * P * (5 + b):3 * P * (6 + b)] for b in range(2)]
        RELU = [att[:, COLS * b:COLS * (b + 1)] for b in range(2)]
        q_rot = [att[:, COLS * (2 + t):COLS * (3 + t)] for t in range(T)]
        w_rt = att[:, 0:KD * N_EXPERTS].rearrange("p (k n) -> p k n", k=KD)
        b_rt = att[:, KD * N_EXPERTS:(KD + 1) * N_EXPERTS]

        XG = mem_q[:, 0:512]
        XGT = mem_q[:, 512:1024].rearrange("p (k s) -> p k s", k=4)
        GC = mem_q[:, 1024:1536]
        LN = mem_q[:, 1536:2048]
        SG = mem_qn[:, 0:512]
        GLU = mem_qn[:, 512:1024]
        AC = mem_qn[:, 1024:1536]
        ACT_T = mem_qn[:, 1536:2048].rearrange("p (k s) -> p k s", k=4)
        Y = mem_qr[:, 0:512]
        PGT = mem_qr[:, 512:1024].rearrange("p (h n) -> p h n", h=2)
        BIAS = mem_kv[:, 0:2048]
        _r = [2048]

        def rt(cols):
            _r[0] += cols
            return mem_kv[:, _r[0] - cols:_r[0]]

        TE = T * N_EXPERTS
        LG, LGE, CH, GT_, D2, ITV, U2, VG = [rt(TE) for _ in range(8)]
        LPAD = rt(T * (N_EXPERTS + 4))
        REP = rt(T * 8)
        nmx, gs, grs, W1, GW = [rt(T) for _ in range(5)]
        NB, ITEM_END, ITEM_AT = [rt(N_EXPERTS) for _ in range(3)]
        ET = mem_qn[:, 0:ITEM_COLS * N_EXPERTS]
        ER = mem_lt[:, 1024:1024 + 64]
        GP = mem_lt[:, 0:T * SLOTS].rearrange("p (t s) -> p t s", t=T)
        PG = mem_lt[:, 128:128 + T * 3 * SLOTS].rearrange("p (t s) -> p t s", t=T)
        assert _r[0] <= 4096
        Y_0 = mem_kv[:, _r[0]:_r[0] + COLS]
        assert _r[0] + COLS <= 4096

        def by_te(ap):
            return ap.rearrange("p (t e) -> p t e", t=T)

        LG3, LGE3, CH3, GT3, D23, LPAD3, REP3 = [by_te(a) for a in (LG, LGE, CH, GT_, D2, LPAD, REP)]
        kr_pad3 = kr_pad[:, :].rearrange("p (t d) -> p t d", t=T)
        ki_pad3 = ki_pad[:, :].rearrange("p (t d) -> p t d", t=T)

        bank = [ctx.enter_context(nc.psum_tensor(f"bank{b}", [P, COLS], fp32)) for b in range(NBANK)]
        BG, BL, BY, BM = bank[4], bank[5], bank[6], bank[7]

        def ps(name):
            return bank[TILE[name][0]]

        unit_loaded = [sem(f"unit_loaded{s}") for s in range(RING)]
        unit_used = [sem(f"unit_used{j}") for j in range(RING)]
        psum_full = [sem(f"psum_full{b}") for b in range(NBANK)]
        psum_emptied = [sem(f"psum_emptied{b}") for b in range(NBANK)]
        const_in = sem("const_in")
        x_in = sem("x_in")
        gain_in = sem("gain_in")
        lora_in = sem("lora_in")
        gate_bias_in = sem("gate_bias_in")
        router_in = sem("router_in")
        out_gain_in = sem("out_gain_in")
        b_down_in = sem("b_down_in")
        bias_in = sem("bias_in")
        squares = sem("squares")
        means = sem("means")
        roots = sem("roots")
        h_ready = sem("h_ready")
        lat_ready = sem("lat_ready")
        idx_roped = sem("idx_roped")
        kr_roped = sem("kr_roped")
        tok_roped = sem("tok_roped")
        relu_used = sem("relu_used")
        masked = sem("masked")
        exped = sem("exped")
        normed = sem("normed")
        gate_sig = sem("gate_sig")
        merged = sem("merged")
        resid_done = sem("resid_done")
        hn_ready = sem("hn_ready")
        logits_in = sem("logits_in")
        router_exp = sem("router_exp")
        chosen = sem("chosen")
        table = sem("table")
        gates_in = sem("gates_in")
        pads_zero = sem("pads_zero")
        zeroed = sem("zeroed")
        dve_step = sem("dve_step")
        p_ready = sem("p_ready")
        pg_ready = sem("pg_ready")
        xg_ps = sem("xg_ps")
        xg_sb = sem("xg_sb")
        xgT_ps = sem("xgT_ps")
        xgT_sb = sem("xgT_sb")
        bias_used = sem("bias_used")
        h_done = sem("h_done")
        clipped = sem("clipped")
        sig = sem("sig")
        act_ready = sem("act_ready")
        actT_ps = sem("actT_ps")
        actT_sb = sem("actT_sb")
        y_ps = sem("y_ps")
        y_sb = sem("y_sb")
        pgT_ps = sem("pgT_ps")
        pgT_sb = sem("pgT_sb")
        acc_done = sem("acc_done")
        moe_step = sem("moe_step")
        out_ready = sem("out_ready")
        stored = sem("stored")

        block = ctx.enter_context(nc.Block())

        def wait_full(eng, name):
            b, n = TILE[name]
            eng.wait_ge(psum_full[b], n + 1)

        def wait_sb(eng, name):
            b, n = TILE[name]
            eng.wait_ge(psum_emptied[b], n + 1)

        def emptied(name):
            return psum_emptied[TILE[name][0]]

        def full(name):
            return psum_full[TILE[name][0]]

        def row(v):
            return v.rearrange("a n -> (a n)").partition_broadcast(P)

        def tok(t):
            return slice(t * P, (t + 1) * P)

        @block.sync
        def _(sp):
            def load(name, parts):
                slot, _, before = UNIT[name]
                if before:
                    wait_full(sp, READER[before])
                for dst, src in parts(ring[slot]):
                    sp.dma_start(dst, src).then_inc(unit_loaded[slot], 16)

            def cols(view, a, n, k):
                return lambda r: [(r[:, 0:k * n].rearrange("p (k n) -> p k n", k=k), view[:, :, a:a + n])]

            for c in range(2):
                load(f"lat{c}", cols(w_in_v, c * LATC, LATC, KD))
            for c in range(2):
                load(f"idx{c}", cols(w_in_v, C_IDX + c * IDXC, IDXC, KD))
            load("uqn", lambda r: [(r[:, k * 1024:(k + 1) * 1024].rearrange("p (h c) -> p h c", c=HD),
                                    uq_v[:, k, :, 0:HD]) for k in range(3)])
            load("uqr", lambda r: [(r[:, k * 512:(k + 1) * 512].rearrange("p (h c) -> p h c", c=MLA_ROPE),
                                    uq_v[:, k, :, HD:MLA_QK]) for k in range(3)])
            load("ukv", lambda r: [(r[:, v * 2048:(v + 1) * 2048].rearrange("p (k n) -> p k n", k=2), w)
                                   for v, w in enumerate((uk_v, uv_v))])
            for c in range(6):
                load(f"qkv{c}", cols(w_in_v, C_QKV + c * COLS, COLS, KD))
            for c in range(4):
                load(f"gate{c}", cols(w_in_v, C_GATE + c * COLS, COLS, KD))
            for n, v in (("oa", oa_v), ("ob", ob_v), ("wo", wo_v)):
                for c in range(2):
                    load(f"{n}{c}", cols(v, c * COLS, COLS, KD))

            def item_load(j, e):
                slot = ITEM_SLOT[j]
                if j < GU_UNITS:
                    src = gu_v[e, j // 2, :, 2 * (j % 2):2 * (j % 2) + 2, :].rearrange("e p k n -> p (e k) n")
                    dst = ring[slot][:, :].rearrange("p (k n) -> p k n", k=2)
                else:
                    src = dn_v[e, j - GU_UNITS, :, :, :].rearrange("e p k n -> p (e k) n")
                    dst = ring[slot][:, :].rearrange("p (k n) -> p k n", k=4)
                sp.dma_start(dst, src).then_inc(unit_loaded[slot], 16)

            for j in range(RING):
                wait_full(sp, LAST_FRONT[j])
                item_load(j, slice(0, 1))
            sp.wait_ge(zeroed, 1)
            sp.dma_start(BIAS[0:1, :], bgu_v[0:1, :]).then_inc(bias_in, 16)
            sp.wait_ge(table, 1)
            n_items = sp.value_load(table_i[0:1, ITEM_COLS:ITEM_COLS + 1], min_val=N_EXPERTS, max_val=MAX_ITEMS)
            with sp.Fori(1, MAX_ITEMS) as i:
                with sp.If(i < n_items):
                    e = sp.value_load(table_i[0:1, bass.ds(i, 1)], min_val=0, max_val=N_EXPERTS - 1)
                    for j in range(RING):
                        if j == 3:
                            sp.wait_ge(h_done, i)
                        elif j == 5:
                            sp.wait_ge(y_ps, i)
                        else:
                            sp.wait_ge(unit_used[j], i)
                        item_load(j, bass.ds(e, 1))
                        if j == 0:
                            sp.wait_ge(bias_used, i)
                            sp.dma_start(BIAS[0:1, :], bgu_v[bass.ds(e, 1), :]).then_inc(bias_in, 16)
            for t in range(T):
                sp.wait_ge(out_ready, t + 1)
                sp.dma_start(out_v[:, t, :], X[:, t, :]).then_inc(stored, 16)
            sp.wait_ge(stored, 16 * T)

        @block.gpsimd
        def _(pool):
            nc.gpsimd.memset(kr_pad[:, :], 0.0).then_inc(pads_zero, 1)
            nc.gpsimd.memset(ki_pad[:, :], 0.0).then_inc(pads_zero, 1)
            wait_sb(pool, f"yb1{T - 1}")
            nc.gpsimd.memset(BIAS[:, :], 0.0).then_inc(zeroed, 1)
            nc.gpsimd.memset(PG[:, :, :], 0.0).then_inc(zeroed, 1)
            nc.gpsimd.memset(Y_0, 0.0).then_inc(zeroed, 1)
            pool.wait_ge(zeroed, 3)
            for h in range(2):
                pool.dma_start(Y_0[SLOTS * h:SLOTS * h + N_EXPERTS, :], bdn_v[:, h * COLS:(h + 1) * COLS])\
                    .then_inc(b_down_in, 16)
            pool.wait_ge(b_down_in, 32)

        @block.scalar
        def _(act):
            for t in range(T):
                act.dma_start(X[:, t, :], x_v[:, t, :]).then_inc(x_in, 16)
            act.dma_start(gain_attn, row(norm_attn_g)).then_inc(gain_in, 16)
            act.dma_start(cst[:, :], consts).then_inc(const_in, 16)
            act.dma_start(lora_gain[:, 0:Q_LORA], row(q_lora_g)).then_inc(lora_in, 16)
            act.dma_start(lora_gain[:, Q_LORA:Q_LORA + KV_LORA], row(kv_lora_g)).then_inc(lora_in, 16)

            n_squares = [0]

            def square(dst, src, junk):
                if n_squares[0]:
                    act.wait_ge(squares, n_squares[0])
                nc.scalar.activation(junk, src, ACT.Square, accum_out=dst).then_inc(squares, 1)
                n_squares[0] += 1

            def roots_of(n, count):
                act.wait_ge(means, n)
                nc.scalar.activation(root[:, 0:count], msq[:, 0:count], ACT.Sqrt).then_inc(roots, 1)

            def evacuate(name, dst, src):
                wait_full(act, name)
                nc.scalar.activation(dst, src, ACT.Copy).then_inc(emptied(name), 1)

            def blocks(name, k=4):
                return ps(name)[:, 0:k * P].rearrange("p (k n) -> p k n", k=k)

            act.wait_ge(x_in, 16 * T)
            for t in range(T):
                square(ssq[:, t:t + 1], X[:, t, :], hT_m[:, 0:D_MODEL])
            roots_of(1, T)
            for t in range(T):
                for q in range(2):
                    evacuate(f"hT{t}{q}", HT[:, 4 * q:4 * q + 4, tok(t)], blocks(f"hT{t}{q}"))
            for c in range(2):
                for t in range(T):
                    evacuate(f"lat{c}{t}", LAT[:, t, c * LATC:(c + 1) * LATC], ps(f"lat{c}{t}")[:, 0:LATC])
            wait_sb(act, f"lat1{T - 1}")
            for t in range(T):
                square(ssq[:, t:t + 1], LAT[:, t, 0:Q_LORA], att[:, 0:Q_LORA])
                square(ssq[:, T + t:T + t + 1], LAT[:, t, Q_LORA:Q_LORA + KV_LORA], att[:, 0:KV_LORA])
            roots_of(2, 2 * T)
            for c in range(2):
                for t in range(T):
                    evacuate(f"idx{c}{t}", IDX[:, t, c * IDXC:(c + 1) * IDXC], ps(f"idx{c}{t}")[:, 0:IDXC])
            for t in range(T):
                evacuate(f"cqT{t}", LT[:, 0:3, tok(t)], blocks(f"cqT{t}", 3))
                n = f"ckvT{t}"
                wait_full(act, n)
                nc.scalar.activation(LT[:, 3:5, tok(t)], blocks(n)[:, 0:2, :], ACT.Copy)
                nc.scalar.activation(KR[:, :, tok(t)], blocks(n)[:, 2:4, :], ACT.Copy).then_inc(emptied(n), 1)
            for g in range(4):
                evacuate(f"qn{g}", QN[:, 2 * g:2 * g + 2, :], ps(f"qn{g}")[:, :].rearrange("p (h n) -> p h n", h=2))
            for g in range(4):
                evacuate(f"kn{g}", KN[:, 2 * g:2 * g + 2, :], ps(f"kn{g}")[:, :].rearrange("p (h n) -> p h n", h=2))
            for c in range(2):
                for t in range(T):
                    evacuate(f"vm{c}{t}", VM[:, t, c * COLS:(c + 1) * COLS], ps(f"vm{c}{t}")[:, :])
            for t in range(T):
                evacuate(f"qiT{t}", QI[:, :, tok(t)], blocks(f"qiT{t}"))
            evacuate("kiT", KI[:, :, :].rearrange("p e (t n) -> p e t n", t=T),
                     ps("kiT")[:, :].rearrange("p (t e n) -> p e t n", t=T, e=2))
            for t in range(T):
                evacuate(f"qrT{t}", QR[:, :, tok(t)], blocks(f"qrT{t}"))
            for t in range(T):
                for g in range(4):
                    n, keys, u = f"raw{t}{g}", P * (t + 1), 4 * t + g
                    if u >= 2:
                        act.wait_ge(relu_used, u - 1)
                    wait_full(act, n)
                    nc.scalar.activation(RELU[u % 2][:, 0:2 * keys], ps(n)[:, 0:2 * keys], ACT.Relu,
                                         scale=IDX_DIM ** -0.5).then_inc(emptied(n), 1)
            for c, t in QK:
                evacuate(f"qkT{c}{t}", (QT, KT)[c // 2][:, 4 * (c % 2):4 * (c % 2) + 4, tok(t)], blocks(f"qkT{c}{t}"))
            for c in range(2):
                for t in range(T):
                    evacuate(f"v{c}{t}", VD[:, t, c * COLS:(c + 1) * COLS], ps(f"v{c}{t}")[:, :])
            for s in range(NH + 2):
                if s < NH:
                    act.wait_ge(masked, s + 1)
                    for t in range(T):
                        a, w, col = t * P, P * (t + 1), s * T + t
                        nc.scalar.activation(PR[s % 3][:, a:a + w], S[s % 2][:, a:a + w], ACT.Exp,
                                             bias=negmax[:, col:col + 1],
                                             accum_out=psums[:, col:col + 1]).then_inc(exped, 1)
                if s >= 2:
                    evacuate(f"pT{s - 2}", PT[s % 2], ps(f"pT{s - 2}")[:, 0:3 * P])
                if s == HEADS + 2:
                    for c in range(4):
                        act.dma_start(gate_bias[c], b_gate[0, c * COLS:(c + 1) * COLS].partition_broadcast(P))\
                            .then_inc(gate_bias_in, 16)
            act.dma_start(gain_ffn, row(norm_ffn_g)).then_inc(gain_in, 16)
            act.dma_start(gain_out, norm_final_g.partition_broadcast(P)).then_inc(out_gain_in, 16)
            act.dma_start(w_rt, wr_v).then_inc(router_in, 16)
            act.dma_start(b_rt, row(b_router)).then_inc(router_in, 16)
            for c in range(4):
                for t in range(T):
                    wait_sb(act, f"gate{c}{t}")
                    g = G[:, t, c * COLS:(c + 1) * COLS]
                    nc.scalar.activation(g, g, ACT.Sigmoid).then_inc(gate_sig, 1)
            for t in range(T):
                for q in range(2):
                    evacuate(f"mT{t}{q}", HT[:, 4 * q:4 * q + 4, tok(t)], blocks(f"mT{t}{q}"))
            for c in range(2):
                for t in range(T):
                    wait_sb(act, f"xo{c}{t}")
            for t in range(T):
                square(ssq[:, t:t + 1], X[:, t, :], mem_q[:, 0:D_MODEL])
            roots_of(3, T)
            for t in range(T):
                for q in range(2):
                    evacuate(f"nT{t}{q}", HT[:, 4 * q:4 * q + 4, tok(t)], blocks(f"nT{t}{q}"))
            act.wait_ge(b_down_in, 32)
            nc.scalar.activation(Y, Y_0, ACT.Copy).then_inc(y_sb, 1)
            act.wait_ge(logits_in, 1)
            for t in range(T):
                e = slice(t * N_EXPERTS, (t + 1) * N_EXPERTS)
                nc.scalar.activation(LGE[:, e], LG[:, e], ACT.Exp, bias=nmx[:, t:t + 1]).then_inc(router_exp, 1)

            def gathered(item):
                act.wait_ge(xg_ps, item + 1)
                nc.scalar.activation(XG, BM[:, :], ACT.Copy).then_inc(xg_sb, 1)
                act.wait_ge(xgT_ps, item + 1)
                nc.scalar.activation(XGT, BY[:, :].rearrange("p (k s) -> p k s", k=4), ACT.Copy).then_inc(xgT_sb, 1)

            gathered(0)
            act.wait_ge(table, 1)
            n_items = act.value_load(table_i[0:1, ITEM_COLS:ITEM_COLS + 1], min_val=N_EXPERTS, max_val=MAX_ITEMS)
            with act.Fori(0, MAX_ITEMS) as i:
                with act.If(i < n_items):
                    act.wait_ge(clipped, i + 1)
                    nc.scalar.activation(SG, GC, ACT.Sigmoid, scale=SWIGLU_ALPHA).then_inc(sig, 1)
                    gathered(i + 1)
                    act.wait_ge(actT_ps, i + 1)
                    nc.scalar.activation(ACT_T, BM[:, :].rearrange("p (k s) -> p k s", k=4), ACT.Copy)\
                        .then_inc(actT_sb, 1)
                    act.wait_ge(y_ps, i + 1)
                    nc.scalar.activation(Y, BY[:, :], ACT.Copy).then_inc(y_sb, 1)
            act.wait_ge(resid_done, 2 * T)
            for t in range(T):
                square(ssq[:, t:t + 1], X[:, t, :], mem_q[:, 0:D_MODEL])
            roots_of(4, T)

        @block.tensor
        def _(pe):
            def claim(name):
                b, n = TILE[name]
                if n:
                    pe.wait_ge(psum_emptied[b], n)
                return bank[b]

            def arrived(name):
                pe.wait_ge(unit_loaded[UNIT[name][0]], UNIT[name][1])
                return ring[UNIT[name][0]]

            def transposes(name, sources):
                o = claim(name)
                for n, src in enumerate(sources):
                    last = nc.tensor.transpose(o[:, n * P:(n + 1) * P], src, ident)
                last.then_inc(full(name), 1)

            def product(o, lhs, rhs, kk):
                for k in range(kk):
                    last = nc.tensor.matmul(o, lhs(k), rhs(k), start=(k == 0), stop=(k == kk - 1))
                return last

            def chunk(unit, name, a, width=COLS):
                w = arrived(unit)[:, 0:KD * width].rearrange("p (k n) -> p k n", k=KD)
                for t in range(T):
                    o = claim(f"{name}{t}")
                    product(o[:, 0:width], lambda k: a[:, k, tok(t)], lambda k: w[:, k, :], KD)\
                        .then_inc(full(f"{name}{t}"), 1)

            def turned(name, a):
                for t in range(T):
                    for q in range(2):
                        transposes(f"{name}{t}{q}", [a[:, t, (4 * q + b) * P:(4 * q + b + 1) * P] for b in range(4)])
                for t in range(T):
                    for q in range(2):
                        wait_sb(pe, f"{name}{t}{q}")

            pe.wait_ge(const_in, 16)
            pe.wait_ge(h_ready, T)
            turned("hT", H)
            for c in range(2):
                chunk(f"lat{c}", f"lat{c}", HT, LATC)
            for c in range(2):
                chunk(f"idx{c}", f"idx{c}", HT, IDXC)
            pe.wait_ge(lat_ready, 2 * T)
            pe.wait_ge(kr_roped, T)
            for t in range(T):
                transposes(f"cqT{t}", [LAT[:, t, k * P:(k + 1) * P] for k in range(3)])
                transposes(f"ckvT{t}", [LAT[:, t, Q_LORA + k * P:Q_LORA + (k + 1) * P] for k in range(2)]
                           + [kr_pad3[:, t, MLA_ROPE:3 * MLA_ROPE], kr_pad3[:, t, 0:2 * MLA_ROPE]])
            for t in range(T):
                wait_sb(pe, f"cqT{t}")
                wait_sb(pe, f"ckvT{t}")
            w = arrived("uqn")[:, 0:3 * 1024].rearrange("p (k n) -> p k n", k=3)
            for g in range(4):
                o = claim(f"qn{g}")
                for h in range(2):
                    last = product(o[:, h * SEQ:(h + 1) * SEQ], lambda k: w[:, k, (2 * g + h) * HD:(2 * g + h + 1) * HD],
                                   lambda k: LT[:, k, :], 3)
                last.then_inc(full(f"qn{g}"), 1)
            wr = arrived("uqr")[:, 0:3 * 512].rearrange("p (k n) -> p k n", k=3)
            for t in range(T):
                o = claim(f"qr{t}")
                product(o[:, :], lambda k: LT[:, k, tok(t)], lambda k: wr[:, k, :], 3).then_inc(full(f"qr{t}"), 1)
            wkv = arrived("ukv")[:, :].rearrange("p (v k n) -> p v k n", v=2, k=2)
            for g in range(4):
                o = claim(f"kn{g}")
                for h in range(2):
                    last = product(o[:, h * SEQ:(h + 1) * SEQ],
                                   lambda k: wkv[:, 0, k, (2 * g + h) * HD:(2 * g + h + 1) * HD],
                                   lambda k: LT[:, 3 + k, :], 2)
                last.then_inc(full(f"kn{g}"), 1)
            for c in range(2):
                for t in range(T):
                    o = claim(f"vm{c}{t}")
                    product(o[:, :], lambda k: LT[:, 3 + k, tok(t)], lambda k: wkv[:, 1, k, c * COLS:(c + 1) * COLS], 2)\
                        .then_inc(full(f"vm{c}{t}"), 1)
            for t in range(T):
                pe.wait_ge(idx_roped, t + 1)
                transposes(f"qiT{t}", [roped[:, t * COLS + g * P:t * COLS + (g + 1) * P] for g in range(4)])
            transposes("kiT", [ki_pad3[:, t, a:a + P] for t in range(T) for a in (IDX_DIM, 0)])
            for t in range(T):
                pe.wait_ge(tok_roped, t + 1)
                transposes(f"qrT{t}", [q_rot[t][:, g * P:(g + 1) * P] for g in range(4)])
            wait_sb(pe, "kiT")
            for t in range(T):
                keys = P * (t + 1)
                for g in range(4):
                    o = claim(f"raw{t}{g}")
                    for e in range(2):
                        last = nc.tensor.matmul(o[:, e * keys:(e + 1) * keys], QI[:, g, tok(t)], KI[:, e, 0:keys],
                                                start=True, stop=True)
                    last.then_inc(full(f"raw{t}{g}"), 1)
            for n in range(len(QK) + 1):
                if n < len(QK):
                    c, t = QK[n]
                    w = arrived(f"qkv{c}")[:, :].rearrange("p (k n) -> p k n", k=KD)
                    o = claim(f"qk{c}{t}")
                    product(o[:, :], lambda k: HT[:, k, tok(t)], lambda k: w[:, k, :], KD).then_inc(full(f"qk{c}{t}"), 1)
                if n:
                    pe.wait_ge(tok_roped, T + n)
                    a = COLS * ((n + 1) % 3)
                    transposes("qkT%d%d" % QK[n - 1], [roped[:, a + g * P:a + (g + 1) * P] for g in range(4)])
            for c in range(2):
                chunk(f"qkv{4 + c}", f"v{c}", HT)
            wait_sb(pe, f"v1{T - 1}")

            for s in range(NH + 3):
                if s < NH:
                    h = s % HEADS
                    o = claim(f"s{s}")
                    for t in range(T):
                        w = P * (t + 1)
                        ot = o[:, t * P:t * P + w]
                        if s < HEADS:
                            nc.tensor.matmul(ot, QN[:, h, tok(t)], KN[:, h, 0:w], start=True, stop=False)
                            last = nc.tensor.matmul(ot, QR[:, h // 2, tok(t)], KR[:, h % 2, 0:w], start=False, stop=True)
                        else:
                            last = nc.tensor.matmul(ot, QT[:, h, tok(t)], KT[:, h, 0:w], start=True, stop=True)
                    last.then_inc(full(f"s{s}"), 1)
                if 2 <= s < NH + 2:
                    pe.wait_ge(normed, s - 1)
                    transposes(f"pT{s - 2}", [PR[(s - 2) % 3][:, a * P:(a + 1) * P] for a in range(3)])
                if s >= 3:
                    h = (s - 3) % HEADS
                    v = (VM if s - 3 < HEADS else VD)
                    pt = PT[(s - 3) % 2]
                    o = claim(f"o{s - 3}")
                    wait_sb(pe, f"pT{s - 3}")
                    nc.tensor.matmul(o[:, 0:SEQ], v[:, 0, h * HD:(h + 1) * HD], pt[:, 0:SEQ], start=True, stop=False)
                    nc.tensor.matmul(o[:, P:SEQ], v[:, 1, h * HD:(h + 1) * HD], pt[:, SEQ:3 * P],
                                     start=False, stop=True).then_inc(full(f"o{s - 3}"), 1)
            for c in range(4):
                chunk(f"gate{c}", f"gate{c}", HT)
            for h in range(HEADS):
                wait_sb(pe, f"o{h}")
            for c in range(2):
                chunk(f"oa{c}", f"ya{c}", QN)
            for h in range(HEADS, NH):
                wait_sb(pe, f"o{h}")
            for c in range(2):
                chunk(f"ob{c}", f"yb{c}", QT)
            pe.wait_ge(merged, 2 * T)
            turned("mT", MG)
            for c in range(2):
                chunk(f"wo{c}", f"xo{c}", HT)
            pe.wait_ge(hn_ready, T)
            turned("nT", HN)
            pe.wait_ge(router_in, 32)
            o = claim("logits")
            for t in range(T):
                last = product(o[:, t * N_EXPERTS:(t + 1) * N_EXPERTS], lambda k: HT[:, k, tok(t)],
                               lambda k: w_rt[:, k, :], KD)
            last.then_inc(full("logits"), 1)
            for b in range(4):
                pe.wait_ge(psum_emptied[b], USES[b])
                nc.tensor.matmul(bank[b][:, :], const("zero"), cst[:, 0:COLS], start=True, stop=False)
            pe.wait_ge(chosen, 1)
            o = claim("rank")
            for t in range(T):
                ot = o[:, t * N_EXPERTS:(t + 1) * N_EXPERTS]
                for b in range(t + 1):
                    last = nc.tensor.matmul(ot, const("ones") if b < t else const("before"), CH3[:, b, :],
                                            start=(b == 0), stop=(b == t))
            last.then_inc(full("rank"), 1)
            o = claim("count")
            product(o[:, 0:N_EXPERTS], lambda b: const("ones"), lambda b: CH3[:, b, :], T).then_inc(full("count"), 1)
            pe.wait_ge(gates_in, 1)

            def gates_turned(o):
                for h in range(2):
                    for t in range(T):
                        a = SLOTS * (1 - h)
                        last = nc.tensor.transpose(o[:, (T * h + t) * P:(T * h + t + 1) * P], PG[:, t, a:a + P], ident)
                return last

            gates_turned(claim("gT")).then_inc(full("gT"), 1)

            def gather(item):
                pe.wait_ge(p_ready, item + 1)
                for t in range(T):
                    for h in range(2):
                        last = nc.tensor.matmul(BM[SLOTS * h:SLOTS * (h + 1), :], GP[:, t, :],
                                                HN[:, t, h * COLS:(h + 1) * COLS], start=(t == 0), stop=(t == T - 1))
                last.then_inc(xg_ps, 1)
                pe.wait_ge(xg_sb, item + 1)
                pe.wait_ge(pgT_sb, item + 1)
                rows = XG.rearrange("p (c k) -> p k c", k=4)
                for k in range(4):
                    last = nc.tensor.transpose(BY[:, k * P:(k + 1) * P], rows[:, k, :], ident)
                last.then_inc(xgT_ps, 1)

            def scatter(stop):
                for h in range(2):
                    for t in range(T):
                        last = nc.tensor.matmul(bank[2 * t + h][:, :], PGT[:, h, tok(t)], Y, start=False, stop=stop)
                return last

            for b in range(4, NBANK):
                pe.wait_ge(psum_emptied[b], USES[b])
            gather(0)
            n_items = pe.value_load(table_i[0:1, ITEM_COLS:ITEM_COLS + 1], min_val=N_EXPERTS, max_val=MAX_ITEMS)
            with pe.Fori(0, MAX_ITEMS) as i:
                with pe.If(i < n_items):
                    pe.wait_ge(bias_in, 16 * i + 16)
                    for n in range(4):
                        last = nc.tensor.matmul((BG, BL)[n // 2][SLOTS * (n % 2):SLOTS * (n % 2 + 1), :],
                                                const("first_row"), BIAS[:, n * COLS:(n + 1) * COLS],
                                                start=True, stop=False)
                    last.then_inc(bias_used, 1)
                    pe.wait_ge(xgT_sb, i + 1)
                    for j in range(GU_UNITS):
                        pe.wait_ge(unit_loaded[ITEM_SLOT[j]], LOADED0[j] + 16 + 16 * i)
                        w = ring[ITEM_SLOT[j]][:, :].rearrange("p (k n) -> p k n", k=2)
                        for k in range(2):
                            lhs = XGT[:, 2 * (j % 2) + k, SLOTS * (j // 2):SLOTS * (j // 2 + 1)]
                            for n in range(4):
                                last = nc.tensor.matmul((BG, BL)[n // 2][SLOTS * (n % 2):SLOTS * (n % 2 + 1), :], lhs,
                                                        w[:, k, n * COLS:(n + 1) * COLS], start=False,
                                                        stop=(j == GU_UNITS - 1 and k == 1))
                        last.then_inc(unit_used[j] if j < GU_UNITS - 1 else h_done, 1)
                    pe.wait_ge(y_sb, i + 1)
                    pe.wait_ge(pgT_sb, i + 1)
                    scatter(False)
                    pe.wait_ge(pg_ready, i + 1)
                    gates_turned(BY).then_inc(pgT_ps, 1)
                    gather(i + 1)
                    pe.wait_ge(act_ready, i + 1)
                    rows = AC.rearrange("p (c k) -> p k c", k=4)
                    for k in range(4):
                        last = nc.tensor.transpose(BM[:, k * P:(k + 1) * P], rows[:, k, :], ident)
                    last.then_inc(actT_ps, 1)
                    pe.wait_ge(actT_sb, i + 1)
                    pe.wait_ge(xgT_sb, i + 2)
                    for h in range(2):
                        j = GU_UNITS + h
                        pe.wait_ge(unit_loaded[ITEM_SLOT[j]], LOADED0[j] + 16 + 16 * i)
                        w = ring[ITEM_SLOT[j]][:, :].rearrange("p (k n) -> p k n", k=4)
                        for k in range(4):
                            for n in range(2):
                                last = nc.tensor.matmul(BY[SLOTS * n:SLOTS * (n + 1), :],
                                                        ACT_T[:, k, SLOTS * h:SLOTS * (h + 1)],
                                                        w[:, k, n * COLS:(n + 1) * COLS],
                                                        start=(h == 0 and k == 0), stop=(h == 1 and k == 3))
                        last.then_inc(unit_used[j] if h == 0 else y_ps, 1)
            pe.wait_ge(y_sb, n_items + 1)
            pe.wait_ge(pgT_sb, n_items + 1)
            scatter(True).then_inc(acc_done, 1)

        @block.vector
        def _(dve):
            steps = [0]

            def step(ins):
                steps[0] += 1
                ins.then_inc(dve_step, 1)
                dve.wait_ge(dve_step, steps[0])

            def norm_scale(n, n_squares, parts):
                dve.wait_ge(squares, n_squares)
                for a, b, width in parts:
                    last = nc.vector.tensor_scalar(msq[:, a:b], ssq[:, a:b], 1.0 / width, NORM_EPS, ALU.mult, ALU.add)
                last.then_inc(means, 1)
                dve.wait_ge(roots, n)
                step(nc.vector.reciprocal(rstd[:, 0:parts[-1][1]], root[:, 0:parts[-1][1]]))

            def rotate(dst, src, cos, sin, groups, half, freed=None, done=None):
                w = 2 * half
                a = rot_a[:, 0:groups * w].rearrange("p (g d) -> p g d", g=groups)
                b = rot_b[:, 0:groups * w].rearrange("p (g d) -> p g d", g=groups)
                c = cos.unsqueeze(1).to_broadcast([P, groups, w])
                s = sin.unsqueeze(1).to_broadcast([P, groups, w])
                nc.vector.tensor_tensor(a, src, c, ALU.mult)
                nc.vector.tensor_tensor(b[:, :, 0:half], src[:, :, half:w], s[:, :, 0:half], ALU.mult)
                ins = nc.vector.tensor_tensor(b[:, :, half:w], src[:, :, 0:half], s[:, :, half:w], ALU.mult)
                if freed:
                    ins.then_inc(freed[0], 1)
                    dve.wait_ge(*freed)
                else:
                    step(ins)
                ins = nc.vector.tensor_tensor(dst, a, b, ALU.add)
                if done:
                    ins.then_inc(done[0], 1)
                    dve.wait_ge(*done)
                else:
                    step(ins)

            def freed_at(name):
                return (emptied(name), TILE[name][1] + 1)

            norm_scale(1, T, [(0, T, D_MODEL)])
            dve.wait_ge(gain_in, 16)
            for t in range(T):
                nc.vector.scalar_tensor_tensor(H[:, t, :], X[:, t, :], rstd[:, t:t + 1], gain_attn, ALU.mult, ALU.mult)\
                    .then_inc(h_ready, 1)
            norm_scale(2, 3 * T, [(0, T, Q_LORA), (T, 2 * T, KV_LORA)])
            dve.wait_ge(lora_in, 32)
            for t in range(T):
                for a, w, col in ((0, Q_LORA, t), (Q_LORA, KV_LORA, T + t)):
                    nc.vector.scalar_tensor_tensor(LAT[:, t, a:a + w], LAT[:, t, a:a + w], rstd[:, col:col + 1],
                                                   lora_gain[:, a:a + w], ALU.mult, ALU.mult).then_inc(lat_ready, 1)
            dve.wait_ge(pads_zero, 1)
            dve.wait_ge(const_in, 16)
            for t in range(T):
                rotate(kr_pad3[:, t, MLA_ROPE:2 * MLA_ROPE].unsqueeze(1), LAT[:, t, W_LAT - MLA_ROPE:W_LAT].unsqueeze(1),
                       const("cos_m", t), const("sin_m", t), 1, MLA_ROPE // 2, done=(kr_roped, t + 1))
            dve.wait_ge(pads_zero, 2)
            for c in range(2):
                for t in range(T):
                    wait_sb(dve, f"idx{c}{t}")
            for t in range(T):
                kq = ki_pad3[:, t, IDX_DIM:2 * IDX_DIM].unsqueeze(1)
                ki = IDX[:, t, IDX_HEADS * IDX_DIM:(IDX_HEADS + 1) * IDX_DIM].unsqueeze(1)
                rotate(kq[:, :, 0:IDX_ROPE], ki[:, :, 0:IDX_ROPE], const("cos_i", t), const("sin_i", t), 1, IDX_ROPE // 2)
                nc.vector.tensor_copy(kq[:, :, IDX_ROPE:IDX_DIM], ki[:, :, IDX_ROPE:IDX_DIM])
                qd = roped[:, t * COLS:(t + 1) * COLS].rearrange("p (h d) -> p h d", d=IDX_DIM)
                qi = IDX[:, t, 0:IDX_HEADS * IDX_DIM].rearrange("p (h d) -> p h d", d=IDX_DIM)
                nc.vector.tensor_copy(qd[:, :, IDX_ROPE:IDX_DIM], qi[:, :, IDX_ROPE:IDX_DIM])
                nc.vector.tensor_scalar(wi[:, t * IDX_HEADS:(t + 1) * IDX_HEADS], IDX[:, t, (IDX_HEADS + 1) * IDX_DIM:W_IDX],
                                        IDX_HEADS ** -0.5, None, ALU.mult)
                rotate(qd[:, :, 0:IDX_ROPE], qi[:, :, 0:IDX_ROPE], const("cos_i", t), const("sin_i", t), IDX_HEADS,
                       IDX_ROPE // 2, done=(idx_roped, t + 1))
            for t in range(T):
                n = f"qr{t}"
                wait_full(dve, n)
                rotate(q_rot[t].rearrange("p (h d) -> p h d", d=MLA_ROPE),
                       ps(n)[:, :].rearrange("p (h d) -> p h d", d=MLA_ROPE), const("cos_m", t), const("sin_m", t),
                       HEADS, MLA_ROPE // 2, freed_at(n), (tok_roped, t + 1))
            for t in range(T):
                keys = P * (t + 1)
                sc = score[:, t * P:t * P + keys]
                for g in range(4):
                    u = 4 * t + g
                    wait_sb(dve, f"raw{t}{g}")
                    for e in range(2):
                        r = RELU[u % 2][:, e * keys:(e + 1) * keys]
                        w = wi[:, t * IDX_HEADS + 2 * g + e:t * IDX_HEADS + 2 * g + e + 1]
                        if g == 0 and e == 0:
                            ins = nc.vector.tensor_scalar(sc, r, w, None, ALU.mult)
                        else:
                            ins = nc.vector.scalar_tensor_tensor(sc, r, w, sc, ALU.mult, ALU.add)
                        if e == 0:
                            step(ins)
                        else:
                            ins.then_inc(relu_used, 1)
                            dve.wait_ge(relu_used, u + 1)
            step(nc.vector.tensor_tensor(score[:, :], score[:, :], const("chunk_mask"), ALU.add))

            def select(t):
                sc = score[:, t * P:t * P + P * (t + 1)]
                for _ in range(TOP_K // 8):
                    step(nc.vector.max(top8[:, :], sc))
                    step(nc.vector.match_replace(sc, top8[:, :], sc, TAKEN))
                step(nc.vector.tensor_scalar(sel_mask[:, t * P:t * P + P * (t + 1)], sc, TAKEN, MASKED,
                                             ALU.not_equal, ALU.mult))

            for n, (c, t) in enumerate(QK):
                name = f"qk{c}{t}"
                if n:
                    wait_full(dve, "qkT%d%d" % QK[n - 3] if n >= 3 else f"qiT{n - 1}")
                wait_full(dve, name)
                a = COLS * ((n + 2) % 3)
                rotate(roped[:, a:a + COLS].rearrange("p (h d) -> p h d", d=HD),
                       ps(name)[:, :].rearrange("p (h d) -> p h d", d=HD), const("cos_d", t), const("sin_d", t),
                       COLS // HD, HD // 2, freed_at(name), (tok_roped, T + n + 1))
                if n < T:
                    select(n)
            for s in range(NH + 3):
                if s < NH:
                    n = f"s{s}"
                    wait_full(dve, n)
                    nc.vector.scalar_tensor_tensor(S[s % 2], ps(n)[:, 0:3 * P],
                                                   (MLA_QK if s < HEADS else HD) ** -0.5,
                                                   const("chunk_mask") if s < HEADS else sel_mask[:, :],
                                                   ALU.mult, ALU.add).then_inc(emptied(n), 1)
                    dve.wait_ge(*freed_at(n))
                    for t in range(T):
                        ins = nc.vector.tensor_reduce(negmax[:, s * T + t:s * T + t + 1],
                                                      S[s % 2][:, t * P:t * P + P * (t + 1)], AX, ALU.max, negate=True)
                    ins.then_inc(masked, 1)
                if 1 <= s <= NH:
                    h = s - 1
                    dve.wait_ge(exped, T * s)
                    step(nc.vector.reciprocal(rsum[:, h * T:(h + 1) * T], psums[:, h * T:(h + 1) * T]))
                    for t in range(T):
                        p = PR[h % 3][:, t * P:t * P + P * (t + 1)]
                        ins = nc.vector.tensor_scalar(p, p, rsum[:, h * T + t:h * T + t + 1], None, ALU.mult)
                    ins.then_inc(normed, 1)
                if s >= 3:
                    n = f"o{s - 3}"
                    wait_full(dve, n)
                    nc.vector.tensor_copy((QN if s - 3 < HEADS else QT)[:, (s - 3) % HEADS, :], ps(n)[:, 0:SEQ])\
                        .then_inc(emptied(n), 1)
            dve.wait_ge(gate_bias_in, 64)
            for c in range(4):
                for t in range(T):
                    n = f"gate{c}{t}"
                    wait_full(dve, n)
                    nc.vector.tensor_tensor(G[:, t, c * COLS:(c + 1) * COLS], ps(n)[:, :], gate_bias[c], ALU.add)\
                        .then_inc(emptied(n), 1)
            for c in range(2):
                for t in range(T):
                    n = f"ya{c}{t}"
                    wait_full(dve, n)
                    dve.wait_ge(gate_sig, T * c + t + 1)
                    nc.vector.tensor_tensor(MG[:, t, c * COLS:(c + 1) * COLS], ps(n)[:, :],
                                            G[:, t, c * COLS:(c + 1) * COLS], ALU.mult).then_inc(emptied(n), 1)
            for c in range(2):
                for t in range(T):
                    n = f"yb{c}{t}"
                    m = MG[:, t, c * COLS:(c + 1) * COLS]
                    wait_full(dve, n)
                    dve.wait_ge(gate_sig, T * (c + 2) + t + 1)
                    nc.vector.tensor_tensor(rot_a[:, :], ps(n)[:, :], G[:, t, D_MODEL + c * COLS:D_MODEL + (c + 1) * COLS],
                                            ALU.mult).then_inc(emptied(n), 1)
                    dve.wait_ge(*freed_at(n))
                    dve.wait_ge(*freed_at(f"ya{c}{t}"))
                    nc.vector.tensor_tensor(m, m, rot_a[:, :], ALU.add).then_inc(merged, 1)
                    dve.wait_ge(merged, T * c + t + 1)
            for c in range(2):
                for t in range(T):
                    n = f"xo{c}{t}"
                    r = X[:, t, c * COLS:(c + 1) * COLS]
                    wait_full(dve, n)
                    nc.vector.tensor_tensor(r, ps(n)[:, :], r, ALU.add).then_inc(emptied(n), 1)
            norm_scale(3, 4 * T, [(0, T, D_MODEL)])
            dve.wait_ge(gain_in, 32)
            for t in range(T):
                nc.vector.scalar_tensor_tensor(HN[:, t, :], X[:, t, :], rstd[:, t:t + 1], gain_ffn, ALU.mult, ALU.mult)\
                    .then_inc(hn_ready, 1)

            dve.wait_ge(router_in, 32)
            nc.vector.memset(LPAD3[:, :, N_EXPERTS:], TAKEN)
            wait_full(dve, "logits")
            nc.vector.tensor_tensor(LG3, ps("logits")[:, 0:TE].rearrange("p (t e) -> p t e", t=T),
                                    b_rt.unsqueeze(1).to_broadcast([P, T, N_EXPERTS]), ALU.add)\
                .then_inc(emptied("logits"), 1)
            dve.wait_ge(*freed_at("logits"))
            nc.vector.tensor_reduce(nmx, LG3, AX, ALU.max, negate=True).then_inc(logits_in, 1)
            nc.vector.tensor_copy(LPAD3[:, :, 0:N_EXPERTS], LG3)
            for t in range(T):
                ins = nc.vector.max(REP3[:, t, :], LG3[:, t, :])
            step(ins)
            step(nc.vector.memset(REP3[:, :, MOE_TOP_K:8], TAKEN))
            for t in range(T):
                step(nc.vector.match_replace(LPAD3[:, t, :], REP3[:, t, :], LPAD3[:, t, :], MASKED))
            nc.vector.tensor_tensor(CH3, LPAD3[:, :, 0:N_EXPERTS], LG3, ALU.not_equal).then_inc(chosen, 1)
            dve.wait_ge(chosen, 1)
            dve.wait_ge(router_exp, T)
            step(nc.vector.tensor_tensor(GT3, LGE3, CH3, ALU.mult))
            step(nc.vector.tensor_reduce(gs, GT3, AX, ALU.add))
            step(nc.vector.reciprocal(grs, gs))
            for t in range(T):
                ins = nc.vector.tensor_scalar(GT3[:, t, :], GT3[:, t, :], grs[:, t:t + 1], None, ALU.mult)
            step(ins)
            dve.wait_ge(zeroed, 2)
            nc.vector.tensor_copy(PG[:, :, SLOTS:SLOTS + N_EXPERTS], GT3).then_inc(gates_in, 1)
            wait_full(dve, "count")
            cnt = ps("count")[:, 0:N_EXPERTS]
            step(nc.vector.tensor_scalar(NB, cnt, SLOTS + 0.5, 1.0, ALU.is_gt, ALU.add))
            step(nc.vector.scalar_tensor_tensor(NB, cnt, 2 * SLOTS + 0.5, NB, ALU.is_gt, ALU.add))
            nc.vector.scalar_tensor_tensor(NB, cnt, 3 * SLOTS + 0.5, NB, ALU.is_gt, ALU.add).then_inc(emptied("count"), 1)
            dve.wait_ge(*freed_at("count"))
            step(nc.vector.tensor_tensor_scan(ITEM_END, const("ones")[:, 0:N_EXPERTS], NB, 0.0, ALU.mult, ALU.add))
            ends = ITEM_END[0:1, :].unsqueeze(1).to_broadcast([1, ITEM_COLS, N_EXPERTS])
            items = const("item_no")[0:1, :].unsqueeze(2).to_broadcast([1, ITEM_COLS, N_EXPERTS])
            cmp = ET[0:1, :].rearrange("p (i e) -> p i e", e=N_EXPERTS)
            step(nc.vector.tensor_tensor(cmp, ends, items, ALU.is_le))
            nc.vector.tensor_copy(ER[0:1, ITEM_COLS:ITEM_COLS + 1], ITEM_END[0:1, N_EXPERTS - 1:N_EXPERTS])
            step(nc.vector.tensor_reduce(ER[0:1, 0:ITEM_COLS], cmp, AX, ALU.add))
            step(nc.vector.tensor_scalar(ER[0:1, 0:ITEM_COLS], ER[0:1, 0:ITEM_COLS], float(N_EXPERTS - 1), None, ALU.min))
            nc.vector.tensor_copy(table_i[0:1, 0:ITEM_COLS + 1], ER[0:1, 0:ITEM_COLS + 1]).then_inc(table, 1)
            step(nc.vector.tensor_tensor(ITEM_AT, ITEM_END, NB, ALU.subtract))
            step(nc.vector.tensor_scalar(ITEM_AT, ITEM_AT, float(SLOTS), 1.0, ALU.mult, ALU.add))
            wait_full(dve, "rank")
            nc.vector.tensor_tensor(D23, ps("rank")[:, 0:TE].rearrange("p (t e) -> p t e", t=T),
                                    ITEM_AT.unsqueeze(1).to_broadcast([P, T, N_EXPERTS]), ALU.add)\
                .then_inc(emptied("rank"), 1)
            dve.wait_ge(*freed_at("rank"))
            step(nc.vector.tensor_tensor(D23, D23, CH3, ALU.mult))

            def route(first_col, do, gathered=None):
                do(nc.vector.tensor_scalar(ITV, D2, first_col, None, ALU.subtract))
                do(nc.vector.scalar_tensor_tensor(U2, ITV, SLOTS + 0.5, ITV, ALU.is_lt, ALU.mult))
                nc.vector.tensor_reduce(W1, by_te(U2), AX, ALU.max)
                do(nc.vector.scalar_tensor_tensor(VG, U2, 0.5, GT_, ALU.is_gt, ALU.mult))
                do(nc.vector.tensor_reduce(GW, by_te(VG), AX, ALU.add))
                if gathered is not None:
                    dve.wait_ge(xg_ps, gathered)
                for t in range(T):
                    ins = nc.vector.tensor_scalar(GP[:, t, :], const("slot_no"), W1[:, t:t + 1], None, ALU.is_equal)
                ins.then_inc(p_ready, 1)

            def slot_gates():
                for t in range(T):
                    ins = nc.vector.tensor_scalar(PG[:, t, SLOTS:2 * SLOTS], const("slot_no"), W1[:, t:t + 1],
                                                  GW[:, t:t + 1], ALU.is_equal, ALU.mult)
                ins.then_inc(pg_ready, 1)

            base = CONST["item_base"][0]
            route(cst[:, base:base + 1], step)
            wait_full(dve, "gT")
            nc.vector.tensor_copy(PGT, ps("gT")[:, :].rearrange("p (h n) -> p h n", h=2)).then_inc(pgT_sb, 1)
            dve.wait_ge(pgT_sb, 1)
            nc.vector.tensor_copy(table_i[0:1, ITEM_COLS + 1:ITEM_COLS + 2], ER[0:1, 0:1]).then_inc(emptied("gT"), 1)
            slot_gates()
            n_items = dve.value_load(table_i[0:1, ITEM_COLS:ITEM_COLS + 1], min_val=N_EXPERTS, max_val=MAX_ITEMS)
            STEPS = 5
            with dve.Fori(0, MAX_ITEMS) as i:
                with dve.If(i < n_items):
                    at = [0]

                    def do(ins):
                        at[0] += 1
                        ins.then_inc(moe_step, 1)
                        dve.wait_ge(moe_step, i * STEPS + at[0])

                    route(cst[:, bass.ds(base + 1 + i, 1)], do, i + 1)
                    dve.wait_ge(h_done, i + 1)
                    nc.vector.tensor_scalar(GC, BG[:, :], SWIGLU_LIMIT, None, ALU.min).then_inc(clipped, 1)
                    nc.vector.tensor_scalar(LN, BL[:, :], SWIGLU_LIMIT, -SWIGLU_LIMIT, ALU.min, ALU.max)
                    dve.wait_ge(sig, i + 1)
                    do(nc.vector.tensor_tensor(GLU, GC, SG, ALU.mult))
                    nc.vector.scalar_tensor_tensor(AC, LN, 1.0, GLU, ALU.add, ALU.mult).then_inc(act_ready, 1)
                    dve.wait_ge(pgT_ps, i + 1)
                    nc.vector.tensor_copy(PGT, BY[:, :].rearrange("p (h n) -> p h n", h=2)).then_inc(pgT_sb, 1)
                    slot_gates()
                    assert at[0] == STEPS, at
            dve.wait_ge(acc_done, 1)
            for t in range(T):
                for h in range(2):
                    r = X[:, t, h * COLS:(h + 1) * COLS]
                    nc.vector.tensor_tensor(r, bank[2 * t + h][:, :], r, ALU.add).then_inc(resid_done, 1)
            norm_scale(4, 5 * T, [(0, T, D_MODEL)])
            dve.wait_ge(out_gain_in, 16)
            for t in range(T):
                nc.vector.scalar_tensor_tensor(X[:, t, :], X[:, t, :], rstd[:, t:t + 1], gain_out, ALU.mult, ALU.mult)\
                    .then_inc(out_ready, 1)


def constants(np):
    c = {"ident": np.eye(P), "ones": np.ones((P, P)), "zero": np.zeros((P, P))}
    pos = np.arange(SEQ, dtype=np.float32).reshape(T, P, 1)

    def tables(rot, key):
        half = rot // 2
        freq = np.float32(ROPE_THETA) ** (-np.arange(half, dtype=np.float32) / np.float32(half))
        ang = (pos * freq.astype(np.float32)).astype(np.float32)
        cos, sin = np.cos(ang), np.sin(ang)
        c["cos_" + key] = np.concatenate([cos, cos], -1).transpose(1, 0, 2).reshape(P, -1)
        c["sin_" + key] = np.concatenate([-sin, sin], -1).transpose(1, 0, 2).reshape(P, -1)

    tables(HD, "d")
    tables(MLA_ROPE, "m")
    tables(IDX_ROPE, "i")
    q = np.arange(P)[:, None]
    parts = [np.where((np.arange(P * (t + 1))[None] // CHUNK) <= (t * P + q) // CHUNK, 0.0, MASKED) for t in range(T)]
    c["chunk_mask"] = np.concatenate(parts, 1)
    c["before"] = (q < np.arange(P)[None]) * 1.0
    c["slot_no"] = np.tile(np.arange(1, SLOTS + 1), (P, 1))
    c["item_base"] = np.tile(np.arange(ITEM_COLS) * SLOTS, (P, 1))
    c["item_no"] = np.tile(np.arange(ITEM_COLS), (P, 1))
    c["first_row"] = (q == 0) * np.ones((1, SLOTS))
    return np.ascontiguousarray(np.concatenate([c[n] for n in CONST], 1).astype(np.float32))


_INS = ['x', 'norm_attn_g', 'w_in', 'q_lora_g', 'kv_lora_g', 'w_uq', 'w_uk', 'w_uv', 'w_o_mla', 'w_o_dsa',
        'b_gate', 'w_out', 'norm_ffn_g', 'w_router', 'b_router', 'w_gate_up', 'b_gate_up', 'w_down',
        'b_down', 'norm_final_g']


def kernel(**inputs):
    import numpy as _np
    import concourse.bacc as _bacc
    from concourse import mybir as _mybir
    from concourse.bass_utils import run_bass_kernel_spmd as _run

    nc = _bacc.Bacc("TRN2", target_bir_lowering=False, num_devices=1)
    arrays, args = {}, []
    for name in _INS:
        a = _np.ascontiguousarray(inputs[name])
        arrays[f"in_{name}"] = a
        args.append(nc.dram_tensor(f"in_{name}", a.shape, _mybir.dt.from_np(a.dtype), kind="ExternalInput").ap())
    a = constants(_np)
    arrays["in_consts"] = a
    args.append(nc.dram_tensor("in_consts", a.shape, _mybir.dt.from_np(a.dtype), kind="ExternalInput").ap())
    o = nc.dram_tensor("out_0", (1, SEQ, D_MODEL), _mybir.dt.float32, kind="ExternalOutput").ap()
    hybrid_block_kernel(nc, *args, o)
    return _run(nc, [arrays], core_ids=[0]).results[0]["out_0"]
```

```python
import concourse.bass as bass
from concourse import mybir
from contextlib import ExitStack

D_MODEL = 1024
SEQ = 256
CHUNK = 64
NORM_EPS = 1e-6
ROPE_THETA = 10000.0
HEADS = 8
HD = 128
Q_LORA = 384
KV_LORA = 256
MLA_ROPE = 64
MLA_QK = HD + MLA_ROPE
IDX_HEADS = 8
IDX_DIM = 64
IDX_ROPE = 32
TOP_K = SEQ // 4
N_EXPERTS = 32
MOE_TOP_K = 4
D_EXPERT = 1024
SWIGLU_LIMIT = 7.0
SWIGLU_ALPHA = 1.702

P = 128
T = SEQ // P
KD = D_MODEL // P
COLS = 512
W_LAT = Q_LORA + KV_LORA + MLA_ROPE
W_IDX = IDX_HEADS * IDX_DIM + IDX_DIM + IDX_HEADS
C_QKV = W_LAT
C_IDX = C_QKV + 3 * HEADS * HD
C_GATE = C_IDX + W_IDX
D_IN = C_GATE + 2 * D_MODEL
LATC = W_LAT // 2
IDXC = W_IDX // 2

SLOTS = 64
ASSIGNED = SEQ * MOE_TOP_K
MAX_EXTRA = (ASSIGNED - 1) // SLOTS
EXTRA_COLS = 16
assert MAX_EXTRA < EXTRA_COLS

MASKED = -(2.0 ** 100)
TAKEN = -(2.0 ** 127)

RING = 6
RINGW = 4096

CONST = {}
_at = 0
for _name, _w in (("ident", P), ("cos_d", T * HD), ("sin_d", T * HD), ("cos_m", T * MLA_ROPE),
                  ("sin_m", T * MLA_ROPE), ("cos_i", T * IDX_ROPE), ("sin_i", T * IDX_ROPE),
                  ("chunk_mask", 3 * P), ("before", P), ("ones", P), ("slot_no", SLOTS),
                  ("extra_base", EXTRA_COLS), ("extra_no", EXTRA_COLS), ("row_of", 4 * SLOTS), ("zero", P)):
    CONST[_name] = (_at, _w)
    _at += _w
CONST_W = _at


def hybrid_block_kernel(nc, x, norm_attn_g, w_in, q_lora_g, kv_lora_g, w_uq, w_uk, w_uv, w_o_mla, w_o_dsa,
                        b_gate, w_out, norm_ffn_g, w_router, b_router, w_gate_up, b_gate_up, w_down,
                        b_down, norm_final_g, consts, out):
    fp32 = mybir.dt.float32
    i32 = mybir.dt.int32
    ALU = mybir.AluOpType
    ACT = mybir.ActivationFunctionType
    AX = mybir.AxisListType.X

    x_v = x.rearrange("b (t p) d -> p (b t) d", p=P)
    out_v = out.rearrange("b (t p) d -> p (b t) d", p=P)
    w_in_v = w_in.rearrange("a (k p) n -> p (a k) n", p=P)
    uq_v = w_uq.rearrange("a (k p) (h c) -> p (a k) h c", p=P, c=MLA_QK)
    uk_v = w_uk.rearrange("a (k p) n -> p (a k) n", p=P)
    uv_v = w_uv.rearrange("a (k p) n -> p (a k) n", p=P)
    oa_v = w_o_mla.rearrange("a (k p) n -> p (a k) n", p=P)
    ob_v = w_o_dsa.rearrange("a (k p) n -> p (a k) n", p=P)
    wo_v = w_out.rearrange("a (k p) n -> p (a k) n", p=P)
    wr_v = w_router.rearrange("a (k p) n -> p (a k) n", p=P)
    gu_v = w_gate_up.rearrange("a e (h p k) n -> (a e) h p k n", h=2, k=4)
    dn_v = w_down.rearrange("a e (h p k) n -> (a e) h p k n", h=2, k=4)
    bgu_v = b_gate_up.rearrange("a e (n c) -> (a e) n c", c=COLS)
    bdn_v = b_down.rearrange("a e n -> (a e) n")

    READER = {"lat0": "lat01", "lat1": "lat11", "idx0": "idx01", "idx1": "idx11", "uqn": "qn3", "uqr": "qr1",
              "ukv": "vm11"}
    READER.update({f"qkv{c}": (f"qk{c}1" if c < 4 else f"v{c - 4}1") for c in range(6)})
    READER.update({f"gate{c}": f"gate{c}1" for c in range(4)})
    READER.update({f"{u}{c}": f"{n}{c}1" for u, n in (("oa", "ya"), ("ob", "yb"), ("wo", "xo")) for c in range(2)})
    UNITS = list(READER)
    DMAS = {"uqn": 3, "uqr": 3, "ukv": 2}
    NU = len(UNITS)
    loaded = [0] * RING
    UNIT = {}
    for n, name in enumerate(UNITS):
        s = n % RING
        loaded[s] += 16 * DMAS.get(name, 1)
        UNIT[name] = (s, loaded[s], UNITS[n - RING] if n >= RING else None)
    ITEM_SLOT = [(NU + j) % RING for j in range(RING)]
    LOADED0 = [loaded[s] for s in ITEM_SLOT]
    LAST_FRONT = [READER[UNITS[NU - RING + j]] for j in range(RING)]
    GU_UNITS = 4
    SPARE = 3
    ITEM_AT = [LOADED0[j] + (16 if j >= SPARE else 0) for j in range(RING)]

    tiles = [f"hT{t}{q}" for t in range(T) for q in range(2)]
    tiles += [f"lat{c}{t}" for c in range(2) for t in range(T)]
    tiles += [f"idx{c}{t}" for c in range(2) for t in range(T)]
    tiles += [f"{n}{t}" for t in range(T) for n in ("cqT", "ckvT")]
    tiles += [f"qn{g}" for g in range(4)] + [f"qr{t}" for t in range(T)] + [f"kn{g}" for g in range(4)]
    tiles += [f"vm{c}{t}" for c in range(2) for t in range(T)]
    tiles += [f"qiT{t}" for t in range(T)] + ["kiT"] + [f"qrT{t}" for t in range(T)]
    tiles += [f"raw{t}{g}" for t in range(T) for g in range(4)]
    QK = [(c, t) for c in range(4) for t in range(T)]
    for n in range(len(QK) + 1):
        if n < len(QK):
            tiles.append("qk%d%d" % QK[n])
        if n:
            tiles.append("qkT%d%d" % QK[n - 1])
    NH = 2 * HEADS
    BETWEEN = {1 + 2 * n: ("v", n // T, n % T) for n in range(2 * T)}
    BETWEEN.update({HEADS + 3 + n: ("gate", n // T, n % T) for n in range(4 * T)})
    for s in range(NH + 3):
        tiles += [f"s{s}"] * (s < NH) + [f"pT{s - 2}"] * (2 <= s < NH + 2) + [f"o{s - 3}"] * (s >= 3)
        if s in BETWEEN:
            tiles.append("%s%d%d" % BETWEEN[s])
    tiles += [f"{n}{c}{t}" for t in range(T) for n in ("ya", "yb") for c in range(2)]
    for t in range(T):
        tiles += [f"mT{t}{q}" for q in range(2)] + [f"xo{c}{t}" for c in range(2)]
    tiles += [f"nT{t}{q}" for t in range(T) for q in range(2)]
    tiles += ["logits", "rank", "count", "gT"]
    NBANK = 8
    ROUTING = {"logits": 4, "rank": 5, "count": 6, "gT": 7}
    TILE, USES = {}, [0] * NBANK
    for n, name in enumerate(tiles):
        b = ROUTING.get(name, n % NBANK)
        TILE[name] = (b, USES[b])
        USES[b] += 1

    with ExitStack() as ctx:
        def sb(name, cols, parts=P, dt=fp32):
            return ctx.enter_context(nc.sbuf_tensor(name, [parts, cols], dt))

        def sem(name):
            return ctx.enter_context(nc.semaphore(name))

        ring = [sb(f"ring{s}", RINGW) for s in range(RING)]
        cst = sb("cst", CONST_W)
        resid = sb("resid", T * D_MODEL)
        hT_m = sb("hT_m", KD * SEQ)
        mem_q = sb("mem_q", 2048)
        mem_k = sb("mem_k", 2048)
        mem_v = sb("mem_v", 2048)
        mem_qn = sb("mem_qn", 2048)
        mem_qr = sb("mem_qr", 1024)
        mem_kv = sb("mem_kv", 4096)
        mem_lt = sb("mem_lt", 1280)
        roped = sb("roped", 3 * COLS)
        rot_a = sb("rot_a", COLS)
        rot_b = sb("rot_b", COLS)
        att = sb("att", 7 * 3 * P)
        kr_pad = sb("kr_pad", T * 3 * MLA_ROPE)
        ki_pad = sb("ki_pad", T * 3 * IDX_DIM)
        krT = sb("krT", 2 * SEQ)
        score = sb("score", 3 * P)
        sel_mask = sb("sel_mask", 3 * P)
        top8 = sb("top8", 8)
        wi = sb("wi", T * IDX_HEADS)
        ssq, msq, root, rstd = [sb(n, 5 * T) for n in ("ssq", "msq", "root", "rstd")]
        N_ATT, N_LAT, N_FFN, N_OUT = 0, T, 3 * T, 4 * T
        negmax = sb("negmax", T * NH)
        psums = sb("psums", T * NH)
        rsum = sb("rsum", T * NH)
        table_i = sb("table_i", 2 * EXTRA_COLS, 1, i32)

        def const(name, t=None):
            a, w = CONST[name]
            if t is None:
                return cst[:, a:a + w]
            w //= T
            return cst[:, a + t * w:a + (t + 1) * w]

        ident = const("ident")

        X = resid[:, :].rearrange("p (t d) -> p t d", t=T)
        HT = hT_m[:, :].rearrange("p (k n) -> p k n", k=KD)
        H = mem_q[:, :].rearrange("p (t d) -> p t d", t=T)
        QI = mem_q[:, 0:1024].rearrange("p (g n) -> p g n", g=4)
        QT = mem_q[:, :].rearrange("p (h n) -> p h n", h=HEADS)
        IDX = mem_k[:, 0:T * W_IDX].rearrange("p (t d) -> p t d", t=T)
        KI = mem_k[:, 1280:1280 + 2 * SEQ].rearrange("p (e n) -> p e n", e=2)
        KT = mem_k[:, :].rearrange("p (h n) -> p h n", h=HEADS)
        gain_ffn = mem_k[:, 0:D_MODEL]
        gain_out = mem_lt[:, 0:D_MODEL]
        LAT = mem_v[:, 0:T * W_LAT].rearrange("p (t d) -> p t d", t=T)
        VD = mem_v[:, :].rearrange("p (t d) -> p t d", t=T)
        MG = VD
        HN = VD
        QN = mem_qn[:, :].rearrange("p (h n) -> p h n", h=HEADS)
        lora_gain = mem_qr[:, 0:Q_LORA + KV_LORA]
        QR = mem_qr[:, :].rearrange("p (g n) -> p g n", g=4)
        gain_attn = mem_kv[:, 0:D_MODEL]
        KN = mem_kv[:, 0:2048].rearrange("p (h n) -> p h n", h=HEADS)
        VM = mem_kv[:, 2048:4096].rearrange("p (t d) -> p t d", t=T)
        G = mem_kv[:, :].rearrange("p (t d) -> p t d", t=T)
        gate_bias = [mem_qr[:, 0:COLS], mem_qr[:, COLS:2 * COLS], mem_lt[:, 0:COLS], mem_lt[:, COLS:2 * COLS]]
        LT = mem_lt[:, :].rearrange("p (k n) -> p k n", k=5)
        KR = krT[:, :].rearrange("p (e n) -> p e n", e=2)
        S = [att[:, 3 * P * b:3 * P * (b + 1)] for b in range(2)]
        PR = [att[:, 3 * P * (2 + b):3 * P * (3 + b)] for b in range(3)]
        PT = [att[:, 3 * P * (5 + b):3 * P * (6 + b)] for b in range(2)]
        RELU = [att[:, COLS * b:COLS * (b + 1)] for b in range(2)]
        q_rot = [att[:, COLS * (2 + t):COLS * (3 + t)] for t in range(T)]
        w_rt = att[:, 0:KD * N_EXPERTS].rearrange("p (k n) -> p k n", k=KD)
        b_rt = att[:, KD * N_EXPERTS:(KD + 1) * N_EXPERTS]

        XG = att[:, 512:1024]
        XGT = att[:, 1024:1536].rearrange("p (k s) -> p k s", k=4)
        GC = att[:, 1536:2048]
        AC = att[:, 2048:2560]
        junk = att[:, 1536:2560]
        SG = roped[:, 0:512]
        Y_0 = roped[:, 0:512]
        ACT_T = roped[:, 512:1024].rearrange("p (k s) -> p k s", k=4)
        BIAS = roped[:, 1024:1536]
        Y = rot_b[:, :]
        PGT = mem_qr[:, 0:512].rearrange("p (h n) -> p h n", h=2)
        GP = mem_qr[:, 512:640].rearrange("p (t s) -> p t s", t=T)
        PG = mem_qr[:, 640:1024].rearrange("p (t s) -> p t s", t=T)
        spare = [(mem_kv[:, 0:2048], mem_kv[:, 2048:4096]), (mem_q[:, :], mem_qn[:, :]), (hT_m[:, :], mem_k[:, :])]

        def by_te(ap):
            return ap.rearrange("p (t e) -> p t e", t=T)

        TE = T * N_EXPERTS
        LGE, CH, GT_, R1, DX, IX, U2, VG = [krT[:, n * TE:(n + 1) * TE] for n in range(8)]
        _r = [0]

        def small(cols):
            _r[0] += cols
            return score[:, _r[0] - cols:_r[0]]

        LPAD, LREP = [small(T * (N_EXPERTS + MOE_TOP_K)) for _ in range(2)]
        REP = small(T * 8)
        nmx, gs, grs, W1, GW = [small(T) for _ in range(5)]
        NB, EXTRA_END, EXTRA_AT = [small(N_EXPERTS) for _ in range(3)]
        assert _r[0] <= 3 * P
        ET = GC
        ER = sel_mask[:, 0:EXTRA_COLS + 1]

        LGE3, CH3, GT3, R13, DX3, LPAD3, LREP3, REP3 = [by_te(a) for a in (LGE, CH, GT_, R1, DX, LPAD, LREP, REP)]
        LG3 = LPAD3[:, :, 0:N_EXPERTS]
        kr_pad3 = kr_pad[:, :].rearrange("p (t d) -> p t d", t=T)
        ki_pad3 = ki_pad[:, :].rearrange("p (t d) -> p t d", t=T)

        bank = [ctx.enter_context(nc.psum_tensor(f"bank{b}", [P, COLS], fp32)) for b in range(NBANK)]
        BG, BL, BY, BM = bank[4], bank[5], bank[6], bank[7]

        def ps(name):
            return bank[TILE[name][0]]

        unit_loaded = [sem(f"unit_loaded{s}") for s in range(RING)]
        unit_used = [sem(f"unit_used{j}") for j in range(RING)]
        psum_full = [sem(f"psum_full{b}") for b in range(NBANK)]
        psum_emptied = [sem(f"psum_emptied{b}") for b in range(NBANK)]
        const_in = sem("const_in")
        ident_in = sem("ident_in")
        x_in = [sem(f"x_in{t}") for t in range(T)]
        gain_in = sem("gain_in")
        lora_in = sem("lora_in")
        gate_bias_in = sem("gate_bias_in")
        router_in = sem("router_in")
        out_gain_in = sem("out_gain_in")
        b_down_in = sem("b_down_in")
        bias_in = sem("bias_in")
        squares = sem("squares")
        means = sem("means")
        roots = sem("roots")
        rstd_ready = sem("rstd_ready")
        h_ready = sem("h_ready")
        lat_ready = sem("lat_ready")
        idx_roped = sem("idx_roped")
        kr_roped = sem("kr_roped")
        tok_roped = sem("tok_roped")
        relu_used = sem("relu_used")
        masked = sem("masked")
        exped = sem("exped")
        normed = sem("normed")
        gate_sig = sem("gate_sig")
        merged = sem("merged")
        resid_done = sem("resid_done")
        hf_ready = sem("hf_ready")
        hn_ready = sem("hn_ready")
        logits_in = sem("logits_in")
        router_exp = sem("router_exp")
        chosen = sem("chosen")
        table = sem("table")
        gates_in = sem("gates_in")
        pads_zero = sem("pads_zero")
        zeroed = sem("zeroed")
        dve_step = sem("dve_step")
        p_ready = sem("p_ready")
        pg_ready = sem("pg_ready")
        xg_ps = sem("xg_ps")
        xg_sb = sem("xg_sb")
        xgT_ps = sem("xgT_ps")
        xgT_sb = sem("xgT_sb")
        bias_used = sem("bias_used")
        h_done = sem("h_done")
        clipped = sem("clipped")
        sig = sem("sig")
        act_ready = sem("act_ready")
        actT_ps = sem("actT_ps")
        actT_sb = sem("actT_sb")
        y_ps = sem("y_ps")
        y_sb = sem("y_sb")
        pgT_ps = sem("pgT_ps")
        pgT_sb = sem("pgT_sb")
        acc_done = sem("acc_done")
        spare_loaded = [sem(f"spare_loaded{j}") for j in range(SPARE)]
        glu_done = sem("glu_done")
        extra_step = sem("extra_step")
        out_ready = sem("out_ready")
        stored = sem("stored")

        block = ctx.enter_context(nc.Block())

        def wait_full(eng, name):
            b, n = TILE[name]
            eng.wait_ge(psum_full[b], n + 1)

        def wait_sb(eng, name):
            b, n = TILE[name]
            eng.wait_ge(psum_emptied[b], n + 1)

        def emptied(name):
            return psum_emptied[TILE[name][0]]

        def full(name):
            return psum_full[TILE[name][0]]

        def over_extra(eng, item, n_extra):
            with eng.If(n_extra > 0):
                with eng.Fori(0, MAX_EXTRA) as q:
                    with eng.If(q < n_extra):
                        item(q)

        def load_n_extra(eng):
            eng.wait_ge(table, 1)
            return eng.value_load(table_i[0:1, EXTRA_COLS:EXTRA_COLS + 1], min_val=0, max_val=MAX_EXTRA)

        def row(v):
            return v.rearrange("a n -> (a n)").partition_broadcast(P)

        def tok(t):
            return slice(t * P, (t + 1) * P)

        @block.sync
        def _(sp):
            def load(name, parts):
                slot, _, before = UNIT[name]
                if before:
                    wait_full(sp, READER[before])
                for dst, src in parts(ring[slot]):
                    sp.dma_start(dst, src).then_inc(unit_loaded[slot], 16)

            def cols(view, a, n, k):
                return lambda r: [(r[:, 0:k * n].rearrange("p (k n) -> p k n", k=k), view[:, :, a:a + n])]

            for t in range(T):
                sp.dma_start(X[:, t, :], x_v[:, t, :]).then_inc(x_in[t], 16)
            for c in range(2):
                load(f"lat{c}", cols(w_in_v, c * LATC, LATC, KD))
            for c in range(2):
                load(f"idx{c}", cols(w_in_v, C_IDX + c * IDXC, IDXC, KD))
            load("uqn", lambda r: [(r[:, k * 1024:(k + 1) * 1024].rearrange("p (h c) -> p h c", c=HD),
                                    uq_v[:, k, :, 0:HD]) for k in range(3)])
            load("uqr", lambda r: [(r[:, k * 512:(k + 1) * 512].rearrange("p (h c) -> p h c", c=MLA_ROPE),
                                    uq_v[:, k, :, HD:MLA_QK]) for k in range(3)])
            load("ukv", lambda r: [(r[:, v * 2048:(v + 1) * 2048].rearrange("p (k n) -> p k n", k=2), w)
                                   for v, w in enumerate((uk_v, uv_v))])
            for c in range(6):
                load(f"qkv{c}", cols(w_in_v, C_QKV + c * COLS, COLS, KD))
            for c in range(4):
                load(f"gate{c}", cols(w_in_v, C_GATE + c * COLS, COLS, KD))
            for n, v in (("oa", oa_v), ("ob", ob_v), ("wo", wo_v)):
                for c in range(2):
                    load(f"{n}{c}", cols(v, c * COLS, COLS, KD))

            def item_load(j, e, dst=None, done=None):
                slot = ITEM_SLOT[j]
                if j < GU_UNITS:
                    src = gu_v[e, j // 2, :, 2 * (j % 2):2 * (j % 2) + 2, :].rearrange("e p k n -> p (e k) n")
                    if dst is not None:
                        for k in range(2):
                            sp.dma_start(dst[k], src[:, k, :]).then_inc(done, 16)
                        return
                    dst = ring[slot][:, :].rearrange("p (k n) -> p k n", k=2)
                else:
                    src = dn_v[e, j - GU_UNITS, :, :, :].rearrange("e p k n -> p (e k) n")
                    dst = ring[slot][:, :].rearrange("p (k n) -> p k n", k=4)
                sp.dma_start(dst, src).then_inc(unit_loaded[slot], 16)

            def bias_load(e):
                sp.dma_start(BIAS[0:4, :], bgu_v[e, :, :].rearrange("e n c -> (e n) c")).then_inc(bias_in, 16)

            first, second = slice(0, 1), slice(1, 2)
            wait_sb(sp, f"yb1{T - 1}")
            item_load(0, first, spare[0], spare_loaded[0])
            item_load(1, first, spare[1], spare_loaded[1])
            for j in range(RING):
                wait_full(sp, LAST_FRONT[j])
                item_load(j, first if j >= SPARE else second)
            sp.wait_ge(zeroed, 3)
            bias_load(first)
            wait_full(sp, "logits")
            sp.wait_ge(hf_ready, 2 * T)
            item_load(2, first, spare[2], spare_loaded[2])

            def item(i, e, missing=range(RING)):
                for j in missing:
                    if j == 3:
                        sp.wait_ge(h_done, i)
                    elif j == 5:
                        sp.wait_ge(y_ps, i)
                    else:
                        sp.wait_ge(unit_used[j], i)
                    item_load(j, e)
                    if j == missing[0]:
                        sp.wait_ge(bias_used, i)
                        bias_load(e)

            item(1, second, range(SPARE, RING))
            with sp.Fori(2, N_EXPERTS) as i:
                item(i, bass.ds(i, 1))

            def extra(q):
                e = sp.value_load(table_i[0:1, bass.ds(q, 1)], min_val=0, max_val=N_EXPERTS - 1)
                item(q + N_EXPERTS, bass.ds(e, 1))

            over_extra(sp, extra, load_n_extra(sp))
            for t in range(T):
                sp.wait_ge(out_ready, t + 1)
                sp.dma_start(out_v[:, t, :], X[:, t, :]).then_inc(stored, 16)
            sp.wait_ge(stored, 16 * T)

        @block.gpsimd
        def _(pool):
            nc.gpsimd.memset(kr_pad[:, :], 0.0).then_inc(pads_zero, 1)
            nc.gpsimd.memset(ki_pad[:, :], 0.0).then_inc(pads_zero, 1)
            wait_sb(pool, f"yb1{T - 1}")
            nc.gpsimd.memset(BIAS[:, :], 0.0).then_inc(zeroed, 1)
            nc.gpsimd.memset(PG[:, :, :], 0.0).then_inc(zeroed, 1)
            nc.gpsimd.memset(Y_0, 0.0).then_inc(zeroed, 1)
            pool.wait_ge(zeroed, 3)
            for h in range(2):
                pool.dma_start(Y_0[SLOTS * h:SLOTS * h + N_EXPERTS, :], bdn_v[:, h * COLS:(h + 1) * COLS])\
                    .then_inc(b_down_in, 16)
            pool.wait_ge(b_down_in, 32)

        @block.scalar
        def _(act):
            act.dma_start(gain_attn, row(norm_attn_g)).then_inc(gain_in, 16)
            act.dma_start(cst[:, 0:P], consts[:, 0:P]).then_inc(ident_in, 16)
            act.dma_start(cst[:, P:CONST_W], consts[:, P:CONST_W]).then_inc(const_in, 16)
            act.dma_start(lora_gain[:, 0:Q_LORA], row(q_lora_g)).then_inc(lora_in, 16)
            act.dma_start(lora_gain[:, Q_LORA:Q_LORA + KV_LORA], row(kv_lora_g)).then_inc(lora_in, 16)

            n_squares = [0]

            def square(dst, src, junk):
                if n_squares[0]:
                    act.wait_ge(squares, n_squares[0])
                nc.scalar.activation(junk, src, ACT.Square, accum_out=dst).then_inc(squares, 1)
                n_squares[0] += 1

            def roots_of(n, a, b):
                act.wait_ge(means, n)
                nc.scalar.activation(root[:, a:b], msq[:, a:b], ACT.Sqrt).then_inc(roots, 1)

            def evacuate(name, dst, src, scale=None):
                wait_full(act, name)
                if scale is None:
                    ins = nc.scalar.activation(dst, src, ACT.Copy)
                else:
                    ins = nc.scalar.activation(dst, src, ACT.Identity, scale=scale)
                ins.then_inc(emptied(name), 1)

            def blocks(name, k=4):
                return ps(name)[:, 0:k * P].rearrange("p (k n) -> p k n", k=k)

            for t in range(T):
                act.wait_ge(x_in[t], 16)
                square(ssq[:, N_ATT + t:N_ATT + t + 1], X[:, t, :], VM[:, 0, :])
            for t in range(T):
                for q in range(2):
                    evacuate(f"hT{t}{q}", HT[:, 4 * q:4 * q + 4, tok(t)], blocks(f"hT{t}{q}"))
            roots_of(1, N_ATT, N_ATT + T)
            act.wait_ge(rstd_ready, 1)

            def att_scale(t):
                return rstd[:, N_ATT + t:N_ATT + t + 1]

            for c in range(2):
                for t in range(T):
                    evacuate(f"lat{c}{t}", LAT[:, t, c * LATC:(c + 1) * LATC], ps(f"lat{c}{t}")[:, 0:LATC], att_scale(t))
            wait_sb(act, f"lat1{T - 1}")
            for t in range(T):
                a = N_LAT + t
                square(ssq[:, a:a + 1], LAT[:, t, 0:Q_LORA], att[:, 0:Q_LORA])
                square(ssq[:, a + T:a + T + 1], LAT[:, t, Q_LORA:Q_LORA + KV_LORA], att[:, 0:KV_LORA])
            roots_of(2, N_LAT, N_LAT + 2 * T)
            for c in range(2):
                for t in range(T):
                    evacuate(f"idx{c}{t}", IDX[:, t, c * IDXC:(c + 1) * IDXC], ps(f"idx{c}{t}")[:, 0:IDXC], att_scale(t))
            for t in range(T):
                evacuate(f"cqT{t}", LT[:, 0:3, tok(t)], blocks(f"cqT{t}", 3))
                n = f"ckvT{t}"
                wait_full(act, n)
                nc.scalar.activation(LT[:, 3:5, tok(t)], blocks(n)[:, 0:2, :], ACT.Copy)
                nc.scalar.activation(KR[:, :, tok(t)], blocks(n)[:, 2:4, :], ACT.Copy).then_inc(emptied(n), 1)
            for g in range(4):
                evacuate(f"qn{g}", QN[:, 2 * g:2 * g + 2, :], ps(f"qn{g}")[:, :].rearrange("p (h n) -> p h n", h=2))
            for g in range(4):
                evacuate(f"kn{g}", KN[:, 2 * g:2 * g + 2, :], ps(f"kn{g}")[:, :].rearrange("p (h n) -> p h n", h=2))
            for c in range(2):
                for t in range(T):
                    evacuate(f"vm{c}{t}", VM[:, t, c * COLS:(c + 1) * COLS], ps(f"vm{c}{t}")[:, :])
            for t in range(T):
                evacuate(f"qiT{t}", QI[:, :, tok(t)], blocks(f"qiT{t}"))
            evacuate("kiT", KI[:, :, :].rearrange("p e (t n) -> p e t n", t=T),
                     ps("kiT")[:, :].rearrange("p (t e n) -> p e t n", t=T, e=2))
            for t in range(T):
                evacuate(f"qrT{t}", QR[:, :, tok(t)], blocks(f"qrT{t}"))
            for t in range(T):
                for g in range(4):
                    n, keys, u = f"raw{t}{g}", P * (t + 1), 4 * t + g
                    if u >= 2:
                        act.wait_ge(relu_used, u - 1)
                    wait_full(act, n)
                    nc.scalar.activation(RELU[u % 2][:, 0:2 * keys], ps(n)[:, 0:2 * keys], ACT.Relu,
                                         scale=IDX_DIM ** -0.5).then_inc(emptied(n), 1)
            for c, t in QK:
                evacuate(f"qkT{c}{t}", (QT, KT)[c // 2][:, 4 * (c % 2):4 * (c % 2) + 4, tok(t)], blocks(f"qkT{c}{t}"))
            for s in range(NH + 2):
                if s < NH:
                    act.wait_ge(masked, s + 1)
                    for t in range(T):
                        a, w, col = t * P, P * (t + 1), s * T + t
                        nc.scalar.activation(PR[s % 3][:, a:a + w], S[s % 2][:, a:a + w], ACT.Exp,
                                             bias=negmax[:, col:col + 1],
                                             accum_out=psums[:, col:col + 1]).then_inc(exped, 1)
                if s >= 2:
                    evacuate(f"pT{s - 2}", PT[s % 2], ps(f"pT{s - 2}")[:, 0:3 * P])
                if s in BETWEEN and BETWEEN[s][0] == "v":
                    _, c, t = BETWEEN[s]
                    evacuate(f"v{c}{t}", VD[:, t, c * COLS:(c + 1) * COLS], ps(f"v{c}{t}")[:, :], att_scale(t))
                if s == HEADS + 2:
                    for c in range(4):
                        act.dma_start(gate_bias[c], b_gate[0, c * COLS:(c + 1) * COLS].partition_broadcast(P))\
                            .then_inc(gate_bias_in, 16)
            act.dma_start(gain_ffn, row(norm_ffn_g)).then_inc(gain_in, 16)
            act.dma_start(w_rt, wr_v).then_inc(router_in, 16)
            act.dma_start(b_rt, row(b_router)).then_inc(router_in, 16)
            for c in range(4):
                for t in range(T):
                    wait_sb(act, f"gate{c}{t}")
                    g = G[:, t, c * COLS:(c + 1) * COLS]
                    nc.scalar.activation(g, g, ACT.Sigmoid).then_inc(gate_sig, 1)
            act.dma_start(gain_out, norm_final_g.partition_broadcast(P)).then_inc(out_gain_in, 16)
            for t in range(T):
                for q in range(2):
                    evacuate(f"mT{t}{q}", HT[:, 4 * q:4 * q + 4, tok(t)], blocks(f"mT{t}{q}"))
            for t in range(T):
                for c in range(2):
                    wait_sb(act, f"xo{c}{t}")
                square(ssq[:, N_FFN + t:N_FFN + t + 1], X[:, t, :], junk)
            for t in range(T):
                for q in range(2):
                    evacuate(f"nT{t}{q}", HT[:, 4 * q:4 * q + 4, tok(t)], blocks(f"nT{t}{q}"))
            roots_of(3, N_FFN, N_FFN + T)
            act.wait_ge(rstd_ready, 3)
            for t in range(T):
                nc.scalar.activation(HN[:, t, :], HN[:, t, :], ACT.Identity,
                                     scale=rstd[:, N_FFN + t:N_FFN + t + 1]).then_inc(hn_ready, 1)
            act.wait_ge(b_down_in, 32)
            nc.scalar.activation(Y, Y_0, ACT.Copy).then_inc(y_sb, 1)
            act.wait_ge(logits_in, 1)
            for t in range(T):
                nc.scalar.activation(LGE3[:, t, :], LG3[:, t, :], ACT.Exp, bias=nmx[:, t:t + 1]).then_inc(router_exp, 1)

            def gathered(item):
                act.wait_ge(xg_ps, item + 1)
                nc.scalar.activation(XG, BM[:, :], ACT.Copy).then_inc(xg_sb, 1)
                act.wait_ge(xgT_ps, item + 1)
                nc.scalar.activation(XGT, BY[:, :].rearrange("p (k s) -> p k s", k=4), ACT.Copy).then_inc(xgT_sb, 1)

            gathered(0)

            def item(i):
                act.wait_ge(clipped, i + 1)
                nc.scalar.activation(SG, GC, ACT.Sigmoid, scale=SWIGLU_ALPHA).then_inc(sig, 1)
                gathered(i + 1)
                act.wait_ge(actT_ps, i + 1)
                nc.scalar.activation(ACT_T, BM[:, :].rearrange("p (k s) -> p k s", k=4), ACT.Copy).then_inc(actT_sb, 1)
                act.wait_ge(y_ps, i + 1)
                nc.scalar.activation(Y, BY[:, :], ACT.Copy).then_inc(y_sb, 1)

            with act.Fori(0, N_EXPERTS) as i:
                item(i)
            over_extra(act, lambda q: item(q + N_EXPERTS), load_n_extra(act))
            nc.scalar.activation(root[:, N_ATT:N_ATT + 1], const("ones")[:, 0:1], ACT.Sqrt)
            for t in range(T):
                act.wait_ge(resid_done, 2 * t + 2)
                square(ssq[:, N_OUT + t:N_OUT + t + 1], X[:, t, :], junk)
            for t in range(T):
                roots_of(4 + t, N_OUT + t, N_OUT + t + 1)

        @block.tensor
        def _(pe):
            def claim(name):
                b, n = TILE[name]
                if n:
                    pe.wait_ge(psum_emptied[b], n)
                return bank[b]

            def arrived(name):
                pe.wait_ge(unit_loaded[UNIT[name][0]], UNIT[name][1])
                return ring[UNIT[name][0]]

            def transposes(name, sources):
                o = claim(name)
                for n, src in enumerate(sources):
                    last = nc.tensor.transpose(o[:, n * P:(n + 1) * P], src, ident)
                last.then_inc(full(name), 1)

            def product(o, lhs, rhs, kk):
                for k in range(kk):
                    last = nc.tensor.matmul(o, lhs(k), rhs(k), start=(k == 0), stop=(k == kk - 1))
                return last

            def chunk(unit, name, a, width=COLS):
                w = arrived(unit)[:, 0:KD * width].rearrange("p (k n) -> p k n", k=KD)
                for t in range(T):
                    o = claim(f"{name}{t}")
                    product(o[:, 0:width], lambda k: a[:, k, tok(t)], lambda k: w[:, k, :], KD)\
                        .then_inc(full(f"{name}{t}"), 1)

            def one(name, unit, c, t, a, width=COLS):
                w = arrived(unit)[:, 0:KD * width].rearrange("p (k n) -> p k n", k=KD)
                o = claim(f"{name}{c}{t}")
                product(o[:, 0:width], lambda k: a[:, k, tok(t)], lambda k: w[:, k, :], KD)\
                    .then_inc(full(f"{name}{c}{t}"), 1)

            def turned(name, a, t):
                for q in range(2):
                    transposes(f"{name}{t}{q}", [a[:, t, (4 * q + b) * P:(4 * q + b + 1) * P] for b in range(4)])

            def turned_in(name, t):
                for q in range(2):
                    wait_sb(pe, f"{name}{t}{q}")

            pe.wait_ge(ident_in, 16)
            for t in range(T):
                pe.wait_ge(h_ready, t + 1)
                turned("hT", H, t)
            for t in range(T):
                turned_in("hT", t)
            for c in range(2):
                chunk(f"lat{c}", f"lat{c}", HT, LATC)
            for c in range(2):
                chunk(f"idx{c}", f"idx{c}", HT, IDXC)
            pe.wait_ge(lat_ready, 2 * T)
            pe.wait_ge(kr_roped, T)
            for t in range(T):
                transposes(f"cqT{t}", [LAT[:, t, k * P:(k + 1) * P] for k in range(3)])
                transposes(f"ckvT{t}", [LAT[:, t, Q_LORA + k * P:Q_LORA + (k + 1) * P] for k in range(2)]
                           + [kr_pad3[:, t, MLA_ROPE:3 * MLA_ROPE], kr_pad3[:, t, 0:2 * MLA_ROPE]])
            for t in range(T):
                wait_sb(pe, f"cqT{t}")
                wait_sb(pe, f"ckvT{t}")
            w = arrived("uqn")[:, 0:3 * 1024].rearrange("p (k n) -> p k n", k=3)
            for g in range(4):
                o = claim(f"qn{g}")
                for h in range(2):
                    last = product(o[:, h * SEQ:(h + 1) * SEQ], lambda k: w[:, k, (2 * g + h) * HD:(2 * g + h + 1) * HD],
                                   lambda k: LT[:, k, :], 3)
                last.then_inc(full(f"qn{g}"), 1)
            wr = arrived("uqr")[:, 0:3 * 512].rearrange("p (k n) -> p k n", k=3)
            for t in range(T):
                o = claim(f"qr{t}")
                product(o[:, :], lambda k: LT[:, k, tok(t)], lambda k: wr[:, k, :], 3).then_inc(full(f"qr{t}"), 1)
            wkv = arrived("ukv")[:, :].rearrange("p (v k n) -> p v k n", v=2, k=2)
            for g in range(4):
                o = claim(f"kn{g}")
                for h in range(2):
                    last = product(o[:, h * SEQ:(h + 1) * SEQ],
                                   lambda k: wkv[:, 0, k, (2 * g + h) * HD:(2 * g + h + 1) * HD],
                                   lambda k: LT[:, 3 + k, :], 2)
                last.then_inc(full(f"kn{g}"), 1)
            for c in range(2):
                for t in range(T):
                    o = claim(f"vm{c}{t}")
                    product(o[:, :], lambda k: LT[:, 3 + k, tok(t)], lambda k: wkv[:, 1, k, c * COLS:(c + 1) * COLS], 2)\
                        .then_inc(full(f"vm{c}{t}"), 1)
            for t in range(T):
                pe.wait_ge(idx_roped, t + 1)
                transposes(f"qiT{t}", [roped[:, t * COLS + g * P:t * COLS + (g + 1) * P] for g in range(4)])
            transposes("kiT", [ki_pad3[:, t, a:a + P] for t in range(T) for a in (IDX_DIM, 0)])
            for t in range(T):
                pe.wait_ge(tok_roped, t + 1)
                transposes(f"qrT{t}", [q_rot[t][:, g * P:(g + 1) * P] for g in range(4)])
            wait_sb(pe, "kiT")
            for t in range(T):
                keys = P * (t + 1)
                for g in range(4):
                    o = claim(f"raw{t}{g}")
                    for e in range(2):
                        last = nc.tensor.matmul(o[:, e * keys:(e + 1) * keys], QI[:, g, tok(t)], KI[:, e, 0:keys],
                                                start=True, stop=True)
                    last.then_inc(full(f"raw{t}{g}"), 1)
            for n in range(len(QK) + 1):
                if n < len(QK):
                    c, t = QK[n]
                    w = arrived(f"qkv{c}")[:, :].rearrange("p (k n) -> p k n", k=KD)
                    o = claim(f"qk{c}{t}")
                    product(o[:, :], lambda k: HT[:, k, tok(t)], lambda k: w[:, k, :], KD).then_inc(full(f"qk{c}{t}"), 1)
                if n:
                    pe.wait_ge(tok_roped, T + n)
                    a = COLS * ((n + 1) % 3)
                    transposes("qkT%d%d" % QK[n - 1], [roped[:, a + g * P:a + (g + 1) * P] for g in range(4)])
            wait_sb(pe, "qkT%d%d" % QK[-1])

            for s in range(NH + 3):
                if s < NH:
                    h = s % HEADS
                    o = claim(f"s{s}")
                    for t in range(T):
                        w = P * (t + 1)
                        ot = o[:, t * P:t * P + w]
                        if s < HEADS:
                            nc.tensor.matmul(ot, QN[:, h, tok(t)], KN[:, h, 0:w], start=True, stop=False)
                            last = nc.tensor.matmul(ot, QR[:, h // 2, tok(t)], KR[:, h % 2, 0:w], start=False, stop=True)
                        else:
                            last = nc.tensor.matmul(ot, QT[:, h, tok(t)], KT[:, h, 0:w], start=True, stop=True)
                    last.then_inc(full(f"s{s}"), 1)
                if 2 <= s < NH + 2:
                    pe.wait_ge(normed, s - 1)
                    transposes(f"pT{s - 2}", [PR[(s - 2) % 3][:, a * P:(a + 1) * P] for a in range(3)])
                if s >= 3:
                    h = (s - 3) % HEADS
                    v = (VM if s - 3 < HEADS else VD)
                    if s - 3 == HEADS:
                        wait_sb(pe, "v11")
                    pt = PT[(s - 3) % 2]
                    o = claim(f"o{s - 3}")
                    wait_sb(pe, f"pT{s - 3}")
                    nc.tensor.matmul(o[:, 0:SEQ], v[:, 0, h * HD:(h + 1) * HD], pt[:, 0:SEQ], start=True, stop=False)
                    nc.tensor.matmul(o[:, P:SEQ], v[:, 1, h * HD:(h + 1) * HD], pt[:, SEQ:3 * P],
                                     start=False, stop=True).then_inc(full(f"o{s - 3}"), 1)
                if s in BETWEEN:
                    kind, c, t = BETWEEN[s]
                    one(kind, f"qkv{4 + c}" if kind == "v" else f"gate{c}", c, t, HT)
            for h in range(NH):
                wait_sb(pe, f"o{h}")
            for t in range(T):
                for name, unit, a in (("ya", "oa", QN), ("yb", "ob", QT)):
                    for c in range(2):
                        one(name, f"{unit}{c}", c, t, a)
            for t in range(T):
                pe.wait_ge(merged, 2 * t + 2)
                turned("mT", MG, t)
                turned_in("mT", t)
                for c in range(2):
                    one("xo", f"wo{c}", c, t, HT)
            for t in range(T):
                pe.wait_ge(hf_ready, 2 * t + 2)
                turned("nT", HN, t)
            for t in range(T):
                turned_in("nT", t)
            pe.wait_ge(router_in, 32)
            o = claim("logits")
            for t in range(T):
                last = product(o[:, t * N_EXPERTS:(t + 1) * N_EXPERTS], lambda k: HT[:, k, tok(t)],
                               lambda k: w_rt[:, k, :], KD)
            last.then_inc(full("logits"), 1)
            for b in range(4):
                pe.wait_ge(psum_emptied[b], USES[b])
                nc.tensor.matmul(bank[b][:, :], const("zero"), cst[:, 0:COLS], start=True, stop=False)
            pe.wait_ge(chosen, 1)
            o = claim("rank")
            for t in range(T):
                ot = o[:, t * N_EXPERTS:(t + 1) * N_EXPERTS]
                for b in range(t + 1):
                    last = nc.tensor.matmul(ot, const("ones") if b < t else const("before"), CH3[:, b, :],
                                            start=(b == 0), stop=(b == t))
            last.then_inc(full("rank"), 1)
            o = claim("count")
            product(o[:, 0:N_EXPERTS], lambda b: const("ones"), lambda b: CH3[:, b, :], T).then_inc(full("count"), 1)
            pe.wait_ge(gates_in, 1)

            def gates_turned(o):
                for h in range(2):
                    for t in range(T):
                        a = SLOTS * (1 - h)
                        last = nc.tensor.transpose(o[:, (T * h + t) * P:(T * h + t + 1) * P], PG[:, t, a:a + P], ident)
                return last

            gates_turned(claim("gT")).then_inc(full("gT"), 1)

            def gather(item):
                pe.wait_ge(p_ready, item + 1)
                for t in range(T):
                    for h in range(2):
                        last = nc.tensor.matmul(BM[SLOTS * h:SLOTS * (h + 1), :], GP[:, t, :],
                                                HN[:, t, h * COLS:(h + 1) * COLS], start=(t == 0), stop=(t == T - 1))
                last.then_inc(xg_ps, 1)
                pe.wait_ge(xg_sb, item + 1)
                pe.wait_ge(pgT_sb, item + 1)
                rows = XG.rearrange("p (c k) -> p k c", k=4)
                for k in range(4):
                    last = nc.tensor.transpose(BY[:, k * P:(k + 1) * P], rows[:, k, :], ident)
                last.then_inc(xgT_ps, 1)

            def scatter(stop):
                for t in range(T):
                    for h in range(2):
                        ins = nc.tensor.matmul(bank[2 * t + h][:, :], PGT[:, h, tok(t)], Y, start=False, stop=stop)
                    if stop:
                        ins.then_inc(acc_done, 1)

            for b in range(4, NBANK - 1):
                pe.wait_ge(psum_emptied[b], USES[b])
            pe.wait_ge(pgT_sb, 1)
            pe.wait_ge(hn_ready, T)
            gather(0)

            def item(i, in_spare=False):
                pe.wait_ge(bias_in, 16 * i + 16)
                for n in range(4):
                    last = nc.tensor.matmul((BG, BL)[n // 2][SLOTS * (n % 2):SLOTS * (n % 2 + 1), :],
                                            const("row_of")[:, n * SLOTS:(n + 1) * SLOTS], BIAS,
                                            start=True, stop=False)
                last.then_inc(bias_used, 1)
                pe.wait_ge(xgT_sb, i + 1)
                for j in range(GU_UNITS):
                    if in_spare and j < SPARE:
                        pe.wait_ge(spare_loaded[j], 32)
                        w = spare[j]
                    else:
                        pe.wait_ge(unit_loaded[ITEM_SLOT[j]], ITEM_AT[j] + 16 * i)
                        r = ring[ITEM_SLOT[j]]
                        w = (r[:, 0:RINGW // 2], r[:, RINGW // 2:RINGW])
                    for k in range(2):
                        lhs = XGT[:, 2 * (j % 2) + k, SLOTS * (j // 2):SLOTS * (j // 2 + 1)]
                        for n in range(4):
                            last = nc.tensor.matmul((BG, BL)[n // 2][SLOTS * (n % 2):SLOTS * (n % 2 + 1), :], lhs,
                                                    w[k][:, n * COLS:(n + 1) * COLS], start=False,
                                                    stop=(j == GU_UNITS - 1 and k == 1))
                    last.then_inc(unit_used[j] if j < GU_UNITS - 1 else h_done, 1)
                pe.wait_ge(y_sb, i + 1)
                pe.wait_ge(pgT_sb, i + 1)
                scatter(False)
                pe.wait_ge(pg_ready, i + 1)
                gates_turned(BY).then_inc(pgT_ps, 1)
                gather(i + 1)
                pe.wait_ge(act_ready, i + 1)
                rows = AC.rearrange("p (c k) -> p k c", k=4)
                for k in range(4):
                    last = nc.tensor.transpose(BM[:, k * P:(k + 1) * P], rows[:, k, :], ident)
                last.then_inc(actT_ps, 1)
                pe.wait_ge(actT_sb, i + 1)
                pe.wait_ge(xgT_sb, i + 2)
                for h in range(2):
                    j = GU_UNITS + h
                    pe.wait_ge(unit_loaded[ITEM_SLOT[j]], ITEM_AT[j] + 16 * i)
                    w = ring[ITEM_SLOT[j]][:, :].rearrange("p (k n) -> p k n", k=4)
                    for k in range(4):
                        for n in range(2):
                            last = nc.tensor.matmul(BY[SLOTS * n:SLOTS * (n + 1), :],
                                                    ACT_T[:, k, SLOTS * h:SLOTS * (h + 1)],
                                                    w[:, k, n * COLS:(n + 1) * COLS],
                                                    start=(h == 0 and k == 0), stop=(h == 1 and k == 3))
                    last.then_inc(unit_used[j] if h == 0 else y_ps, 1)

            item(0, in_spare=True)
            with pe.Fori(1, N_EXPERTS) as i:
                item(i)
            n_extra = load_n_extra(pe)
            over_extra(pe, lambda q: item(q + N_EXPERTS), n_extra)
            pe.wait_ge(y_sb, n_extra + (N_EXPERTS + 1))
            pe.wait_ge(pgT_sb, n_extra + (N_EXPERTS + 1))
            scatter(True)

        @block.vector
        def _(dve):
            steps = [0]

            def step(ins):
                steps[0] += 1
                ins.then_inc(dve_step, 1)
                dve.wait_ge(dve_step, steps[0])

            def norm_scale(n, n_squares, *parts):
                dve.wait_ge(squares, n_squares)
                for a, b, width in parts:
                    last = nc.vector.tensor_scalar(msq[:, a:b], ssq[:, a:b], 1.0 / width, NORM_EPS, ALU.mult, ALU.add)
                last.then_inc(means, 1)
                dve.wait_ge(roots, n)
                a, b = parts[0][0], parts[-1][1]
                nc.vector.reciprocal(rstd[:, a:b], root[:, a:b]).then_inc(rstd_ready, 1)
                dve.wait_ge(rstd_ready, n)

            def rotate(dst, src, cos, sin, groups, half, freed=None, done=None, scale=1.0):
                w = 2 * half
                a = rot_a[:, 0:groups * w].rearrange("p (g d) -> p g d", g=groups)
                b = rot_b[:, 0:groups * w].rearrange("p (g d) -> p g d", g=groups)
                c = cos.unsqueeze(1).to_broadcast([P, groups, w])
                s = sin.unsqueeze(1).to_broadcast([P, groups, w])
                lo, hi = slice(0, half), slice(half, w)
                nc.vector.scalar_tensor_tensor(a, src, scale, c, ALU.mult, ALU.mult)
                nc.vector.scalar_tensor_tensor(b[:, :, lo], src[:, :, hi], scale, s[:, :, lo], ALU.mult, ALU.mult)
                ins = nc.vector.scalar_tensor_tensor(b[:, :, hi], src[:, :, lo], scale, s[:, :, hi], ALU.mult, ALU.mult)
                if freed:
                    ins.then_inc(freed[0], 1)
                    dve.wait_ge(*freed)
                else:
                    step(ins)
                ins = nc.vector.tensor_tensor(dst, a, b, ALU.add)
                if done:
                    ins.then_inc(done[0], 1)
                    dve.wait_ge(*done)
                else:
                    step(ins)

            def freed_at(name):
                return (emptied(name), TILE[name][1] + 1)

            dve.wait_ge(gain_in, 16)
            for t in range(T):
                dve.wait_ge(x_in[t], 16)
                nc.vector.tensor_tensor(H[:, t, :], X[:, t, :], gain_attn, ALU.mult).then_inc(h_ready, 1)
            norm_scale(1, T, (N_ATT, N_ATT + T, D_MODEL))
            norm_scale(2, 3 * T, (N_LAT, N_LAT + T, Q_LORA), (N_LAT + T, N_LAT + 2 * T, KV_LORA))
            dve.wait_ge(lora_in, 32)
            for t in range(T):
                for a, w, col in ((0, Q_LORA, N_LAT + t), (Q_LORA, KV_LORA, N_LAT + T + t)):
                    nc.vector.scalar_tensor_tensor(LAT[:, t, a:a + w], LAT[:, t, a:a + w], rstd[:, col:col + 1],
                                                   lora_gain[:, a:a + w], ALU.mult, ALU.mult).then_inc(lat_ready, 1)
            dve.wait_ge(pads_zero, 1)
            dve.wait_ge(const_in, 16)
            for t in range(T):
                rotate(kr_pad3[:, t, MLA_ROPE:2 * MLA_ROPE].unsqueeze(1), LAT[:, t, W_LAT - MLA_ROPE:W_LAT].unsqueeze(1),
                       const("cos_m", t), const("sin_m", t), 1, MLA_ROPE // 2, done=(kr_roped, t + 1))
            dve.wait_ge(pads_zero, 2)
            for c in range(2):
                for t in range(T):
                    wait_sb(dve, f"idx{c}{t}")
            for t in range(T):
                kq = ki_pad3[:, t, IDX_DIM:2 * IDX_DIM].unsqueeze(1)
                ki = IDX[:, t, IDX_HEADS * IDX_DIM:(IDX_HEADS + 1) * IDX_DIM].unsqueeze(1)
                rotate(kq[:, :, 0:IDX_ROPE], ki[:, :, 0:IDX_ROPE], const("cos_i", t), const("sin_i", t), 1, IDX_ROPE // 2)
                nc.vector.tensor_copy(kq[:, :, IDX_ROPE:IDX_DIM], ki[:, :, IDX_ROPE:IDX_DIM])
                qd = roped[:, t * COLS:(t + 1) * COLS].rearrange("p (h d) -> p h d", d=IDX_DIM)
                qi = IDX[:, t, 0:IDX_HEADS * IDX_DIM].rearrange("p (h d) -> p h d", d=IDX_DIM)
                nc.vector.tensor_copy(qd[:, :, IDX_ROPE:IDX_DIM], qi[:, :, IDX_ROPE:IDX_DIM])
                nc.vector.tensor_scalar(wi[:, t * IDX_HEADS:(t + 1) * IDX_HEADS], IDX[:, t, (IDX_HEADS + 1) * IDX_DIM:W_IDX],
                                        IDX_HEADS ** -0.5, None, ALU.mult)
                rotate(qd[:, :, 0:IDX_ROPE], qi[:, :, 0:IDX_ROPE], const("cos_i", t), const("sin_i", t), IDX_HEADS,
                       IDX_ROPE // 2, done=(idx_roped, t + 1))
            for t in range(T):
                n = f"qr{t}"
                wait_full(dve, n)
                rotate(q_rot[t].rearrange("p (h d) -> p h d", d=MLA_ROPE),
                       ps(n)[:, :].rearrange("p (h d) -> p h d", d=MLA_ROPE), const("cos_m", t), const("sin_m", t),
                       HEADS, MLA_ROPE // 2, freed_at(n), (tok_roped, t + 1))
            for t in range(T):
                keys = P * (t + 1)
                sc = score[:, t * P:t * P + keys]
                for g in range(4):
                    u = 4 * t + g
                    wait_sb(dve, f"raw{t}{g}")
                    for e in range(2):
                        r = RELU[u % 2][:, e * keys:(e + 1) * keys]
                        w = wi[:, t * IDX_HEADS + 2 * g + e:t * IDX_HEADS + 2 * g + e + 1]
                        if g == 0 and e == 0:
                            ins = nc.vector.tensor_scalar(sc, r, w, None, ALU.mult)
                        else:
                            ins = nc.vector.scalar_tensor_tensor(sc, r, w, sc, ALU.mult, ALU.add)
                        if e == 0:
                            step(ins)
                        else:
                            ins.then_inc(relu_used, 1)
                            dve.wait_ge(relu_used, u + 1)
            step(nc.vector.tensor_tensor(score[:, :], score[:, :], const("chunk_mask"), ALU.add))

            def select(t):
                sc = score[:, t * P:t * P + P * (t + 1)]
                for _ in range(TOP_K // 8):
                    step(nc.vector.max(top8[:, :], sc))
                    step(nc.vector.match_replace(sc, top8[:, :], sc, TAKEN))
                step(nc.vector.tensor_scalar(sel_mask[:, t * P:t * P + P * (t + 1)], sc, TAKEN, MASKED,
                                             ALU.not_equal, ALU.mult))

            for n, (c, t) in enumerate(QK):
                name = f"qk{c}{t}"
                if n:
                    wait_full(dve, "qkT%d%d" % QK[n - 3] if n >= 3 else f"qiT{n - 1}")
                wait_full(dve, name)
                a = COLS * ((n + 2) % 3)
                rotate(roped[:, a:a + COLS].rearrange("p (h d) -> p h d", d=HD),
                       ps(name)[:, :].rearrange("p (h d) -> p h d", d=HD), const("cos_d", t), const("sin_d", t),
                       COLS // HD, HD // 2, freed_at(name), (tok_roped, T + n + 1),
                       rstd[:, N_ATT + t:N_ATT + t + 1])
                if n < T:
                    select(n)
            for s in range(NH + 3):
                if s < NH:
                    n = f"s{s}"
                    wait_full(dve, n)
                    nc.vector.scalar_tensor_tensor(S[s % 2], ps(n)[:, 0:3 * P],
                                                   (MLA_QK if s < HEADS else HD) ** -0.5,
                                                   const("chunk_mask") if s < HEADS else sel_mask[:, :],
                                                   ALU.mult, ALU.add).then_inc(emptied(n), 1)
                    dve.wait_ge(*freed_at(n))
                    for t in range(T):
                        ins = nc.vector.tensor_reduce(negmax[:, s * T + t:s * T + t + 1],
                                                      S[s % 2][:, t * P:t * P + P * (t + 1)], AX, ALU.max, negate=True)
                    ins.then_inc(masked, 1)
                if 1 <= s <= NH:
                    h = s - 1
                    dve.wait_ge(exped, T * s)
                    step(nc.vector.reciprocal(rsum[:, h * T:(h + 1) * T], psums[:, h * T:(h + 1) * T]))
                    for t in range(T):
                        p = PR[h % 3][:, t * P:t * P + P * (t + 1)]
                        ins = nc.vector.tensor_scalar(p, p, rsum[:, h * T + t:h * T + t + 1], None, ALU.mult)
                    ins.then_inc(normed, 1)
                if s >= 3:
                    n = f"o{s - 3}"
                    wait_full(dve, n)
                    nc.vector.tensor_copy((QN if s - 3 < HEADS else QT)[:, (s - 3) % HEADS, :], ps(n)[:, 0:SEQ])\
                        .then_inc(emptied(n), 1)
                if s in BETWEEN and BETWEEN[s][0] == "gate":
                    _, c, t = BETWEEN[s]
                    n = f"gate{c}{t}"
                    dve.wait_ge(gate_bias_in, 64)
                    wait_full(dve, n)
                    nc.vector.scalar_tensor_tensor(G[:, t, c * COLS:(c + 1) * COLS], ps(n)[:, :],
                                                   rstd[:, N_ATT + t:N_ATT + t + 1], gate_bias[c],
                                                   ALU.mult, ALU.add).then_inc(emptied(n), 1)
            for t in range(T):
                for c in range(2):
                    n = f"ya{c}{t}"
                    wait_full(dve, n)
                    dve.wait_ge(gate_sig, T * c + t + 1)
                    nc.vector.tensor_tensor(MG[:, t, c * COLS:(c + 1) * COLS], ps(n)[:, :],
                                            G[:, t, c * COLS:(c + 1) * COLS], ALU.mult).then_inc(emptied(n), 1)
                for c in range(2):
                    n = f"yb{c}{t}"
                    m = MG[:, t, c * COLS:(c + 1) * COLS]
                    wait_full(dve, n)
                    dve.wait_ge(gate_sig, T * (c + 2) + t + 1)
                    nc.vector.tensor_tensor(rot_a[:, :], ps(n)[:, :], G[:, t, D_MODEL + c * COLS:D_MODEL + (c + 1) * COLS],
                                            ALU.mult).then_inc(emptied(n), 1)
                    dve.wait_ge(*freed_at(n))
                    dve.wait_ge(*freed_at(f"ya{c}{t}"))
                    nc.vector.tensor_tensor(m, m, rot_a[:, :], ALU.add).then_inc(merged, 1)
                    dve.wait_ge(merged, 2 * t + c + 1)
            dve.wait_ge(gain_in, 32)
            for t in range(T):
                for c in range(2):
                    n, cols = f"xo{c}{t}", slice(c * COLS, (c + 1) * COLS)
                    wait_full(dve, n)
                    nc.vector.tensor_tensor(X[:, t, cols], ps(n)[:, :], X[:, t, cols], ALU.add).then_inc(emptied(n), 1)
                    dve.wait_ge(*freed_at(n))
                    nc.vector.tensor_tensor(HN[:, t, cols], X[:, t, cols], gain_ffn[:, cols], ALU.mult)\
                        .then_inc(hf_ready, 1)
            norm_scale(3, 4 * T, (N_FFN, N_FFN + T, D_MODEL))

            dve.wait_ge(router_in, 32)
            nc.vector.memset(LPAD3[:, :, N_EXPERTS:], TAKEN)
            wait_full(dve, "logits")
            for t in range(T):
                ins = nc.vector.scalar_tensor_tensor(LG3[:, t, :], ps("logits")[:, t * N_EXPERTS:(t + 1) * N_EXPERTS],
                                                     rstd[:, N_FFN + t:N_FFN + t + 1], b_rt, ALU.mult, ALU.add)
            ins.then_inc(emptied("logits"), 1)
            dve.wait_ge(*freed_at("logits"))
            for t in range(T):
                ins = nc.vector.max(REP3[:, t, :], LG3[:, t, :])
            step(ins)
            nc.vector.tensor_scalar(nmx.unsqueeze(2), REP3[:, :, 0:1], -1.0, None, ALU.mult).then_inc(logits_in, 1)
            step(nc.vector.memset(REP3[:, :, MOE_TOP_K:8], TAKEN))
            for t in range(T):
                ins = nc.vector.match_replace(LREP3[:, t, :], REP3[:, t, :], LPAD3[:, t, :], MASKED)
            step(ins)
            nc.vector.tensor_tensor(CH3, LREP3[:, :, 0:N_EXPERTS], LG3, ALU.not_equal).then_inc(chosen, 1)
            dve.wait_ge(chosen, 1)
            wait_full(dve, "rank")
            nc.vector.scalar_tensor_tensor(R1, ps("rank")[:, 0:TE], 1.0, CH, ALU.add, ALU.mult)\
                .then_inc(emptied("rank"), 1)
            dve.wait_ge(*freed_at("rank"))

            def te(ap, t, e):
                return ap[:, bass.ds(e + t * N_EXPERTS, 1)]

            def one_hot(item, done):
                for t in range(T):
                    ins = nc.vector.tensor_scalar(GP[:, t, :], const("slot_no"), te(R1, t, item), None, ALU.is_equal)
                ins.then_inc(done, 1)

            one_hot(0, p_ready)
            dve.wait_ge(router_exp, T)
            step(nc.vector.tensor_tensor(GT3, LGE3, CH3, ALU.mult))
            step(nc.vector.tensor_reduce(gs, GT3, AX, ALU.add))
            step(nc.vector.reciprocal(grs, gs))
            for t in range(T):
                ins = nc.vector.tensor_scalar(GT3[:, t, :], GT3[:, t, :], grs[:, t:t + 1], None, ALU.mult)
            step(ins)
            dve.wait_ge(zeroed, 2)
            nc.vector.tensor_copy(PG[:, :, SLOTS:SLOTS + N_EXPERTS], GT3).then_inc(gates_in, 1)
            wait_full(dve, "gT")
            nc.vector.tensor_copy(PGT, ps("gT")[:, :].rearrange("p (h n) -> p h n", h=2)).then_inc(pgT_sb, 1)

            def gated(item, done):
                for t in range(T):
                    ins = nc.vector.tensor_scalar(PG[:, t, SLOTS:2 * SLOTS], const("slot_no"), te(R1, t, item),
                                                  te(GT_, t, item), ALU.is_equal, ALU.mult)
                ins.then_inc(done, 1)

            gated(0, pg_ready)
            wait_full(dve, "count")
            cnt = ps("count")[:, 0:N_EXPERTS]
            step(nc.vector.tensor_scalar(NB, cnt, SLOTS + 0.5, None, ALU.is_gt))
            step(nc.vector.scalar_tensor_tensor(NB, cnt, 2 * SLOTS + 0.5, NB, ALU.is_gt, ALU.add))
            nc.vector.scalar_tensor_tensor(NB, cnt, 3 * SLOTS + 0.5, NB, ALU.is_gt, ALU.add).then_inc(emptied("count"), 1)
            dve.wait_ge(*freed_at("count"))
            step(nc.vector.tensor_tensor_scan(EXTRA_END, const("ones")[:, 0:N_EXPERTS], NB, 0.0, ALU.mult, ALU.add))
            ends = EXTRA_END[0:1, :].unsqueeze(1).to_broadcast([1, EXTRA_COLS, N_EXPERTS])
            items = const("extra_no")[0:1, :].unsqueeze(2).to_broadcast([1, EXTRA_COLS, N_EXPERTS])
            cmp = ET[0:1, :].rearrange("p (i e) -> p i e", e=N_EXPERTS)
            step(nc.vector.tensor_tensor(cmp, ends, items, ALU.is_le))
            nc.vector.tensor_copy(ER[0:1, EXTRA_COLS:EXTRA_COLS + 1], EXTRA_END[0:1, N_EXPERTS - 1:N_EXPERTS])
            step(nc.vector.tensor_reduce(ER[0:1, 0:EXTRA_COLS], cmp, AX, ALU.add))
            step(nc.vector.tensor_scalar(ER[0:1, 0:EXTRA_COLS], ER[0:1, 0:EXTRA_COLS], float(N_EXPERTS - 1), None, ALU.min))
            nc.vector.tensor_copy(table_i[0:1, 0:EXTRA_COLS + 1], ER[0:1, :]).then_inc(table, 1)
            step(nc.vector.tensor_tensor(EXTRA_AT, EXTRA_END, NB, ALU.subtract))
            step(nc.vector.tensor_scalar(EXTRA_AT, EXTRA_AT, float(SLOTS), float(-SLOTS), ALU.mult, ALU.add))
            step(nc.vector.tensor_tensor(DX3, R13, EXTRA_AT.unsqueeze(1).to_broadcast([P, T, N_EXPERTS]), ALU.add))
            step(nc.vector.scalar_tensor_tensor(DX, R1, SLOTS + 0.5, DX, ALU.is_gt, ALU.mult))

            EXTRA_STEPS = 4

            def extra_route(q):
                at = [0]

                def do(ins):
                    at[0] += 1
                    ins.then_inc(extra_step, 1)
                    dve.wait_ge(extra_step, q * EXTRA_STEPS + at[0])

                first = cst[:, bass.ds(q + CONST["extra_base"][0], 1)]
                do(nc.vector.tensor_scalar(IX, DX, first, None, ALU.subtract))
                do(nc.vector.scalar_tensor_tensor(U2, IX, SLOTS + 0.5, IX, ALU.is_lt, ALU.mult))
                nc.vector.tensor_reduce(W1, by_te(U2), AX, ALU.max)
                do(nc.vector.scalar_tensor_tensor(VG, U2, 0.5, GT_, ALU.is_gt, ALU.mult))
                do(nc.vector.tensor_reduce(GW, by_te(VG), AX, ALU.add))
                assert at[0] == EXTRA_STEPS

            def item(i, nxt=None, extra=None):
                if extra is not None:
                    extra_route(extra)
                dve.wait_ge(xg_ps, i + 1)
                if extra is None:
                    one_hot(nxt, p_ready)
                else:
                    for t in range(T):
                        ins = nc.vector.tensor_scalar(GP[:, t, :], const("slot_no"), W1[:, t:t + 1], None, ALU.is_equal)
                    ins.then_inc(p_ready, 1)
                dve.wait_ge(h_done, i + 1)
                nc.vector.tensor_scalar(GC, BG[:, :], SWIGLU_LIMIT, None, ALU.min).then_inc(clipped, 1)
                nc.vector.tensor_scalar(AC, BL[:, :], SWIGLU_LIMIT, -SWIGLU_LIMIT, ALU.min, ALU.max)
                dve.wait_ge(sig, i + 1)
                nc.vector.tensor_tensor(GC, GC, SG, ALU.mult).then_inc(glu_done, 1)
                dve.wait_ge(glu_done, i + 1)
                nc.vector.scalar_tensor_tensor(AC, AC, 1.0, GC, ALU.add, ALU.mult).then_inc(act_ready, 1)
                dve.wait_ge(pgT_ps, i + 1)
                nc.vector.tensor_copy(PGT, BY[:, :].rearrange("p (h n) -> p h n", h=2)).then_inc(pgT_sb, 1)
                if extra is None:
                    gated(nxt, pg_ready)
                else:
                    for t in range(T):
                        ins = nc.vector.tensor_scalar(PG[:, t, SLOTS:2 * SLOTS], const("slot_no"), W1[:, t:t + 1],
                                                      GW[:, t:t + 1], ALU.is_equal, ALU.mult)
                    ins.then_inc(pg_ready, 1)

            with dve.Fori(0, N_EXPERTS - 1) as i:
                item(i, nxt=i + 1)
            item(N_EXPERTS - 1, extra=0)
            over_extra(dve, lambda q: item(q + N_EXPERTS, extra=q + 1), load_n_extra(dve))
            for t in range(T):
                dve.wait_ge(acc_done, t + 1)
                for h in range(2):
                    r = X[:, t, h * COLS:(h + 1) * COLS]
                    nc.vector.tensor_tensor(r, bank[2 * t + h][:, :], r, ALU.add).then_inc(resid_done, 1)
            dve.wait_ge(out_gain_in, 16)
            for t in range(T):
                norm_scale(4 + t, 4 * T + t + 1, (N_OUT + t, N_OUT + t + 1, D_MODEL))
                nc.vector.scalar_tensor_tensor(X[:, t, :], X[:, t, :], rstd[:, N_OUT + t:N_OUT + t + 1], gain_out,
                                               ALU.mult, ALU.mult).then_inc(out_ready, 1)


def constants(np):
    c = {"ident": np.eye(P), "ones": np.ones((P, P)), "zero": np.zeros((P, P))}
    pos = np.arange(SEQ, dtype=np.float32).reshape(T, P, 1)

    def tables(rot, key):
        half = rot // 2
        freq = np.float32(ROPE_THETA) ** (-np.arange(half, dtype=np.float32) / np.float32(half))
        ang = (pos * freq.astype(np.float32)).astype(np.float32)
        cos, sin = np.cos(ang), np.sin(ang)
        c["cos_" + key] = np.concatenate([cos, cos], -1).transpose(1, 0, 2).reshape(P, -1)
        c["sin_" + key] = np.concatenate([-sin, sin], -1).transpose(1, 0, 2).reshape(P, -1)

    tables(HD, "d")
    tables(MLA_ROPE, "m")
    tables(IDX_ROPE, "i")
    q = np.arange(P)[:, None]
    parts = [np.where((np.arange(P * (t + 1))[None] // CHUNK) <= (t * P + q) // CHUNK, 0.0, MASKED) for t in range(T)]
    c["chunk_mask"] = np.concatenate(parts, 1)
    c["before"] = (q < np.arange(P)[None]) * 1.0
    c["slot_no"] = np.tile(np.arange(1, SLOTS + 1), (P, 1))
    c["extra_base"] = np.tile(np.arange(EXTRA_COLS) * SLOTS, (P, 1))
    c["extra_no"] = np.tile(np.arange(EXTRA_COLS), (P, 1))
    c["row_of"] = (q == np.arange(4 * SLOTS)[None] // SLOTS) * 1.0
    return np.ascontiguousarray(np.concatenate([c[n] for n in CONST], 1).astype(np.float32))


_INS = ['x', 'norm_attn_g', 'w_in', 'q_lora_g', 'kv_lora_g', 'w_uq', 'w_uk', 'w_uv', 'w_o_mla', 'w_o_dsa',
        'b_gate', 'w_out', 'norm_ffn_g', 'w_router', 'b_router', 'w_gate_up', 'b_gate_up', 'w_down',
        'b_down', 'norm_final_g']


def kernel(**inputs):
    import numpy as _np
    import concourse.bacc as _bacc
    from concourse import mybir as _mybir
    from concourse.bass_utils import run_bass_kernel_spmd as _run

    nc = _bacc.Bacc("TRN2", target_bir_lowering=False, num_devices=1)
    arrays, args = {}, []
    for name in _INS:
        a = _np.ascontiguousarray(inputs[name])
        arrays[f"in_{name}"] = a
        args.append(nc.dram_tensor(f"in_{name}", a.shape, _mybir.dt.from_np(a.dtype), kind="ExternalInput").ap())
    a = constants(_np)
    arrays["in_consts"] = a
    args.append(nc.dram_tensor("in_consts", a.shape, _mybir.dt.from_np(a.dtype), kind="ExternalInput").ap())
    o = nc.dram_tensor("out_0", (1, SEQ, D_MODEL), _mybir.dt.float32, kind="ExternalOutput").ap()
    hybrid_block_kernel(nc, *args, o)
    return _run(nc, [arrays], core_ids=[0]).results[0]["out_0"]
```

```python
import concourse.bass as bass
from concourse import mybir
from contextlib import ExitStack

D_MODEL = 1024
SEQ = 256
CHUNK = 64
NORM_EPS = 1e-6
ROPE_THETA = 10000.0
HEADS = 8
HD = 128
Q_LORA = 384
KV_LORA = 256
MLA_ROPE = 64
MLA_QK = HD + MLA_ROPE
IDX_HEADS = 8
IDX_DIM = 64
IDX_ROPE = 32
TOP_K = SEQ // 4
N_EXPERTS = 32
MOE_TOP_K = 4
SWIGLU_LIMIT = 7.0
SWIGLU_ALPHA = 1.702

P = 128
T = SEQ // P
KD = D_MODEL // P
COLS = 512
W_LAT = Q_LORA + KV_LORA + MLA_ROPE
W_IDX = IDX_HEADS * IDX_DIM + IDX_DIM + IDX_HEADS
C_QKV = W_LAT
C_IDX = C_QKV + 3 * HEADS * HD
C_GATE = C_IDX + W_IDX
LATC = W_LAT // 2
IDXC = W_IDX // 2

SLOTS = 64
ASSIGNED = SEQ * MOE_TOP_K
MAX_EXTRA = (ASSIGNED - 1) // SLOTS
EXTRA_COLS = 16
assert MAX_EXTRA < EXTRA_COLS

MASKED = -(2.0 ** 100)
TAKEN = -(2.0 ** 127)

RING = 6
RINGW = 4096

CONST = {}
_at = 0
for _name, _w in (("ident", P), ("cos_d", T * HD), ("sin_d", T * HD), ("cos_m", T * MLA_ROPE),
                  ("sin_m", T * MLA_ROPE), ("cos_i", T * IDX_ROPE), ("sin_i", T * IDX_ROPE),
                  ("chunk_mask", 3 * P), ("before", P), ("ones", P), ("slot_no", SLOTS),
                  ("extra_base", EXTRA_COLS), ("extra_no", EXTRA_COLS), ("row_of", 4 * SLOTS)):
    CONST[_name] = (_at, _w)
    _at += _w
CONST_W = _at


def hybrid_block_kernel(nc, x, norm_attn_g, w_in, q_lora_g, kv_lora_g, w_uq, w_uk, w_uv, w_o_mla, w_o_dsa,
                        b_gate, w_out, norm_ffn_g, w_router, b_router, w_gate_up, b_gate_up, w_down,
                        b_down, norm_final_g, consts, out):
    fp32 = mybir.dt.float32
    i32 = mybir.dt.int32
    ALU = mybir.AluOpType
    ACT = mybir.ActivationFunctionType
    AX = mybir.AxisListType.X

    x_v = x.rearrange("b (t p) d -> p (b t) d", p=P)
    out_v = out.rearrange("b (t p) d -> p (b t) d", p=P)
    w_in_v = w_in.rearrange("a (k p) n -> p (a k) n", p=P)
    uq_v = w_uq.rearrange("a (k p) (h c) -> p (a k) h c", p=P, c=MLA_QK)
    uk_v = w_uk.rearrange("a (k p) n -> p (a k) n", p=P)
    uv_v = w_uv.rearrange("a (k p) n -> p (a k) n", p=P)
    oa_v = w_o_mla.rearrange("a (k p) n -> p (a k) n", p=P)
    ob_v = w_o_dsa.rearrange("a (k p) n -> p (a k) n", p=P)
    wo_v = w_out.rearrange("a (k p) n -> p (a k) n", p=P)
    wr_v = w_router.rearrange("a (k p) n -> p (a k) n", p=P)
    gu_v = w_gate_up.rearrange("a e (h p k) n -> (a e) h p k n", h=2, k=4)
    dn_v = w_down.rearrange("a e (h p k) n -> (a e) h p k n", h=2, k=4)
    bgu_v = b_gate_up.rearrange("a e (n c) -> (a e) n c", c=COLS)
    bdn_v = b_down.rearrange("a e n -> (a e) n")

    READER = {"lat0": "lat01", "lat1": "lat11", "idx0": "idx01", "idx1": "idx11", "uqn": "qn3", "uqr": "qr1",
              "ukv": "vm11"}
    READER.update({f"qkv{c}": (f"qk{c}1" if c < 4 else f"v{c - 4}1") for c in range(6)})
    READER.update({f"gate{c}": f"gate{c}1" for c in range(4)})
    READER.update({f"{u}{c}": f"{n}{c}1" for u, n in (("oa", "ya"), ("ob", "yb"), ("wo", "xo")) for c in range(2)})
    UNITS = list(READER)
    DMAS = {"uqn": 3, "uqr": 3, "ukv": 2}
    NU = len(UNITS)
    loaded = [0] * RING
    UNIT = {}
    for n, name in enumerate(UNITS):
        s = n % RING
        loaded[s] += 16 * DMAS.get(name, 1)
        UNIT[name] = (s, loaded[s], UNITS[n - RING] if n >= RING else None)
    LOADS, PLACES, PERIOD = 6, 9, 3
    GU_LOADS = 4
    freed = [(NU + j) % RING for j in range(RING)]
    SPARE_A, SPARE_B, SPARE_C = RING, RING + 1, RING + 2
    ORDER = freed[0:3] + [SPARE_A, SPARE_B] + freed[3:] + [SPARE_C]
    LAST_FRONT = {s: READER[UNITS[NU - RING + j]] for j, s in enumerate(freed)}

    tiles = [f"hT{t}{q}" for t in range(T) for q in range(2)]
    tiles += [f"lat{c}{t}" for c in range(2) for t in range(T)]
    tiles += ["idx00", "idx01", "idx10"] + [f"{n}{t}" for t in range(T) for n in ("cqT", "ckvT")] + ["idx11"]
    tiles += [f"qn{g}" for g in range(4)] + [f"qr{t}" for t in range(T)] + [f"kn{g}" for g in range(4)]
    tiles += [f"vm{c}{t}" for c in range(2) for t in range(T)]
    tiles += [f"qiT{t}" for t in range(T)] + ["kiT"] + [f"qrT{t}" for t in range(T)]
    tiles += [f"raw{t}{g}" for t in range(T) for g in range(4)]
    QK = [(c, t) for c in range(4) for t in range(T)]
    for n in range(len(QK) + 1):
        if n < len(QK):
            tiles.append("qk%d%d" % QK[n])
        if 0 < n < len(QK):
            tiles.append("qkT%d%d" % QK[n - 1])
    NH = 2 * HEADS
    BETWEEN = {1 + 2 * n: ("v", n // T, n % T) for n in range(2 * T)}
    BETWEEN.update({HEADS + 3 + n: ("gate", n // T, n % T) for n in range(4 * T)})
    for s in range(NH + 3):
        tiles += [f"s{s}"] * (s < NH) + ["qkT%d%d" % QK[-1]] * (s == 1)
        tiles += [f"pT{s - 2}"] * (2 <= s < NH + 2) + [f"o{s - 3}"] * (s >= 3)
        if s in BETWEEN:
            tiles.append("%s%d%d" % BETWEEN[s])
    tiles += [f"{n}{c}{t}" for n in ("ya", "yb") for c in range(2) for t in range(T)][:-1]
    tiles += ["mT00", "yb11", "mT01", "xo00", "mT10", "mT11", "xo10", "xo01", "nT00", "nT01", "xo11"]
    tiles += ["logits", "nT10", "nT11", "rank", "count", "gT"]
    NBANK = 8
    ROUTING = {"logits": 7, "nT10": 4, "nT11": 5, "rank": 5, "count": 4, "gT": 5}
    TILE, USES = {}, [0] * NBANK
    for n, name in enumerate(tiles):
        b = ROUTING.get(name, n % NBANK)
        TILE[name] = (b, USES[b])
        USES[b] += 1

    with ExitStack() as ctx:
        def sb(name, cols, parts=P, dt=fp32):
            return ctx.enter_context(nc.sbuf_tensor(name, [parts, cols], dt))

        def sem(name):
            return ctx.enter_context(nc.semaphore(name))

        ring = [sb(f"ring{s}", RINGW) for s in range(RING)]
        cst = sb("cst", CONST_W)
        resid = sb("resid", T * D_MODEL)
        hT_m = sb("hT_m", KD * SEQ)
        mem_q = sb("mem_q", 2048)
        mem_k = sb("mem_k", 2048)
        mem_v = sb("mem_v", 2048)
        mem_qn = sb("mem_qn", 2048)
        mem_qr = sb("mem_qr", 1024)
        mem_kv = sb("mem_kv", 4096)
        mem_lt = sb("mem_lt", 1280)
        roped = sb("roped", 3 * COLS)
        rot_a = sb("rot_a", COLS)
        rot_b = sb("rot_b", COLS)
        att = sb("att", 7 * 3 * P)
        kr_pad = sb("kr_pad", T * 3 * MLA_ROPE)
        ki_pad = sb("ki_pad", T * 3 * IDX_DIM)
        krT = sb("krT", 2 * SEQ)
        score = sb("score", 3 * P)
        sel_mask = sb("sel_mask", 3 * P)
        top8 = sb("top8", 8)
        wi = sb("wi", T * IDX_HEADS)
        ssq, msq, root, rstd = [sb(n, 5 * T) for n in ("ssq", "msq", "root", "rstd")]
        N_ATT, N_LAT, N_FFN, N_OUT = 0, T, 3 * T, 4 * T
        negmax = sb("negmax", T * NH)
        psums = sb("psums", T * NH)
        rsum = sb("rsum", T * NH)
        table_i = sb("table_i", 2 * EXTRA_COLS, 1, i32)

        def const(name, t=None):
            a, w = CONST[name]
            if t is None:
                return cst[:, a:a + w]
            w //= T
            return cst[:, a + t * w:a + (t + 1) * w]

        ident = const("ident")

        X = resid[:, :].rearrange("p (t d) -> p t d", t=T)
        HT = hT_m[:, :].rearrange("p (k n) -> p k n", k=KD)
        H = mem_q[:, :].rearrange("p (t d) -> p t d", t=T)
        QI = mem_q[:, 0:1024].rearrange("p (g n) -> p g n", g=4)
        QT = mem_q[:, :].rearrange("p (h n) -> p h n", h=HEADS)
        IDX = mem_k[:, 0:T * W_IDX].rearrange("p (t d) -> p t d", t=T)
        KI = mem_k[:, 1280:1280 + 2 * SEQ].rearrange("p (e n) -> p e n", e=2)
        KT = mem_k[:, :].rearrange("p (h n) -> p h n", h=HEADS)
        gain_ffn = mem_k[:, 0:D_MODEL]
        gain_out = mem_lt[:, 0:D_MODEL]
        LAT = mem_v[:, 0:T * W_LAT].rearrange("p (t d) -> p t d", t=T)
        VD = mem_v[:, :].rearrange("p (t d) -> p t d", t=T)
        MG = VD
        HN = VD
        QN = mem_qn[:, :].rearrange("p (h n) -> p h n", h=HEADS)
        lora_gain = mem_qr[:, 0:Q_LORA + KV_LORA]
        QR = mem_qr[:, :].rearrange("p (g n) -> p g n", g=4)
        gain_attn = mem_kv[:, 0:D_MODEL]
        KN = mem_kv[:, 0:2048].rearrange("p (h n) -> p h n", h=HEADS)
        VM = mem_kv[:, 2048:4096].rearrange("p (t d) -> p t d", t=T)
        G = mem_kv[:, :].rearrange("p (t d) -> p t d", t=T)
        gate_bias = [mem_qr[:, 0:COLS], mem_qr[:, COLS:2 * COLS], mem_lt[:, 0:COLS], mem_lt[:, COLS:2 * COLS]]
        LT = mem_lt[:, :].rearrange("p (k n) -> p k n", k=5)
        KR = krT[:, :].rearrange("p (e n) -> p e n", e=2)
        S = [att[:, 3 * P * b:3 * P * (b + 1)] for b in range(2)]
        PR = [att[:, 3 * P * (2 + b):3 * P * (3 + b)] for b in range(3)]
        PT = [att[:, 3 * P * (5 + b):3 * P * (6 + b)] for b in range(2)]
        RELU = [att[:, COLS * b:COLS * (b + 1)] for b in range(2)]
        q_rot = [att[:, COLS * (2 + t):COLS * (3 + t)] for t in range(T)]
        w_rt = att[:, 0:KD * N_EXPERTS].rearrange("p (k n) -> p k n", k=KD)
        b_rt = att[:, KD * N_EXPERTS:(KD + 1) * N_EXPERTS]

        XG = att[:, 512:1024]
        XGT = att[:, 1024:1536].rearrange("p (k s) -> p k s", k=4)
        GC = att[:, 1536:2048]
        AC = att[:, 2048:2560]
        junk = att[:, 1536:2560]
        SG = roped[:, 0:512]
        Y_0 = roped[:, 0:512]
        ACT_T = roped[:, 512:1024].rearrange("p (k s) -> p k s", k=4)
        BIAS = [roped[:, 1024:1536], rot_a[:, :], att[:, 0:512]]
        Y = rot_b[:, :]
        PGT = mem_qr[:, 0:512].rearrange("p (h n) -> p h n", h=2)
        GP = mem_qr[:, 512:640].rearrange("p (t s) -> p t s", t=T)
        PG = mem_qr[:, 640:1024].rearrange("p (t s) -> p t s", t=T)
        place = [(r[:, 0:RINGW // 2], r[:, RINGW // 2:RINGW]) for r in ring]
        place += [(mem_kv[:, 0:2048], mem_kv[:, 2048:4096]), (mem_q[:, :], mem_qn[:, :]), (hT_m[:, :], mem_k[:, :])]
        whole = [r[:, :] for r in ring] + [mem_kv[:, :], None, None]

        def by_te(ap):
            return ap.rearrange("p (t e) -> p t e", t=T)

        TE = T * N_EXPERTS
        LGE, CH, GT_, R1, DX, IX, U2, VG = [krT[:, n * TE:(n + 1) * TE] for n in range(8)]
        _r = [0]

        def small(cols):
            _r[0] += cols
            return score[:, _r[0] - cols:_r[0]]

        LPAD, LREP = [small(T * (N_EXPERTS + MOE_TOP_K)) for _ in range(2)]
        REP = small(T * 8)
        nmx, gs, grs, W1, GW = [small(T) for _ in range(5)]
        NB, EXTRA_END, EXTRA_AT = [small(N_EXPERTS) for _ in range(3)]
        assert _r[0] <= 3 * P
        ET = GC
        ER = sel_mask[:, 0:EXTRA_COLS + 1]

        LGE3, CH3, GT3, R13, DX3, LPAD3, LREP3, REP3 = [by_te(a) for a in (LGE, CH, GT_, R1, DX, LPAD, LREP, REP)]
        LG3 = LPAD3[:, :, 0:N_EXPERTS]
        kr_pad3 = kr_pad[:, :].rearrange("p (t d) -> p t d", t=T)
        ki_pad3 = ki_pad[:, :].rearrange("p (t d) -> p t d", t=T)

        bank = [ctx.enter_context(nc.psum_tensor(f"bank{b}", [P, COLS], fp32)) for b in range(NBANK)]
        BG, BL, BY, BM = bank[4], bank[5], bank[6], bank[7]

        def ps(name):
            return bank[TILE[name][0]]

        unit_loaded = [sem(f"unit_loaded{s}") for s in range(RING)]
        load_used = [sem(f"load_used{j}") for j in range(LOADS)]
        psum_full = [sem(f"psum_full{b}") for b in range(NBANK)]
        psum_emptied = [sem(f"psum_emptied{b}") for b in range(NBANK)]
        const_in = sem("const_in")
        ident_in = sem("ident_in")
        x_in = [sem(f"x_in{t}") for t in range(T)]
        gain_in = sem("gain_in")
        lora_in = sem("lora_in")
        gate_bias_in = sem("gate_bias_in")
        router_in = sem("router_in")
        out_gain_in = sem("out_gain_in")
        b_down_in = sem("b_down_in")
        bias_in = [sem(f"bias_in{r}") for r in range(3)]
        squares = sem("squares")
        means = sem("means")
        roots = sem("roots")
        rstd_ready = sem("rstd_ready")
        h_ready = sem("h_ready")
        lat_ready = sem("lat_ready")
        idx_roped = sem("idx_roped")
        kr_roped = sem("kr_roped")
        tok_roped = sem("tok_roped")
        relu_used = sem("relu_used")
        masked = sem("masked")
        exped = sem("exped")
        normed = sem("normed")
        gate_sig = sem("gate_sig")
        merged = sem("merged")
        resid_done = sem("resid_done")
        hf_ready = sem("hf_ready")
        hn_ready = sem("hn_ready")
        logits_in = sem("logits_in")
        router_exp = sem("router_exp")
        chosen = sem("chosen")
        table = sem("table")
        gates_in = sem("gates_in")
        pads_zero = sem("pads_zero")
        zeroed = sem("zeroed")
        dve_step = sem("dve_step")
        p_ready = sem("p_ready")
        pg_ready = sem("pg_ready")
        xg_ps = sem("xg_ps")
        xg_sb = sem("xg_sb")
        xgT_ps = sem("xgT_ps")
        xgT_sb = sem("xgT_sb")
        bias_used = sem("bias_used")
        h_done = sem("h_done")
        clipped = sem("clipped")
        sig = sem("sig")
        act_ready = sem("act_ready")
        actT_ps = sem("actT_ps")
        actT_sb = sem("actT_sb")
        y_ps = sem("y_ps")
        y_sb = sem("y_sb")
        pgT_ps = sem("pgT_ps")
        pgT_sb = sem("pgT_sb")
        acc_done = sem("acc_done")
        place_loaded = unit_loaded + [sem(f"spare_loaded{j}") for j in range(PLACES - RING)]
        glu_done = sem("glu_done")
        extra_step = sem("extra_step")
        out_ready = sem("out_ready")
        stored = sem("stored")

        block = ctx.enter_context(nc.Block())

        def wait_full(eng, name):
            b, n = TILE[name]
            eng.wait_ge(psum_full[b], n + 1)

        def wait_sb(eng, name):
            b, n = TILE[name]
            eng.wait_ge(psum_emptied[b], n + 1)

        def emptied(name):
            return psum_emptied[TILE[name][0]]

        def full(name):
            return psum_full[TILE[name][0]]

        def loads_landed(m, r, j):
            n = LOADS * r + j
            s = ORDER[n % PLACES]
            each = 16 if whole[s] is not None else 32
            before = loaded[s] if s < RING else 0
            return s, before + each * (n // PLACES + 1) + each * 2 * m

        def over_extra(eng, prepare, item, n_extra):
            with eng.If(n_extra > 0):
                prepare()
                with eng.Fori(0, MAX_EXTRA) as q:
                    with eng.If(q < n_extra):
                        item(q)

        def over_extra_by_period(eng, prepare, item, n_extra):
            m0, r0 = divmod(N_EXPERTS, PERIOD)
            with eng.If(n_extra > 0):
                prepare()
                with eng.Fori(0, MAX_EXTRA // PERIOD) as g:
                    for k in range(PERIOD):
                        dm, r = divmod(r0 + k, PERIOD)
                        with eng.If(g * PERIOD + k < n_extra):
                            item(g + (m0 + dm), r, g * PERIOD + k)

        def load_n_extra(eng):
            eng.wait_ge(table, 1)
            return eng.value_load(table_i[0:1, EXTRA_COLS:EXTRA_COLS + 1], min_val=0, max_val=MAX_EXTRA)

        def row(v):
            return v.rearrange("a n -> (a n)").partition_broadcast(P)

        def tok(t):
            return slice(t * P, (t + 1) * P)

        @block.sync
        def _(sp):
            def load(name, parts):
                slot, _, before = UNIT[name]
                if before:
                    wait_full(sp, READER[before])
                for dst, src in parts(ring[slot]):
                    sp.dma_start(dst, src).then_inc(unit_loaded[slot], 16)

            def cols(view, a, n, k):
                return lambda r: [(r[:, 0:k * n].rearrange("p (k n) -> p k n", k=k), view[:, :, a:a + n])]

            for t in range(T):
                sp.dma_start(X[:, t, :], x_v[:, t, :]).then_inc(x_in[t], 16)
            for c in range(2):
                load(f"lat{c}", cols(w_in_v, c * LATC, LATC, KD))
            for c in range(2):
                load(f"idx{c}", cols(w_in_v, C_IDX + c * IDXC, IDXC, KD))
            load("uqn", lambda r: [(r[:, k * 1024:(k + 1) * 1024].rearrange("p (h c) -> p h c", c=HD),
                                    uq_v[:, k, :, 0:HD]) for k in range(3)])
            load("uqr", lambda r: [(r[:, k * 512:(k + 1) * 512].rearrange("p (h c) -> p h c", c=MLA_ROPE),
                                    uq_v[:, k, :, HD:MLA_QK]) for k in range(3)])
            load("ukv", lambda r: [(r[:, v * 2048:(v + 1) * 2048].rearrange("p (k n) -> p k n", k=2), w)
                                   for v, w in enumerate((uk_v, uv_v))])
            for c in range(6):
                load(f"qkv{c}", cols(w_in_v, C_QKV + c * COLS, COLS, KD))
            for c in range(4):
                load(f"gate{c}", cols(w_in_v, C_GATE + c * COLS, COLS, KD))
            for n, v in (("oa", oa_v), ("ob", ob_v), ("wo", wo_v)):
                for c in range(2):
                    load(f"{n}{c}", cols(v, c * COLS, COLS, KD))

            def item_load(r, j, e):
                s = ORDER[(LOADS * r + j) % PLACES]
                if j < GU_LOADS:
                    src, k = gu_v[e, j // 2, :, 2 * (j % 2):2 * (j % 2) + 2, :], 2
                else:
                    src, k = dn_v[e, j - GU_LOADS, :, :, :], 4
                src = src.rearrange("e p k n -> p (e k) n")
                if whole[s] is not None:
                    sp.dma_start(whole[s].rearrange("p (k n) -> p k n", k=k), src).then_inc(place_loaded[s], 16)
                else:
                    for h in range(2):
                        sp.dma_start(place[s][h].rearrange("p (k n) -> p k n", k=k // 2),
                                     src[:, h * k // 2:(h + 1) * k // 2, :]).then_inc(place_loaded[s], 16)

            def bias_load(r, e):
                sp.dma_start(BIAS[r][0:4, :], bgu_v[e, :, :].rearrange("e n c -> (e n) c")).then_inc(bias_in[r], 16)

            for n in range(PLACES):
                if ORDER[n] < RING:
                    wait_full(sp, LAST_FRONT[ORDER[n]])
                elif ORDER[n] == SPARE_C:
                    wait_full(sp, "logits")
                    sp.wait_ge(hf_ready, 2 * T)
                else:
                    wait_sb(sp, f"yb1{T - 1}")
                if n == LOADS:
                    sp.wait_ge(zeroed, 3)
                    bias_load(0, slice(0, 1))
                i, j = divmod(n, LOADS)
                item_load(i, j, slice(i, i + 1))

            def item(i, r, e, first=0):
                for j in range(first, LOADS):
                    if j == 3:
                        if isinstance(i, int) and i < PERIOD:
                            sp.wait_ge(zeroed, i + 3)
                        else:
                            sp.wait_ge(bias_used, i - 2)
                        bias_load(r, e)
                    if j == 0:
                        sp.wait_ge(h_done, i - 1)
                    elif j == 1:
                        sp.wait_ge(load_used[4], i - 1)
                    elif j == 2:
                        sp.wait_ge(y_ps, i - 1)
                    else:
                        sp.wait_ge(load_used[j - 3], i)
                    item_load(r, j, e)

            item(1, 1, slice(1, 2), 3)
            item(2, 2, slice(2, 3))
            with sp.Fori(1, N_EXPERTS // PERIOD) as m:
                for r in range(PERIOD):
                    item(m * PERIOD + r, r, bass.ds(m * PERIOD + r, 1))
            for i in range(N_EXPERTS - N_EXPERTS % PERIOD, N_EXPERTS):
                item(i, i % PERIOD, slice(i, i + 1))

            def extra(m, r, q):
                e = sp.value_load(table_i[0:1, bass.ds(q, 1)], min_val=0, max_val=N_EXPERTS - 1)
                item(q + N_EXPERTS, r, bass.ds(e, 1))

            over_extra_by_period(sp, lambda: None, extra, load_n_extra(sp))
            for t in range(T):
                sp.wait_ge(out_ready, t + 1)
                sp.dma_start(out_v[:, t, :], X[:, t, :]).then_inc(stored, 16)
            sp.wait_ge(stored, 16 * T)

        @block.gpsimd
        def _(pool):
            nc.gpsimd.memset(kr_pad[:, :], 0.0).then_inc(pads_zero, 1)
            nc.gpsimd.memset(ki_pad[:, :], 0.0).then_inc(pads_zero, 1)
            wait_sb(pool, f"yb1{T - 1}")
            nc.gpsimd.memset(BIAS[0], 0.0).then_inc(zeroed, 1)
            nc.gpsimd.memset(PG[:, :, :], 0.0).then_inc(zeroed, 1)
            nc.gpsimd.memset(Y_0, 0.0).then_inc(zeroed, 1)
            pool.wait_ge(zeroed, 3)
            for h in range(2):
                pool.dma_start(Y_0[SLOTS * h:SLOTS * h + N_EXPERTS, :], bdn_v[:, h * COLS:(h + 1) * COLS])\
                    .then_inc(b_down_in, 16)
            pool.wait_ge(merged, 2 * T)
            nc.gpsimd.memset(BIAS[1], 0.0).then_inc(zeroed, 1)
            wait_sb(pool, "logits")
            nc.gpsimd.memset(BIAS[2], 0.0).then_inc(zeroed, 1)
            pool.wait_ge(b_down_in, 32)

        @block.scalar
        def _(act):
            act.dma_start(gain_attn, row(norm_attn_g)).then_inc(gain_in, 16)
            act.dma_start(cst[:, 0:P], consts[:, 0:P]).then_inc(ident_in, 16)
            act.dma_start(cst[:, P:CONST_W], consts[:, P:CONST_W]).then_inc(const_in, 16)
            act.dma_start(lora_gain[:, 0:Q_LORA], row(q_lora_g)).then_inc(lora_in, 16)
            act.dma_start(lora_gain[:, Q_LORA:Q_LORA + KV_LORA], row(kv_lora_g)).then_inc(lora_in, 16)

            n_squares = [0]

            def square(dst, src, junk):
                if n_squares[0]:
                    act.wait_ge(squares, n_squares[0])
                nc.scalar.activation(junk, src, ACT.Square, accum_out=dst).then_inc(squares, 1)
                n_squares[0] += 1

            def roots_of(n, a, b):
                act.wait_ge(means, n)
                nc.scalar.activation(root[:, a:b], msq[:, a:b], ACT.Sqrt).then_inc(roots, 1)

            def evacuate(name, dst, src, scale=None):
                wait_full(act, name)
                if scale is None:
                    ins = nc.scalar.activation(dst, src, ACT.Copy)
                else:
                    ins = nc.scalar.activation(dst, src, ACT.Identity, scale=scale)
                ins.then_inc(emptied(name), 1)

            def blocks(name, k=4):
                return ps(name)[:, 0:k * P].rearrange("p (k n) -> p k n", k=k)

            for t in range(T):
                act.wait_ge(x_in[t], 16)
                square(ssq[:, N_ATT + t:N_ATT + t + 1], X[:, t, :], VM[:, 0, :])
                for q in range(2):
                    evacuate(f"hT{t}{q}", HT[:, 4 * q:4 * q + 4, tok(t)], blocks(f"hT{t}{q}"))
            roots_of(1, N_ATT, N_ATT + T)
            act.wait_ge(rstd_ready, 1)

            def att_scale(t):
                return rstd[:, N_ATT + t:N_ATT + t + 1]

            for c in range(2):
                for t in range(T):
                    evacuate(f"lat{c}{t}", LAT[:, t, c * LATC:(c + 1) * LATC], ps(f"lat{c}{t}")[:, 0:LATC], att_scale(t))
            wait_sb(act, f"lat1{T - 1}")
            for t in range(T):
                a = N_LAT + t
                square(ssq[:, a:a + 1], LAT[:, t, 0:Q_LORA], att[:, 0:Q_LORA])
                square(ssq[:, a + T:a + T + 1], LAT[:, t, Q_LORA:Q_LORA + KV_LORA], att[:, 0:KV_LORA])
            roots_of(2, N_LAT, N_LAT + 2 * T)
            def indexer(c, t):
                evacuate(f"idx{c}{t}", IDX[:, t, c * IDXC:(c + 1) * IDXC], ps(f"idx{c}{t}")[:, 0:IDXC], att_scale(t))

            for c, t in ((0, 0), (0, 1), (1, 0)):
                indexer(c, t)
            for t in range(T):
                evacuate(f"cqT{t}", LT[:, 0:3, tok(t)], blocks(f"cqT{t}", 3))
                n = f"ckvT{t}"
                wait_full(act, n)
                nc.scalar.activation(LT[:, 3:5, tok(t)], blocks(n)[:, 0:2, :], ACT.Copy)
                nc.scalar.activation(KR[:, :, tok(t)], blocks(n)[:, 2:4, :], ACT.Copy).then_inc(emptied(n), 1)
            indexer(1, 1)
            for g in range(4):
                evacuate(f"qn{g}", QN[:, 2 * g:2 * g + 2, :], ps(f"qn{g}")[:, :].rearrange("p (h n) -> p h n", h=2))
            for g in range(4):
                evacuate(f"kn{g}", KN[:, 2 * g:2 * g + 2, :], ps(f"kn{g}")[:, :].rearrange("p (h n) -> p h n", h=2))
            for c in range(2):
                for t in range(T):
                    evacuate(f"vm{c}{t}", VM[:, t, c * COLS:(c + 1) * COLS], ps(f"vm{c}{t}")[:, :])
            for t in range(T):
                evacuate(f"qiT{t}", QI[:, :, tok(t)], blocks(f"qiT{t}"))
            evacuate("kiT", KI[:, :, :].rearrange("p e (t n) -> p e t n", t=T),
                     ps("kiT")[:, :].rearrange("p (t e n) -> p e t n", t=T, e=2))
            for t in range(T):
                evacuate(f"qrT{t}", QR[:, :, tok(t)], blocks(f"qrT{t}"))
            for t in range(T):
                for g in range(4):
                    n, keys, u = f"raw{t}{g}", P * (t + 1), 4 * t + g
                    if u >= 2:
                        act.wait_ge(relu_used, u - 1)
                    wait_full(act, n)
                    nc.scalar.activation(RELU[u % 2][:, 0:2 * keys], ps(n)[:, 0:2 * keys], ACT.Relu,
                                         scale=IDX_DIM ** -0.5).then_inc(emptied(n), 1)
            for c, t in QK:
                evacuate(f"qkT{c}{t}", (QT, KT)[c // 2][:, 4 * (c % 2):4 * (c % 2) + 4, tok(t)], blocks(f"qkT{c}{t}"))
            for s in range(NH + 2):
                if s < NH:
                    act.wait_ge(masked, s + 1)
                    for t in range(T):
                        a, w, col = t * P, P * (t + 1), s * T + t
                        nc.scalar.activation(PR[s % 3][:, a:a + w], S[s % 2][:, a:a + w], ACT.Exp,
                                             bias=negmax[:, col:col + 1],
                                             accum_out=psums[:, col:col + 1]).then_inc(exped, 1)
                if s >= 2:
                    evacuate(f"pT{s - 2}", PT[s % 2], ps(f"pT{s - 2}")[:, 0:3 * P])
                if BETWEEN.get(s - 1, " ")[0] == "v":
                    _, c, t = BETWEEN[s - 1]
                    evacuate(f"v{c}{t}", VD[:, t, c * COLS:(c + 1) * COLS], ps(f"v{c}{t}")[:, :], att_scale(t))
                if s == HEADS + 2:
                    for c in range(4):
                        act.dma_start(gate_bias[c], b_gate[0, c * COLS:(c + 1) * COLS].partition_broadcast(P))\
                            .then_inc(gate_bias_in, 16)
            act.dma_start(gain_ffn, row(norm_ffn_g)).then_inc(gain_in, 16)
            act.dma_start(w_rt, wr_v).then_inc(router_in, 16)
            act.dma_start(b_rt, row(b_router)).then_inc(router_in, 16)
            for c in range(4):
                for t in range(T):
                    wait_sb(act, f"gate{c}{t}")
                    g = G[:, t, c * COLS:(c + 1) * COLS]
                    nc.scalar.activation(g, g, ACT.Sigmoid).then_inc(gate_sig, 1)
            act.dma_start(gain_out, norm_final_g.partition_broadcast(P)).then_inc(out_gain_in, 16)
            for t in range(T):
                for q in range(2):
                    evacuate(f"mT{t}{q}", HT[:, 4 * q:4 * q + 4, tok(t)], blocks(f"mT{t}{q}"))
            for t in range(T):
                for c in range(2):
                    wait_sb(act, f"xo{c}{t}")
                square(ssq[:, N_FFN + t:N_FFN + t + 1], X[:, t, :], junk)
                for q in range(2):
                    evacuate(f"nT{t}{q}", HT[:, 4 * q:4 * q + 4, tok(t)], blocks(f"nT{t}{q}"))
            roots_of(3, N_FFN, N_FFN + T)
            act.wait_ge(rstd_ready, 3)
            for t in range(T):
                nc.scalar.activation(HN[:, t, :], HN[:, t, :], ACT.Identity,
                                     scale=rstd[:, N_FFN + t:N_FFN + t + 1]).then_inc(hn_ready, 1)
            act.wait_ge(b_down_in, 32)
            nc.scalar.activation(Y, Y_0, ACT.Copy).then_inc(y_sb, 1)
            act.wait_ge(logits_in, 1)
            for t in range(T):
                nc.scalar.activation(LGE3[:, t, :], LG3[:, t, :], ACT.Exp, bias=nmx[:, t:t + 1]).then_inc(router_exp, 1)

            def gathered(item):
                act.wait_ge(xg_ps, item + 1)
                nc.scalar.activation(XG, BM[:, :], ACT.Copy).then_inc(xg_sb, 1)
                act.wait_ge(xgT_ps, item + 1)
                nc.scalar.activation(XGT, BY[:, :].rearrange("p (k s) -> p k s", k=4), ACT.Copy).then_inc(xgT_sb, 1)

            gathered(0)

            def item(i, last=False):
                act.wait_ge(clipped, i + 1)
                nc.scalar.activation(SG, GC, ACT.Sigmoid, scale=SWIGLU_ALPHA).then_inc(sig, 1)
                if not last:
                    gathered(i + 1)
                act.wait_ge(actT_ps, i + 1)
                nc.scalar.activation(ACT_T, BM[:, :].rearrange("p (k s) -> p k s", k=4), ACT.Copy).then_inc(actT_sb, 1)
                act.wait_ge(y_ps, i + 1)
                nc.scalar.activation(Y, BY[:, :], ACT.Copy).then_inc(y_sb, 1)

            with act.Fori(0, N_EXPERTS - 1) as i:
                item(i)
            item(N_EXPERTS - 1, last=True)
            over_extra(act, lambda: gathered(N_EXPERTS), lambda q: item(q + N_EXPERTS), load_n_extra(act))
            nc.scalar.activation(root[:, N_ATT:N_ATT + 1], const("ones")[:, 0:1], ACT.Sqrt)
            for t in range(T):
                act.wait_ge(resid_done, 2 * t + 2)
                square(ssq[:, N_OUT + t:N_OUT + t + 1], X[:, t, :], junk)
                roots_of(4 + t, N_OUT + t, N_OUT + t + 1)

        @block.tensor
        def _(pe):
            def claim(name):
                b, n = TILE[name]
                if n:
                    pe.wait_ge(psum_emptied[b], n)
                return bank[b]

            def arrived(name):
                pe.wait_ge(unit_loaded[UNIT[name][0]], UNIT[name][1])
                return ring[UNIT[name][0]]

            def transposes(name, sources):
                o = claim(name)
                for n, src in enumerate(sources):
                    last = nc.tensor.transpose(o[:, n * P:(n + 1) * P], src, ident)
                last.then_inc(full(name), 1)

            def product(o, lhs, rhs, kk):
                for k in range(kk):
                    last = nc.tensor.matmul(o, lhs(k), rhs(k), start=(k == 0), stop=(k == kk - 1))
                return last

            def one(name, unit, c, t, a, width=COLS, ks=range(KD), k_waits={}):
                w = arrived(unit)[:, 0:KD * width].rearrange("p (k n) -> p k n", k=KD)
                tile = f"{name}{c}{t}"
                o = claim(tile) if ks[0] == 0 else bank[TILE[tile][0]]
                for k in ks:
                    if k in k_waits:
                        wait_sb(pe, k_waits[k])
                    last = nc.tensor.matmul(o[:, 0:width], a[:, k, tok(t)], w[:, k, :], start=(k == 0), stop=(k == KD - 1))
                if ks[-1] == KD - 1:
                    last.then_inc(full(tile), 1)

            def turned(name, a, t, halves=range(2)):
                for q in halves:
                    transposes(f"{name}{t}{q}", [a[:, t, (4 * q + b) * P:(4 * q + b + 1) * P] for b in range(4)])

            def turned_in(name, t):
                for q in range(2):
                    wait_sb(pe, f"{name}{t}{q}")

            pe.wait_ge(ident_in, 16)
            for t in range(T):
                pe.wait_ge(h_ready, t + 1)
                turned("hT", H, t)
            for c in range(2):
                for t in range(T):
                    if c == 0:
                        turned_in("hT", t)
                    one("lat", f"lat{c}", c, t, HT, LATC)
            for c, t in ((0, 0), (0, 1), (1, 0)):
                one("idx", f"idx{c}", c, t, HT, IDXC)
            pe.wait_ge(lat_ready, 2 * T)
            pe.wait_ge(kr_roped, T)
            for t in range(T):
                transposes(f"cqT{t}", [LAT[:, t, k * P:(k + 1) * P] for k in range(3)])
                transposes(f"ckvT{t}", [LAT[:, t, Q_LORA + k * P:Q_LORA + (k + 1) * P] for k in range(2)]
                           + [kr_pad3[:, t, MLA_ROPE:3 * MLA_ROPE], kr_pad3[:, t, 0:2 * MLA_ROPE]])
            one("idx", "idx1", 1, 1, HT, IDXC)
            for t in range(T):
                wait_sb(pe, f"cqT{t}")
                wait_sb(pe, f"ckvT{t}")
            w = arrived("uqn")[:, 0:3 * 1024].rearrange("p (k n) -> p k n", k=3)
            for g in range(4):
                o = claim(f"qn{g}")
                for h in range(2):
                    last = product(o[:, h * SEQ:(h + 1) * SEQ], lambda k: w[:, k, (2 * g + h) * HD:(2 * g + h + 1) * HD],
                                   lambda k: LT[:, k, :], 3)
                last.then_inc(full(f"qn{g}"), 1)
            wr = arrived("uqr")[:, 0:3 * 512].rearrange("p (k n) -> p k n", k=3)
            for t in range(T):
                o = claim(f"qr{t}")
                product(o[:, :], lambda k: LT[:, k, tok(t)], lambda k: wr[:, k, :], 3).then_inc(full(f"qr{t}"), 1)
            wkv = arrived("ukv")[:, :].rearrange("p (v k n) -> p v k n", v=2, k=2)
            for g in range(4):
                o = claim(f"kn{g}")
                for h in range(2):
                    last = product(o[:, h * SEQ:(h + 1) * SEQ],
                                   lambda k: wkv[:, 0, k, (2 * g + h) * HD:(2 * g + h + 1) * HD],
                                   lambda k: LT[:, 3 + k, :], 2)
                last.then_inc(full(f"kn{g}"), 1)
            for c in range(2):
                for t in range(T):
                    o = claim(f"vm{c}{t}")
                    product(o[:, :], lambda k: LT[:, 3 + k, tok(t)], lambda k: wkv[:, 1, k, c * COLS:(c + 1) * COLS], 2)\
                        .then_inc(full(f"vm{c}{t}"), 1)
            for t in range(T):
                pe.wait_ge(idx_roped, t + 1)
                transposes(f"qiT{t}", [roped[:, t * COLS + g * P:t * COLS + (g + 1) * P] for g in range(4)])
            transposes("kiT", [ki_pad3[:, t, a:a + P] for t in range(T) for a in (IDX_DIM, 0)])
            for t in range(T):
                pe.wait_ge(tok_roped, t + 1)
                transposes(f"qrT{t}", [q_rot[t][:, g * P:(g + 1) * P] for g in range(4)])
            wait_sb(pe, "kiT")
            for t in range(T):
                keys = P * (t + 1)
                for g in range(4):
                    o = claim(f"raw{t}{g}")
                    for e in range(2):
                        last = nc.tensor.matmul(o[:, e * keys:(e + 1) * keys], QI[:, g, tok(t)], KI[:, e, 0:keys],
                                                start=True, stop=True)
                    last.then_inc(full(f"raw{t}{g}"), 1)
            def qk_turned(n):
                pe.wait_ge(tok_roped, T + n + 1)
                a = COLS * ((n + 2) % 3)
                transposes("qkT%d%d" % QK[n], [roped[:, a + g * P:a + (g + 1) * P] for g in range(4)])

            for n, (c, t) in enumerate(QK):
                w = arrived(f"qkv{c}")[:, :].rearrange("p (k n) -> p k n", k=KD)
                o = claim(f"qk{c}{t}")
                product(o[:, :], lambda k: HT[:, k, tok(t)], lambda k: w[:, k, :], KD).then_inc(full(f"qk{c}{t}"), 1)
                if n:
                    qk_turned(n - 1)
            wait_sb(pe, "qkT%d%d" % QK[-2])

            for s in range(NH + 3):
                if s == HEADS:
                    wait_sb(pe, "qkT%d%d" % QK[-1])
                if s < NH:
                    h = s % HEADS
                    o = claim(f"s{s}")
                    for t in range(T):
                        w = P * (t + 1)
                        ot = o[:, t * P:t * P + w]
                        if s < HEADS:
                            nc.tensor.matmul(ot, QN[:, h, tok(t)], KN[:, h, 0:w], start=True, stop=False)
                            last = nc.tensor.matmul(ot, QR[:, h // 2, tok(t)], KR[:, h % 2, 0:w], start=False, stop=True)
                        else:
                            last = nc.tensor.matmul(ot, QT[:, h, tok(t)], KT[:, h, 0:w], start=True, stop=True)
                    last.then_inc(full(f"s{s}"), 1)
                if s == 1:
                    qk_turned(len(QK) - 1)
                if 2 <= s < NH + 2:
                    pe.wait_ge(normed, s - 1)
                    transposes(f"pT{s - 2}", [PR[(s - 2) % 3][:, a * P:(a + 1) * P] for a in range(3)])
                if s >= 3:
                    h = (s - 3) % HEADS
                    v = (VM if s - 3 < HEADS else VD)
                    if s - 3 == HEADS:
                        wait_sb(pe, "v11")
                    pt = PT[(s - 3) % 2]
                    o = claim(f"o{s - 3}")
                    wait_sb(pe, f"pT{s - 3}")
                    nc.tensor.matmul(o[:, 0:SEQ], v[:, 0, h * HD:(h + 1) * HD], pt[:, 0:SEQ], start=True, stop=False)
                    nc.tensor.matmul(o[:, P:SEQ], v[:, 1, h * HD:(h + 1) * HD], pt[:, SEQ:3 * P],
                                     start=False, stop=True).then_inc(full(f"o{s - 3}"), 1)
                for begun in (s, s - 1):
                    kind, c, t = BETWEEN.get(begun, (None, 0, 0))
                    if kind == "v":
                        half = s - begun
                        one("v", f"qkv{4 + c}", c, t, HT, ks=range(4 * half, 4 * half + 4))
                    elif kind == "gate" and begun == s:
                        one("gate", f"gate{c}", c, t, HT)
            for h in range(NH):
                wait_sb(pe, f"o{h}")
            for name, unit, a in (("ya", "oa", QN), ("yb", "ob", QT)):
                for c in range(2):
                    for t in range(T):
                        if (name, c, t) == ("yb", 1, 1):
                            pe.wait_ge(merged, 1)
                            turned("mT", MG, 0, [0])
                        one(name, f"{unit}{c}", c, t, a)
            pe.wait_ge(merged, T + 1)
            turned("mT", MG, 0, [1])
            for t in range(T):
                if t:
                    turned_in("mT", t)
                for c in range(2):
                    if (t, c) == (0, 1):
                        pe.wait_ge(merged, 2 * T)
                        turned("mT", MG, 1)
                    elif (t, c) == (1, 1):
                        pe.wait_ge(hf_ready, 2)
                        turned("nT", HN, 0)
                    one("xo", f"wo{c}", c, t, HT, k_waits={0: "mT00", 4: "mT01"} if (t, c) == (0, 0) else {})
            turned_in("nT", 0)
            pe.wait_ge(router_in, 32)
            o = claim("logits")
            for t in range(T):
                for k in range(KD):
                    if (t, k) == (0, 4):
                        pe.wait_ge(hf_ready, 2 * T)
                        turned("nT", HN, 1)
                    elif (t, k) == (1, 0):
                        turned_in("nT", 1)
                    last = nc.tensor.matmul(o[:, t * N_EXPERTS:(t + 1) * N_EXPERTS], HT[:, k, tok(t)], w_rt[:, k, :],
                                            start=(k == 0), stop=(k == KD - 1))
            last.then_inc(full("logits"), 1)
            pe.wait_ge(chosen, 1)
            o = claim("rank")
            for t in range(T):
                ot = o[:, t * N_EXPERTS:(t + 1) * N_EXPERTS]
                for b in range(t + 1):
                    last = nc.tensor.matmul(ot, const("ones") if b < t else const("before"), CH3[:, b, :],
                                            start=(b == 0), stop=(b == t))
            last.then_inc(full("rank"), 1)
            o = claim("count")
            product(o[:, 0:N_EXPERTS], lambda b: const("ones"), lambda b: CH3[:, b, :], T).then_inc(full("count"), 1)

            def gates_turned(o):
                for h in range(2):
                    for t in range(T):
                        a = SLOTS * (1 - h)
                        last = nc.tensor.transpose(o[:, (T * h + t) * P:(T * h + t + 1) * P], PG[:, t, a:a + P], ident)
                return last

            def gather(item):
                pe.wait_ge(p_ready, item + 1)
                for t in range(T):
                    for h in range(2):
                        last = nc.tensor.matmul(BM[SLOTS * h:SLOTS * (h + 1), :], GP[:, t, :],
                                                HN[:, t, h * COLS:(h + 1) * COLS], start=(t == 0), stop=(t == T - 1))
                last.then_inc(xg_ps, 1)

            def turn_rows(item):
                pe.wait_ge(xg_sb, item + 1)
                if not (isinstance(item, int) and item == 0):
                    pe.wait_ge(pgT_sb, item + 1)
                rows = XG.rearrange("p (c k) -> p k c", k=4)
                for k in range(4):
                    last = nc.tensor.transpose(BY[:, k * P:(k + 1) * P], rows[:, k, :], ident)
                last.then_inc(xgT_ps, 1)

            def scatter(start=False, stop=False):
                for t in range(T):
                    for h in range(2):
                        ins = nc.tensor.matmul(bank[2 * t + h][:, :], PGT[:, h, tok(t)], Y, start=start, stop=stop)
                        if stop:
                            ins.then_inc(acc_done, 1)

            wait_sb(pe, "logits")
            pe.wait_ge(hn_ready, T)
            gather(0)
            pe.wait_ge(gates_in, 1)
            gates_turned(claim("gT")).then_inc(full("gT"), 1)
            turn_rows(0)
            for b in range(5):
                pe.wait_ge(psum_emptied[b], USES[b])
            pe.wait_ge(pgT_sb, 1)

            def scatter_previous(i):
                pe.wait_ge(y_sb, i + 1)
                pe.wait_ge(pgT_sb, i + 1)
                scatter(start=isinstance(i, int) and i == 0)
                pe.wait_ge(pg_ready, i + 1)
                gates_turned(BY).then_inc(pgT_ps, 1)

            def item(m, r, last=False):
                i = m * PERIOD + r

                def landed(j):
                    s, value = loads_landed(m, r, j)
                    pe.wait_ge(place_loaded[s], value)
                    return place[s]

                pe.wait_ge(xgT_sb, i + 1)
                for j in range(GU_LOADS):
                    if j == GU_LOADS - 1:
                        pe.wait_ge(bias_in[r], m * 16 + 16)
                        for n in range(4):
                            ins = nc.tensor.matmul((BG, BL)[n // 2][SLOTS * (n % 2):SLOTS * (n % 2 + 1), :],
                                                   const("row_of")[:, n * SLOTS:(n + 1) * SLOTS], BIAS[r],
                                                   start=False, stop=False)
                        ins.then_inc(bias_used, 1)
                    w = landed(j)
                    for k in range(2):
                        lhs = XGT[:, 2 * (j % 2) + k, SLOTS * (j // 2):SLOTS * (j // 2 + 1)]
                        for n in range(4):
                            ins = nc.tensor.matmul((BG, BL)[n // 2][SLOTS * (n % 2):SLOTS * (n % 2 + 1), :], lhs,
                                                   w[k][:, n * COLS:(n + 1) * COLS], start=(j == 0 and k == 0),
                                                   stop=(j == GU_LOADS - 1 and k == 1))
                    ins.then_inc(load_used[j] if j < GU_LOADS - 1 else h_done, 1)
                scatter_previous(i)
                if not last:
                    gather(i + 1)
                    turn_rows(i + 1)
                pe.wait_ge(act_ready, i + 1)
                rows = AC.rearrange("p (c k) -> p k c", k=4)
                for k in range(4):
                    ins = nc.tensor.transpose(BM[:, k * P:(k + 1) * P], rows[:, k, :], ident)
                ins.then_inc(actT_ps, 1)
                pe.wait_ge(actT_sb, i + 1)
                if last:
                    pe.wait_ge(pgT_sb, i + 2)
                else:
                    pe.wait_ge(xgT_sb, i + 2)
                for h in range(2):
                    w = landed(GU_LOADS + h)
                    for k in range(4):
                        for n in range(2):
                            a = (k % 2) * D_MODEL + n * COLS
                            ins = nc.tensor.matmul(BY[SLOTS * n:SLOTS * (n + 1), :],
                                                    ACT_T[:, k, SLOTS * h:SLOTS * (h + 1)], w[k // 2][:, a:a + COLS],
                                                    start=(h == 0 and k == 0), stop=(h == 1 and k == 3))
                    ins.then_inc(load_used[GU_LOADS] if h == 0 else y_ps, 1)

            for r in range(PERIOD):
                item(0, r)
            with pe.Fori(1, N_EXPERTS // PERIOD) as m:
                for r in range(PERIOD):
                    item(m, r)
            for i in range(N_EXPERTS - N_EXPERTS % PERIOD, N_EXPERTS):
                item(i // PERIOD, i % PERIOD, last=(i == N_EXPERTS - 1))
            n_extra = load_n_extra(pe)

            def prepare():
                gather(N_EXPERTS)
                pe.wait_ge(y_sb, N_EXPERTS + 1)
                turn_rows(N_EXPERTS)

            over_extra_by_period(pe, prepare, lambda m, r, q: item(m, r), n_extra)
            pe.wait_ge(y_sb, n_extra + (N_EXPERTS + 1))
            pe.wait_ge(pgT_sb, n_extra + (N_EXPERTS + 1))
            scatter(stop=True)

        @block.vector
        def _(dve):
            steps = [0]

            def step(ins):
                steps[0] += 1
                ins.then_inc(dve_step, 1)
                dve.wait_ge(dve_step, steps[0])

            def norm_scale(n, n_squares, *parts):
                dve.wait_ge(squares, n_squares)
                for a, b, width in parts:
                    last = nc.vector.tensor_scalar(msq[:, a:b], ssq[:, a:b], 1.0 / width, NORM_EPS, ALU.mult, ALU.add)
                last.then_inc(means, 1)
                dve.wait_ge(roots, n)
                a, b = parts[0][0], parts[-1][1]
                nc.vector.reciprocal(rstd[:, a:b], root[:, a:b]).then_inc(rstd_ready, 1)
                dve.wait_ge(rstd_ready, n)

            def rotate(dst, src, cos, sin, groups, half, freed=None, done=None, scale=1.0):
                w = 2 * half
                a = rot_a[:, 0:groups * w].rearrange("p (g d) -> p g d", g=groups)
                b = rot_b[:, 0:groups * w].rearrange("p (g d) -> p g d", g=groups)
                c = cos.unsqueeze(1).to_broadcast([P, groups, w])
                s = sin.unsqueeze(1).to_broadcast([P, groups, w])
                lo, hi = slice(0, half), slice(half, w)
                nc.vector.scalar_tensor_tensor(a, src, scale, c, ALU.mult, ALU.mult)
                nc.vector.scalar_tensor_tensor(b[:, :, lo], src[:, :, hi], scale, s[:, :, lo], ALU.mult, ALU.mult)
                ins = nc.vector.scalar_tensor_tensor(b[:, :, hi], src[:, :, lo], scale, s[:, :, hi], ALU.mult, ALU.mult)
                if freed:
                    ins.then_inc(freed[0], 1)
                    dve.wait_ge(*freed)
                else:
                    step(ins)
                ins = nc.vector.tensor_tensor(dst, a, b, ALU.add)
                if done:
                    ins.then_inc(done[0], 1)
                    dve.wait_ge(*done)
                else:
                    step(ins)

            def freed_at(name):
                return (emptied(name), TILE[name][1] + 1)

            dve.wait_ge(gain_in, 16)
            for t in range(T):
                dve.wait_ge(x_in[t], 16)
                nc.vector.tensor_tensor(H[:, t, :], X[:, t, :], gain_attn, ALU.mult).then_inc(h_ready, 1)
            norm_scale(1, T, (N_ATT, N_ATT + T, D_MODEL))
            norm_scale(2, 3 * T, (N_LAT, N_LAT + T, Q_LORA), (N_LAT + T, N_LAT + 2 * T, KV_LORA))
            dve.wait_ge(lora_in, 32)
            for t in range(T):
                for a, w, col in ((0, Q_LORA, N_LAT + t), (Q_LORA, KV_LORA, N_LAT + T + t)):
                    nc.vector.scalar_tensor_tensor(LAT[:, t, a:a + w], LAT[:, t, a:a + w], rstd[:, col:col + 1],
                                                   lora_gain[:, a:a + w], ALU.mult, ALU.mult).then_inc(lat_ready, 1)
            dve.wait_ge(pads_zero, 1)
            dve.wait_ge(const_in, 16)
            for t in range(T):
                rotate(kr_pad3[:, t, MLA_ROPE:2 * MLA_ROPE].unsqueeze(1), LAT[:, t, W_LAT - MLA_ROPE:W_LAT].unsqueeze(1),
                       const("cos_m", t), const("sin_m", t), 1, MLA_ROPE // 2, done=(kr_roped, t + 1))
            dve.wait_ge(pads_zero, 2)
            for c in range(2):
                for t in range(T):
                    wait_sb(dve, f"idx{c}{t}")
            for t in range(T):
                kq = ki_pad3[:, t, IDX_DIM:2 * IDX_DIM].unsqueeze(1)
                ki = IDX[:, t, IDX_HEADS * IDX_DIM:(IDX_HEADS + 1) * IDX_DIM].unsqueeze(1)
                rotate(kq[:, :, 0:IDX_ROPE], ki[:, :, 0:IDX_ROPE], const("cos_i", t), const("sin_i", t), 1, IDX_ROPE // 2)
                nc.vector.tensor_copy(kq[:, :, IDX_ROPE:IDX_DIM], ki[:, :, IDX_ROPE:IDX_DIM])
                qd = roped[:, t * COLS:(t + 1) * COLS].rearrange("p (h d) -> p h d", d=IDX_DIM)
                qi = IDX[:, t, 0:IDX_HEADS * IDX_DIM].rearrange("p (h d) -> p h d", d=IDX_DIM)
                nc.vector.tensor_copy(qd[:, :, IDX_ROPE:IDX_DIM], qi[:, :, IDX_ROPE:IDX_DIM])
                nc.vector.tensor_scalar(wi[:, t * IDX_HEADS:(t + 1) * IDX_HEADS], IDX[:, t, (IDX_HEADS + 1) * IDX_DIM:W_IDX],
                                        IDX_HEADS ** -0.5, None, ALU.mult)
                rotate(qd[:, :, 0:IDX_ROPE], qi[:, :, 0:IDX_ROPE], const("cos_i", t), const("sin_i", t), IDX_HEADS,
                       IDX_ROPE // 2, done=(idx_roped, t + 1))
            for t in range(T):
                n = f"qr{t}"
                wait_full(dve, n)
                rotate(q_rot[t].rearrange("p (h d) -> p h d", d=MLA_ROPE),
                       ps(n)[:, :].rearrange("p (h d) -> p h d", d=MLA_ROPE), const("cos_m", t), const("sin_m", t),
                       HEADS, MLA_ROPE // 2, freed_at(n), (tok_roped, t + 1))
            for t in range(T):
                keys = P * (t + 1)
                sc = score[:, t * P:t * P + keys]
                for g in range(4):
                    u = 4 * t + g
                    wait_sb(dve, f"raw{t}{g}")
                    for e in range(2):
                        r = RELU[u % 2][:, e * keys:(e + 1) * keys]
                        w = wi[:, t * IDX_HEADS + 2 * g + e:t * IDX_HEADS + 2 * g + e + 1]
                        if g == 0 and e == 0:
                            ins = nc.vector.tensor_scalar(sc, r, w, None, ALU.mult)
                        else:
                            ins = nc.vector.scalar_tensor_tensor(sc, r, w, sc, ALU.mult, ALU.add)
                        if e == 0:
                            step(ins)
                        else:
                            ins.then_inc(relu_used, 1)
                            dve.wait_ge(relu_used, u + 1)
            step(nc.vector.tensor_tensor(score[:, :], score[:, :], const("chunk_mask"), ALU.add))

            def select(t):
                sc = score[:, t * P:t * P + P * (t + 1)]
                for _ in range(TOP_K // 8):
                    step(nc.vector.max(top8[:, :], sc))
                    step(nc.vector.match_replace(sc, top8[:, :], sc, TAKEN))
                step(nc.vector.tensor_scalar(sel_mask[:, t * P:t * P + P * (t + 1)], sc, TAKEN, MASKED,
                                             ALU.not_equal, ALU.mult))

            for n, (c, t) in enumerate(QK):
                name = f"qk{c}{t}"
                if n:
                    wait_full(dve, "qkT%d%d" % QK[n - 3] if n >= 3 else f"qiT{n - 1}")
                wait_full(dve, name)
                a = COLS * ((n + 2) % 3)
                rotate(roped[:, a:a + COLS].rearrange("p (h d) -> p h d", d=HD),
                       ps(name)[:, :].rearrange("p (h d) -> p h d", d=HD), const("cos_d", t), const("sin_d", t),
                       COLS // HD, HD // 2, freed_at(name), (tok_roped, T + n + 1),
                       rstd[:, N_ATT + t:N_ATT + t + 1])
                if n < T:
                    select(n)
            for s in range(NH + 3):
                if s < NH:
                    n = f"s{s}"
                    wait_full(dve, n)
                    nc.vector.scalar_tensor_tensor(S[s % 2], ps(n)[:, 0:3 * P],
                                                   (MLA_QK if s < HEADS else HD) ** -0.5,
                                                   const("chunk_mask") if s < HEADS else sel_mask[:, :],
                                                   ALU.mult, ALU.add).then_inc(emptied(n), 1)
                    dve.wait_ge(*freed_at(n))
                    for t in range(T):
                        ins = nc.vector.tensor_reduce(negmax[:, s * T + t:s * T + t + 1],
                                                      S[s % 2][:, t * P:t * P + P * (t + 1)], AX, ALU.max, negate=True)
                    ins.then_inc(masked, 1)
                if 1 <= s <= NH:
                    h = s - 1
                    dve.wait_ge(exped, T * s)
                    step(nc.vector.reciprocal(rsum[:, h * T:(h + 1) * T], psums[:, h * T:(h + 1) * T]))
                    for t in range(T):
                        p = PR[h % 3][:, t * P:t * P + P * (t + 1)]
                        ins = nc.vector.tensor_scalar(p, p, rsum[:, h * T + t:h * T + t + 1], None, ALU.mult)
                    ins.then_inc(normed, 1)
                if s >= 3:
                    n = f"o{s - 3}"
                    wait_full(dve, n)
                    nc.vector.tensor_copy((QN if s - 3 < HEADS else QT)[:, (s - 3) % HEADS, :], ps(n)[:, 0:SEQ])\
                        .then_inc(emptied(n), 1)
                if s in BETWEEN and BETWEEN[s][0] == "gate":
                    _, c, t = BETWEEN[s]
                    n = f"gate{c}{t}"
                    dve.wait_ge(gate_bias_in, 64)
                    wait_full(dve, n)
                    nc.vector.scalar_tensor_tensor(G[:, t, c * COLS:(c + 1) * COLS], ps(n)[:, :],
                                                   rstd[:, N_ATT + t:N_ATT + t + 1], gate_bias[c],
                                                   ALU.mult, ALU.add).then_inc(emptied(n), 1)
            for c in range(2):
                for t in range(T):
                    n = f"ya{c}{t}"
                    wait_full(dve, n)
                    dve.wait_ge(gate_sig, T * c + t + 1)
                    nc.vector.tensor_tensor(MG[:, t, c * COLS:(c + 1) * COLS], ps(n)[:, :],
                                            G[:, t, c * COLS:(c + 1) * COLS], ALU.mult).then_inc(emptied(n), 1)
            for c in range(2):
                for t in range(T):
                    n = f"yb{c}{t}"
                    m = MG[:, t, c * COLS:(c + 1) * COLS]
                    wait_full(dve, n)
                    dve.wait_ge(gate_sig, T * (c + 2) + t + 1)
                    nc.vector.tensor_tensor(rot_a[:, :], ps(n)[:, :], G[:, t, D_MODEL + c * COLS:D_MODEL + (c + 1) * COLS],
                                            ALU.mult).then_inc(emptied(n), 1)
                    dve.wait_ge(*freed_at(n))
                    dve.wait_ge(*freed_at(f"ya{c}{t}"))
                    nc.vector.tensor_tensor(m, m, rot_a[:, :], ALU.add).then_inc(merged, 1)
                    dve.wait_ge(merged, T * c + t + 1)
            dve.wait_ge(gain_in, 32)
            for t in range(T):
                for c in range(2):
                    n, cols = f"xo{c}{t}", slice(c * COLS, (c + 1) * COLS)
                    wait_full(dve, n)
                    nc.vector.tensor_tensor(X[:, t, cols], ps(n)[:, :], X[:, t, cols], ALU.add).then_inc(emptied(n), 1)
                    dve.wait_ge(*freed_at(n))
                    nc.vector.tensor_tensor(HN[:, t, cols], X[:, t, cols], gain_ffn[:, cols], ALU.mult)\
                        .then_inc(hf_ready, 1)
            norm_scale(3, 4 * T, (N_FFN, N_FFN + T, D_MODEL))

            dve.wait_ge(router_in, 32)
            nc.vector.memset(LPAD3[:, :, N_EXPERTS:], TAKEN)
            wait_full(dve, "logits")
            for t in range(T):
                ins = nc.vector.scalar_tensor_tensor(LG3[:, t, :], ps("logits")[:, t * N_EXPERTS:(t + 1) * N_EXPERTS],
                                                     rstd[:, N_FFN + t:N_FFN + t + 1], b_rt, ALU.mult, ALU.add)
            ins.then_inc(emptied("logits"), 1)
            dve.wait_ge(*freed_at("logits"))
            for t in range(T):
                ins = nc.vector.max(REP3[:, t, :], LG3[:, t, :])
            step(ins)
            step(nc.vector.memset(REP3[:, :, MOE_TOP_K:8], TAKEN))
            for t in range(T):
                ins = nc.vector.match_replace(LREP3[:, t, :], REP3[:, t, :], LPAD3[:, t, :], MASKED)
            step(ins)
            nc.vector.tensor_tensor(CH3, LREP3[:, :, 0:N_EXPERTS], LG3, ALU.not_equal).then_inc(chosen, 1)
            nc.vector.tensor_scalar(nmx.unsqueeze(2), REP3[:, :, 0:1], -1.0, None, ALU.mult).then_inc(logits_in, 1)
            dve.wait_ge(chosen, 1)
            wait_full(dve, "rank")
            nc.vector.scalar_tensor_tensor(R1, ps("rank")[:, 0:TE], 1.0, CH, ALU.add, ALU.mult)\
                .then_inc(emptied("rank"), 1)
            dve.wait_ge(*freed_at("rank"))

            def te(ap, t, e):
                return ap[:, bass.ds(e + t * N_EXPERTS, 1)]

            def one_hot(item, done):
                for t in range(T):
                    ins = nc.vector.tensor_scalar(GP[:, t, :], const("slot_no"), te(R1, t, item), None, ALU.is_equal)
                ins.then_inc(done, 1)

            one_hot(0, p_ready)
            dve.wait_ge(router_exp, T)
            step(nc.vector.tensor_tensor(GT3, LGE3, CH3, ALU.mult))
            step(nc.vector.tensor_reduce(gs, GT3, AX, ALU.add))
            step(nc.vector.reciprocal(grs, gs))
            for t in range(T):
                ins = nc.vector.tensor_scalar(GT3[:, t, :], GT3[:, t, :], grs[:, t:t + 1], None, ALU.mult)
            step(ins)
            dve.wait_ge(zeroed, 2)
            nc.vector.tensor_copy(PG[:, :, SLOTS:SLOTS + N_EXPERTS], GT3).then_inc(gates_in, 1)
            def gated(item, done):
                for t in range(T):
                    ins = nc.vector.tensor_scalar(PG[:, t, SLOTS:2 * SLOTS], const("slot_no"), te(R1, t, item),
                                                  te(GT_, t, item), ALU.is_equal, ALU.mult)
                ins.then_inc(done, 1)

            wait_full(dve, "count")
            cnt = ps("count")[:, 0:N_EXPERTS]
            step(nc.vector.tensor_scalar(NB, cnt, SLOTS + 0.5, None, ALU.is_gt))
            step(nc.vector.scalar_tensor_tensor(NB, cnt, 2 * SLOTS + 0.5, NB, ALU.is_gt, ALU.add))
            nc.vector.scalar_tensor_tensor(NB, cnt, 3 * SLOTS + 0.5, NB, ALU.is_gt, ALU.add).then_inc(emptied("count"), 1)
            dve.wait_ge(*freed_at("count"))
            wait_full(dve, "gT")
            nc.vector.tensor_copy(PGT, ps("gT")[:, :].rearrange("p (h n) -> p h n", h=2)).then_inc(pgT_sb, 1)

            gated(0, pg_ready)
            step(nc.vector.tensor_tensor_scan(EXTRA_END, const("ones")[:, 0:N_EXPERTS], NB, 0.0, ALU.mult, ALU.add))
            ends = EXTRA_END[0:1, :].unsqueeze(1).to_broadcast([1, EXTRA_COLS, N_EXPERTS])
            items = const("extra_no")[0:1, :].unsqueeze(2).to_broadcast([1, EXTRA_COLS, N_EXPERTS])
            cmp = ET[0:1, :].rearrange("p (i e) -> p i e", e=N_EXPERTS)
            step(nc.vector.tensor_tensor(cmp, ends, items, ALU.is_le))
            nc.vector.tensor_copy(ER[0:1, EXTRA_COLS:EXTRA_COLS + 1], EXTRA_END[0:1, N_EXPERTS - 1:N_EXPERTS])
            step(nc.vector.tensor_reduce(ER[0:1, 0:EXTRA_COLS], cmp, AX, ALU.add))
            step(nc.vector.tensor_scalar(ER[0:1, 0:EXTRA_COLS], ER[0:1, 0:EXTRA_COLS], float(N_EXPERTS - 1), None, ALU.min))
            nc.vector.tensor_copy(table_i[0:1, 0:EXTRA_COLS + 1], ER[0:1, :]).then_inc(table, 1)
            step(nc.vector.tensor_tensor(EXTRA_AT, EXTRA_END, NB, ALU.subtract))
            step(nc.vector.tensor_scalar(EXTRA_AT, EXTRA_AT, float(SLOTS), float(-SLOTS), ALU.mult, ALU.add))
            step(nc.vector.tensor_tensor(DX3, R13, EXTRA_AT.unsqueeze(1).to_broadcast([P, T, N_EXPERTS]), ALU.add))
            step(nc.vector.scalar_tensor_tensor(DX, R1, SLOTS + 0.5, DX, ALU.is_gt, ALU.mult))

            EXTRA_STEPS = 4

            def extra_route(q):
                at = [0]

                def do(ins):
                    at[0] += 1
                    ins.then_inc(extra_step, 1)
                    dve.wait_ge(extra_step, q * EXTRA_STEPS + at[0])

                first = cst[:, bass.ds(q + CONST["extra_base"][0], 1)]
                do(nc.vector.tensor_scalar(IX, DX, first, None, ALU.subtract))
                do(nc.vector.scalar_tensor_tensor(U2, IX, SLOTS + 0.5, IX, ALU.is_lt, ALU.mult))
                nc.vector.tensor_reduce(W1, by_te(U2), AX, ALU.max)
                do(nc.vector.scalar_tensor_tensor(VG, U2, 0.5, GT_, ALU.is_gt, ALU.mult))
                do(nc.vector.tensor_reduce(GW, by_te(VG), AX, ALU.add))
                assert at[0] == EXTRA_STEPS

            def extra_one_hot():
                for t in range(T):
                    ins = nc.vector.tensor_scalar(GP[:, t, :], const("slot_no"), W1[:, t:t + 1], None, ALU.is_equal)
                ins.then_inc(p_ready, 1)

            def extra_gated():
                for t in range(T):
                    ins = nc.vector.tensor_scalar(PG[:, t, SLOTS:2 * SLOTS], const("slot_no"), W1[:, t:t + 1],
                                                  GW[:, t:t + 1], ALU.is_equal, ALU.mult)
                ins.then_inc(pg_ready, 1)

            def gates_in_sbuf(i):
                dve.wait_ge(pgT_ps, i + 1)
                nc.vector.tensor_copy(PGT, BY[:, :].rearrange("p (h n) -> p h n", h=2)).then_inc(pgT_sb, 1)

            def swiglu(i):
                dve.wait_ge(h_done, i + 1)
                nc.vector.tensor_scalar(GC, BG[:, :], SWIGLU_LIMIT, None, ALU.min).then_inc(clipped, 1)
                nc.vector.tensor_scalar(AC, BL[:, :], SWIGLU_LIMIT, -SWIGLU_LIMIT, ALU.min, ALU.max)
                dve.wait_ge(sig, i + 1)
                nc.vector.tensor_tensor(GC, GC, SG, ALU.mult).then_inc(glu_done, 1)
                dve.wait_ge(glu_done, i + 1)
                nc.vector.scalar_tensor_tensor(AC, AC, 1.0, GC, ALU.add, ALU.mult).then_inc(act_ready, 1)

            with dve.Fori(0, N_EXPERTS - 1) as i:
                dve.wait_ge(xg_ps, i + 1)
                one_hot(i + 1, p_ready)
                swiglu(i)
                gates_in_sbuf(i)
                gated(i + 1, pg_ready)
            swiglu(N_EXPERTS - 1)
            gates_in_sbuf(N_EXPERTS - 1)

            def prepare():
                extra_route(0)
                dve.wait_ge(xg_ps, N_EXPERTS)
                extra_one_hot()
                extra_gated()

            def extra(q):
                i = q + N_EXPERTS
                extra_route(q + 1)
                dve.wait_ge(xg_ps, i + 1)
                extra_one_hot()
                swiglu(i)
                gates_in_sbuf(i)
                extra_gated()

            over_extra(dve, prepare, extra, load_n_extra(dve))
            for t in range(T):
                for h in range(2):
                    dve.wait_ge(acc_done, 2 * t + h + 1)
                    r = X[:, t, h * COLS:(h + 1) * COLS]
                    nc.vector.tensor_tensor(r, bank[2 * t + h][:, :], r, ALU.add).then_inc(resid_done, 1)
            dve.wait_ge(out_gain_in, 16)
            for t in range(T):
                norm_scale(4 + t, 4 * T + t + 1, (N_OUT + t, N_OUT + t + 1, D_MODEL))
                nc.vector.scalar_tensor_tensor(X[:, t, :], X[:, t, :], rstd[:, N_OUT + t:N_OUT + t + 1], gain_out,
                                               ALU.mult, ALU.mult).then_inc(out_ready, 1)


def constants(np):
    c = {"ident": np.eye(P), "ones": np.ones((P, P))}
    pos = np.arange(SEQ, dtype=np.float32).reshape(T, P, 1)

    def tables(rot, key):
        half = rot // 2
        freq = np.float32(ROPE_THETA) ** (-np.arange(half, dtype=np.float32) / np.float32(half))
        ang = (pos * freq.astype(np.float32)).astype(np.float32)
        cos, sin = np.cos(ang), np.sin(ang)
        c["cos_" + key] = np.concatenate([cos, cos], -1).transpose(1, 0, 2).reshape(P, -1)
        c["sin_" + key] = np.concatenate([-sin, sin], -1).transpose(1, 0, 2).reshape(P, -1)

    tables(HD, "d")
    tables(MLA_ROPE, "m")
    tables(IDX_ROPE, "i")
    q = np.arange(P)[:, None]
    parts = [np.where((np.arange(P * (t + 1))[None] // CHUNK) <= (t * P + q) // CHUNK, 0.0, MASKED) for t in range(T)]
    c["chunk_mask"] = np.concatenate(parts, 1)
    c["before"] = (q < np.arange(P)[None]) * 1.0
    c["slot_no"] = np.tile(np.arange(1, SLOTS + 1), (P, 1))
    c["extra_base"] = np.tile(np.arange(EXTRA_COLS) * SLOTS, (P, 1))
    c["extra_no"] = np.tile(np.arange(EXTRA_COLS), (P, 1))
    c["row_of"] = (q == np.arange(4 * SLOTS)[None] // SLOTS) * 1.0
    return np.ascontiguousarray(np.concatenate([c[n] for n in CONST], 1).astype(np.float32))


_INS = ['x', 'norm_attn_g', 'w_in', 'q_lora_g', 'kv_lora_g', 'w_uq', 'w_uk', 'w_uv', 'w_o_mla', 'w_o_dsa',
        'b_gate', 'w_out', 'norm_ffn_g', 'w_router', 'b_router', 'w_gate_up', 'b_gate_up', 'w_down',
        'b_down', 'norm_final_g']


def kernel(**inputs):
    import numpy as _np
    import concourse.bacc as _bacc
    from concourse import mybir as _mybir
    from concourse.bass_utils import run_bass_kernel_spmd as _run

    nc = _bacc.Bacc("TRN2", target_bir_lowering=False, num_devices=1)
    arrays, args = {}, []
    for name in _INS:
        a = _np.ascontiguousarray(inputs[name])
        arrays[f"in_{name}"] = a
        args.append(nc.dram_tensor(f"in_{name}", a.shape, _mybir.dt.from_np(a.dtype), kind="ExternalInput").ap())
    a = constants(_np)
    arrays["in_consts"] = a
    args.append(nc.dram_tensor("in_consts", a.shape, _mybir.dt.from_np(a.dtype), kind="ExternalInput").ap())
    o = nc.dram_tensor("out_0", (1, SEQ, D_MODEL), _mybir.dt.float32, kind="ExternalOutput").ap()
    hybrid_block_kernel(nc, *args, o)
    return _run(nc, [arrays], core_ids=[0]).results[0]["out_0"]
```
